# Optimizing a Trainium2 kernel written in Bass

```python
import jax, jax.numpy as jnp
from jax import lax
import numpy as np

D_MODEL = 1024
BATCH = 1
SEQ = 256
DEPTH = 1

PLE_DIM = 256
POOL_GROUPS = 4
POOL_GROUP_W = 128
POOL_WINDOWS = (2, 4, 8, 16)
POOL_W = POOL_GROUPS * POOL_GROUP_W
N_HEADS = 8
N_KV_HEADS = 2
HEAD_DIM = 64
ATTN_W = N_HEADS * HEAD_DIM
KV_W = N_KV_HEADS * HEAD_DIM
IDX_HEADS = 8
IDX_DIM = 64
TOPK_MAX = 256
Q_BLOCK = 128
N_EXPERTS = 32
TOP_K = 4
D_FF = D_MODEL
SWIGLU_LIMIT = 7.0
SWIGLU_ALPHA = 1.702
RMS_EPS = 1e-6
IN_SIZES = (POOL_W, ATTN_W, KV_W, KV_W, IDX_HEADS * IDX_DIM, IDX_DIM, IDX_HEADS, 2 * D_MODEL)
IN_COLS = sum(IN_SIZES)
IN_SPLITS = tuple(int(c) for c in np.cumsum(IN_SIZES)[:-1])

kernel_name = "hybrid_pool_dsa_moe_ple_block"

def _rmsnorm(x, g):
    xf = x.astype(jnp.float32)
    y = xf * lax.rsqrt(jnp.mean(xf * xf, axis=-1, keepdims=True) + RMS_EPS)
    return (y * g.astype(jnp.float32)).astype(x.dtype)

def _pool_mixer(u, pool_w, pool_scale):
    b, s, _ = u.shape
    ug = u.reshape(b, s, POOL_GROUPS, POOL_GROUP_W).astype(jnp.float32)
    csum = jnp.cumsum(ug, axis=1)
    count = jnp.arange(1, s + 1, dtype=jnp.float32)
    mixed = []
    for g, w in enumerate(POOL_WINDOWS):
        c = csum[:, :, g]
        lagged = jnp.pad(c, ((0, 0), (w, 0), (0, 0)))[:, :s]
        mean = (c - lagged) / jnp.minimum(count, float(w))[None, :, None]
        mixed.append(mean - ug[:, :, g])
    mixed = jnp.stack(mixed, axis=2).astype(u.dtype)
    y = jnp.einsum('bsgc,gcd->bsgd', mixed, pool_w)
    return y.reshape(b, s, POOL_W) * pool_scale

def _dsa_attention(q, k, v, q_idx, k_idx, w_idx):
    b, s = q.shape[:2]
    n_sel = min(TOPK_MAX, s // 4)
    nb = s // Q_BLOCK
    group = N_HEADS // N_KV_HEADS
    key_pos = jnp.arange(s)
    k_idx32 = k_idx.astype(jnp.float32)

    def to_blocks(a):
        return jnp.moveaxis(a.reshape(b, nb, Q_BLOCK, *a.shape[2:]), 1, 0)

    def block_fn(args):
        qb, qib, wib, start = args
        qpos = start + jnp.arange(Q_BLOCK)
        logit = jnp.einsum('bthd,bsd->bths', qib.astype(jnp.float32), k_idx32) * (IDX_DIM ** -0.5)
        score = jnp.einsum('bths,bth->bts', jax.nn.relu(logit),
                           wib.astype(jnp.float32) * (IDX_HEADS ** -0.5))
        causal = key_pos[None, :] <= qpos[:, None]
        score = jnp.where(causal[None], score, -jnp.inf)
        _, idx = lax.top_k(score, n_sel)
        k_sel = jax.vmap(lambda kb, ib: kb[ib])(k, idx)
        v_sel = jax.vmap(lambda vb, ib: vb[ib])(v, idx)
        qg = qb.reshape(b, Q_BLOCK, N_KV_HEADS, group, HEAD_DIM)
        att = jnp.einsum('btkgd,btnkd->btkgn', qg, k_sel).astype(jnp.float32) * (HEAD_DIM ** -0.5)
        valid = (idx <= qpos[None, :, None])[:, :, None, None, :]
        att = jnp.where(valid, att, -jnp.inf)
        prob = jax.nn.softmax(att, axis=-1).astype(v.dtype)
        o = jnp.einsum('btkgn,btnkd->btkgd', prob, v_sel)
        return o.reshape(b, Q_BLOCK, ATTN_W)

    starts = jnp.arange(nb) * Q_BLOCK
    out = lax.map(block_fn, (to_blocks(q), to_blocks(q_idx), to_blocks(w_idx), starts))
    return jnp.moveaxis(out, 0, 1).reshape(b, s, ATTN_W)

def _moe(h, router_w, router_b, w1, b1, w2, b2):
    logits = (h @ router_w + router_b).astype(jnp.float32)
    top_val, top_idx = lax.top_k(logits, TOP_K)
    gate = jax.nn.softmax(top_val, axis=-1)
    comb = jnp.sum(jax.nn.one_hot(top_idx, N_EXPERTS, dtype=jnp.float32) * gate[..., None],
                   axis=-2).astype(h.dtype)
    out = jnp.zeros_like(h)
    for e in range(N_EXPERTS):
        gu = h @ w1[e] + b1[e]
        g_lin, up = jnp.split(gu, 2, axis=-1)
        g_lin = jnp.minimum(g_lin, SWIGLU_LIMIT)
        up = jnp.clip(up, -SWIGLU_LIMIT, SWIGLU_LIMIT)
        act = (up + 1.0) * (g_lin * jax.nn.sigmoid(SWIGLU_ALPHA * g_lin))
        out = out + comb[..., e:e + 1] * (act @ w2[e] + b2[e])
    return out

def setup_inputs(seed: int = 0) -> dict:
    key = jax.random.key(seed)
    ks = jax.random.split(key, 24)
    f32 = jnp.float32

    def nrm(k, shape, scale):
        return jax.random.normal(k, shape, f32) * scale

    def gain(k, shape):
        return 1.0 + 0.05 * jax.random.normal(k, shape, f32)

    L, D, E = DEPTH, D_MODEL, N_EXPERTS
    return {
        "x": nrm(ks[0], (BATCH, SEQ, D), 1.0),
        "p": nrm(ks[1], (DEPTH, BATCH, SEQ, PLE_DIM), 1.0),
        "norm1_g": gain(ks[2], (L, D)),
        "w_in": nrm(ks[3], (L, D, IN_COLS), D ** -0.5),
        "pool_w": nrm(ks[4], (L, POOL_GROUPS, POOL_GROUP_W, POOL_GROUP_W), POOL_GROUP_W ** -0.5),
        "pool_scale": gain(ks[5], (L, POOL_W)),
        "w_branch_pool": nrm(ks[6], (L, POOL_W, D), POOL_W ** -0.5),
        "w_branch_attn": nrm(ks[7], (L, ATTN_W, D), ATTN_W ** -0.5),
        "w_out": nrm(ks[8], (L, D, D), D ** -0.5),
        "norm2_g": gain(ks[9], (L, D)),
        "router_w": nrm(ks[10], (L, D, E), D ** -0.5),
        "router_b": nrm(ks[11], (L, E), 0.01),
        "exp_w1": nrm(ks[12], (L, E, D, 2 * D_FF), D ** -0.5),
        "exp_b1": nrm(ks[13], (L, E, 2 * D_FF), 0.02),
        "exp_w2": nrm(ks[14], (L, E, D_FF, D), D_FF ** -0.5),
        "exp_b2": nrm(ks[15], (L, E, D), 0.02),
        "ple_norm_g": gain(ks[16], (L, D)),
        "ple_gate_w": nrm(ks[17], (L, D, D), D ** -0.5),
        "ple_proj_w": nrm(ks[18], (L, PLE_DIM, D), PLE_DIM ** -0.5),
        "final_g": gain(ks[19], (D,)),
    }

def reference(x, p, norm1_g, w_in, pool_w, pool_scale, w_branch_pool, w_branch_attn, w_out,
              norm2_g, router_w, router_b, exp_w1, exp_b1, exp_w2, exp_b2,
              ple_norm_g, ple_gate_w, ple_proj_w, final_g):
    b, s, _ = x.shape
    for i in range(DEPTH):
        h = _rmsnorm(x, norm1_g[i])
        proj = h @ w_in[i]
        u, q, k, v, qi, ki, wi, gates = jnp.split(proj, IN_SPLITS, axis=-1)
        y_pool = _pool_mixer(u, pool_w[i], pool_scale[i]) @ w_branch_pool[i]
        y_attn = _dsa_attention(
            q.reshape(b, s, N_HEADS, HEAD_DIM),
            k.reshape(b, s, N_KV_HEADS, HEAD_DIM),
            v.reshape(b, s, N_KV_HEADS, HEAD_DIM),
            qi.reshape(b, s, IDX_HEADS, IDX_DIM), ki, wi) @ w_branch_attn[i]
        g_pool, g_attn = jnp.split(jax.nn.sigmoid(gates), 2, axis=-1)
        x = x + (g_pool * y_pool + g_attn * y_attn) @ w_out[i]
        h2 = _rmsnorm(x, norm2_g[i])
        x = x + _moe(h2, router_w[i], router_b[i], exp_w1[i], exp_b1[i], exp_w2[i], exp_b2[i])
        hp = _rmsnorm(x, ple_norm_g[i])
        x = x + jax.nn.sigmoid(hp @ ple_gate_w[i]) * (p[i].astype(x.dtype) @ ple_proj_w[i])
    return _rmsnorm(x, final_g)


_drawn_inputs = setup_inputs


def setup_inputs(seed=0):
    import zlib

    import numpy as np

    out = dict(_drawn_inputs(seed))
    spreads = {}
    factors = {'exp_b1': 5.941, 'exp_b2': 6.879, 'ple_norm_g': 7.238}
    for name, (base, spread) in spreads.items():
        noise = np.random.default_rng([zlib.crc32(name.encode()), seed]).standard_normal(out[name].shape)
        drawn = base * np.exp(spread * noise) if base else spread * noise
        out[name] = __import__('jax').numpy.asarray(drawn.astype(out[name].dtype))
    for name, factor in factors.items():
        out[name] = (out[name] * factor).astype(out[name].dtype)
    return out
```

```python
import concourse.bass as bass
from concourse import mybir
from contextlib import ExitStack


def hybrid_block(nc, x_d, p_d, norm1_g, w_in, pool_w, pool_scale, w_bp, w_ba, w_out,
                 norm2_g, router_w, router_b, exp_w1, exp_b1, exp_w2, exp_b2,
                 ple_norm_g, ple_gate_w, ple_proj_w, final_g, out_d):
    f32 = mybir.dt.float32
    i32 = mybir.dt.int32
    ALU = mybir.AluOpType
    ACT = mybir.ActivationFunctionType
    AX = mybir.AxisListType

    P = 128
    S, D = x_d.shape[1], x_d.shape[2]
    NT = S // P
    KD = D // P
    HALF = 512
    PW = pool_scale.shape[1]
    NG = PW // P
    WINDOWS = (2, 4, 8, 16)
    PAD = 16
    NH, DH = 8, 64
    NKV = 2
    GROUP = NH // NKV
    AW = NH * DH
    TOPK = S // 4
    E = router_w.shape[2]
    F = exp_w2.shape[2]
    KF = F // P
    NU = 2 * KF
    TOPE = 4
    SLOT = 64
    MAXIT = E * (S // SLOT)
    EPS = 1e-6
    FILL, TAKEN, BIG = -1e38, -3e38, 1e30

    C_U, C_Q = 0, PW
    C_K = C_Q + AW
    C_V = C_K + NKV * DH
    C_QI = C_V + NKV * DH
    C_KI = C_QI + NH * DH
    C_WI = C_KI + DH
    C_G = C_WI + NH

    GW = 256
    GROUPS = [(C_KI, DH + NH), (C_QI, GW), (C_QI + GW, GW), (C_K, GW), (C_Q, GW), (C_Q + GW, GW),
              (C_U, GW), (C_U + GW, GW)] + [(C_G + GW * i, GW) for i in range(2 * D // GW)]
    GROUP_STEPS = ["wi", "qi0", "qi1", "v", "q0", "q1", "u0", "u1"] + [f"g{i}" for i in range(2 * D // GW)]
    NSTREAM = 4
    SLOTF = KD * GW
    NRING = 12

    ctx = ExitStack()
    with ctx:
        def sb(name, shape, dt=f32):
            return ctx.enter_context(nc.sbuf_tensor(name, shape, dt))

        def sem(name):
            return ctx.enter_context(nc.semaphore(name))

        ring = sb("ring", [P, NRING, SLOTF])
        stream = sb("stream", [P, NSTREAM, SLOTF])
        work = sb("work", [P, 12864])
        x_sb = sb("x_sb", [P, NT, D])
        hn = sb("hn", [P, NT, D])
        gain = sb("gain", [P, D])
        ident = sb("ident", [P, P])
        tri = sb("tri", [P, P])
        ones = sb("ones", [P, P])
        slot_no = sb("slot_no", [P, 2, SLOT])
        pos = sb("pos", [P, NT, MAXIT + 1])
        gate = sb("gate", [P, NT, MAXIT + 1])
        rb_row = sb("rb_row", [1, E])
        scale_rows = sb("scale_rows", [NG, P])
        scale_col = sb("scale_col", [P, NG])
        ss = sb("ss", [P, NT])
        rstd = sb("rstd", [P, NT])
        top8 = sb("top8", [P, NT, 8])
        wi_sb = sb("wi_sb", [P, NT, NH])
        smax = sb("smax", [P, NH])
        ssum = sb("ssum", [P, NH])
        first_inv = sb("first_inv", [P, NG, PAD])
        lpad = sb("lpad", [P, NT, E + 4])
        top4 = sb("top4", [P, NT, 8])
        mask = sb("mask", [P, NT, E])
        expl = sb("expl", [P, NT, E])
        small = sb("small", [P, 8])
        least = sb("least", [P, NT])
        gsum = sb("gsum", [P, NT])
        iters = sb("iters", [P, 1], i32)

        sgT = ring[:, 8:10, :].rearrange("p a (c s) -> p (a c) s", s=S)
        sm1 = ring[:, 10, :].rearrange("p (h s) -> p h s", h=NH)
        PT1 = ring[:, 11, :].rearrange("p (h k s) -> p h k s", h=NH, k=NT)

        def cut(a, n):
            return work[:, a:a + n]

        hT = cut(0, 2048).rearrange("p (k s) -> p k s", k=KD)
        qiT = cut(2048, 1024).rearrange("p (c s) -> p c s", s=S)
        qT = cut(3072, 1024).rearrange("p (c s) -> p c s", s=S)
        kiT = cut(4096, 256)
        kT = cut(4352, 512).rearrange("p (v s) -> p v s", v=NKV)
        v_sb = cut(4864, 256).rearrange("p (t c) -> p t c", t=NT)
        relu = cut(5120, 1024).rearrange("p (b c) -> p b c", b=2)
        sm0 = cut(5120, 1024).rearrange("p (h s) -> p h s", h=NH)
        score = [cut(6144, P), cut(6272, 2 * P)]
        uT = cut(6656, NG * (PAD + S)).rearrange("p (g s) -> p g s", g=NG)
        PT0 = cut(6656, 1024).rearrange("p (h s) -> p h s", h=NH)
        mixed = cut(7744, 1024).rearrange("p (g s) -> p g s", g=NG)
        s2 = cut(8768, NG * (PAD + S)).rearrange("p (g s) -> p g s", g=NG)
        s4 = cut(8768 + NG * (PAD + S), (NG - 1) * (PAD + S)).rearrange("p (g s) -> p g s", g=NG - 1)
        s8 = cut(10816, (NG - 2) * (PAD + S)).rearrange("p (g s) -> p g s", g=NG - 2)
        s16 = cut(10816 + 544, PAD + S).rearrange("p (g s) -> p g s", g=1)
        mT = cut(8768, 2048).rearrange("p (k s) -> p k s", k=KD)
        y1T = cut(10816, 1024).rearrange("p (g s) -> p g s", g=NG)
        oT = cut(11840, 1024).rearrange("p (c s) -> p c s", s=S)
        mix_tmp = PT1.rearrange("p h k s -> p (h k s)").rearrange("p (b s) -> p b s", b=4)
        poolw_sb = hn[:, 0, 0:NG * P].rearrange("p (g d) -> p g d", g=NG)
        bp_sb = stream[:, 0:2, :].rearrange("p a (c n) -> p (a c) n", n=D)
        ba_sb = stream[:, 2:4, :].rearrange("p a (c n) -> p (a c) n", n=D)
        wide = stream[:, :, :].rearrange("p a (c n) -> p (a c) n", n=D)

        ppj = cut(2048, 2048).rearrange("p (t n) -> p t n", t=NT)
        combT = work[0:E, 7424:7424 + S]
        b2_rows = work[0:E, 7744:7744 + D]
        p_sb = cut(6144, 512).rearrange("p (t n) -> p t n", t=NT)
        pT = cut(6656, 512).rearrange("p (k s) -> p k s", k=2)
        proj_sb = cut(8768, 2048).rearrange("p (k n) -> p k n", k=2)
        router_sb = cut(7168, KD * E).rearrange("p (k e) -> p k e", e=E)
        h2T = hT

        b1_sb = cut(4096, 2 * F)
        xg_rows = cut(0, HALF)
        xgT = cut(512, KD * SLOT).rearrange("p (c q j) -> p c q j", q=2, j=SLOT)
        sel = cut(1024, NT * SLOT).rearrange("p (t j) -> p t j", t=NT)
        gsel = cut(1152, NT * 2 * SLOT).rearrange("p (t q j) -> p t q j", t=NT, q=2)
        gselT = cut(1408, S)
        pick = cut(1664, SLOT)
        y_sb = cut(7168, HALF)
        lin = cut(7744, HALF)
        up = cut(8256, HALF)
        sigm = cut(10816, HALF)
        actT = cut(11328, HALF).rearrange("p (c q j) -> p c q j", q=2, j=SLOT)
        act_rows = cut(11840, HALF)

        final_gain = cut(8768, D)
        sgate = cut(4096, 2048).rearrange("p (b n) -> p b n", b=4)

        bank = [ctx.enter_context(nc.psum_tensor(f"bank{i}", [P, HALF], f32)) for i in range(8)]
        lin_ps, up_ps, xg_ps, y_ps = [bank[i][:, :] for i in range(4)]

        def pair(b):
            return bank[b][:, :].rearrange("p (c s) -> p c s", c=2)

        acc = bank[4:8]

        gain_in, pool_in, scale_in = sem("gain_in"), sem("pool_in"), sem("scale_in")
        x_in = [sem(f"x_in{t}") for t in range(NT)]
        stream_in = [sem(f"stream_in{i}") for i in range(NSTREAM)]
        ring_in = [sem(f"ring_in{i}") for i in range(NRING)]
        ring_used = [sem(f"ring_used{i}") for i in range(NRING)]
        rb_in, router_in, b1_in, b2_in, p_in, proj_in = sem("rb_in"), sem("router_in"), sem("b1_in"), sem("b2_in"), sem("p_in"), sem("proj_in")
        gain2_in, gain3_in, final_in, plew_in = sem("gain2_in"), sem("gain3_in"), sem("final_in"), sem("plew_in")
        branch_in = [sem("branch_pool_in"), sem("branch_attn_in")]
        wout_in = [sem("wout_low_in"), sem("wout_high_in")]
        out_sem = sem("out_written")

        STEPS = {
            "pe": (
                "hT0 hT1 hT2 hT3 scaleT ki wi qi0 qi1 k v ix0e ix0o ix1a ix1b ix1c ix1d q0 q1 u0 u1 g0 g1 g2 g3 "
                "sc0e sc0o sc1a sc1b sc1c sc1d g4 g5 g6 g7 y1a y1b PT0a PT0b PT1a PT1b PT1c PT1d o0 o1 yp0 yp1 "
                "yp2 yp3 ya0 ya1 ya2 ya3 wout pT ppj h2T0 h2T1 h2T2 h2T3 logits pos count combT comb_b2 hpT0 hpT1 "
                "hpT2 hpT3 pg0 pg1 pg2 pg3").split(),
            "act": (
                "sq0 sq1 std hT0 hT2 scale ki0 ki1 qi0 qi1 k0 k1 relu0 relu1 relu2 relu3 relu4 relu5 q0 q1 u0 u1 "
                "sg0 sg1 sg2 sg3 exp0 sg4 sg5 exp1 sg6 sg7 PT0a PT0b PT1a PT1b PT1c PT1d o0 o1 sq20 sq21 std2 pT "
                "ppj0 ppj1 h2T0 h2T2 rexp0 rexp1 combT sq30 sq31 std3 hpT0 hpT2 sgp0 sgp1 sgp2 sgp3 sqf0 sqf1 "
                "stdf").split(),
            "dve": (
                "ms rstd h0 h1 hT1 hT3 first_inv wi k2 k3 v ix0h0 ix0h1 ix0h2 ix0h3 ix0h4 ix0h5 ix0h6 ix0 ix1h0 "
                "ix1h1 ix1h2 ix1h3 ix1h4 ix1h5 ix1h6 ix1 tk0m0 tk1m0 tk0r0 tk1r0 tk0m1 tk1m1 tk0r1 tk1r1 tk0m2 "
                "tk1m2 tk0r2 tk1r2 tk0m3 tk1m3 tk0r3 tk1r3 tk0m4 tk1m4 tk0r4 tk1r4 tk0m5 tk1m5 tk0r5 tk1r5 tk0m6 "
                "tk1m6 tk0r6 tk1r6 tk0m7 tk1m7 tk0r7 tk1r7 neg0 neg1 msk0e msk0o max0 nmax0 msk1a msk1b msk1c "
                "msk1d rcp0 P0 max1 nmax1 rcp1 P1 y1a y1b yp0 yp1 yp2 yp3 ya0 ya1 ya2 ya3 x1a x1b x1c x1d ms2 "
                "rstd2 h20 h21 ppj2 ppj3 h2T1 h2T3 l top0 top1 nm t4 mr0 mr1 mask em rs rr gt cmax over osum "
                "iters p1 p2 pm1 gm1 pm2 gm2 pm3 gm3 sel_first x2a x2b x2c x2d ms3 rstd3 h30 h31 hpT1 hpT3 pl0 "
                "x30 pl1 x31 pl2 x32 pl3 x33 msf rstdf o0 o1").split(),
            "pool": (
                "ident0 ident tri0 tri ones slot_no pad iota inv_min causal0 causal1 s2 s4 s8 s16 mx0 mx1 mx2 mx3 "
                "fix0 fix1 fix2 fix3 mixed causal_neg0 causal_neg1 m0 m1 m2 m3 b1_zero lpad endcol").split(),
        }
        STEP_SEM = {e: sem(f"{e}_step") for e in STEPS}
        AT = {e: {n: i + 1 for i, n in enumerate(names)} for e, names in STEPS.items()}
        told = {e: [] for e in STEPS}

        def tell(engine, name):
            told[engine].append(name)
            assert STEPS[engine][len(told[engine]) - 1] == name, (engine, name, len(told[engine]))
            return STEP_SEM[engine], 1

        def done(engine, name):
            return STEP_SEM[engine], AT[engine][name]

        xg_ready, act_ready = sem("xg_ready"), sem("act_ready")
        sel_ready, gsel_ready = sem("sel_ready"), sem("gsel_ready")
        picked, xg_turned, xgT_ready = sem("picked"), sem("xg_turned"), sem("xgT_ready")
        act_turned, actT_ready = sem("act_turned"), sem("actT_ready")
        gathered, gsel_turned, gselT_ready = sem("gathered"), sem("gsel_turned"), sem("gselT_ready")
        lin_ready, up_ready = sem("lin_ready"), sem("up_ready")
        sig_ready, prod_ready = sem("sig_ready"), sem("prod_ready")
        y_ready, scattered = sem("y_ready"), sem("scattered")

        block = ctx.enter_context(nc.Block())

        w1_v = exp_w1[0].rearrange("e (k p) n -> e p k n", p=P)
        w2_v = exp_w2[0].rearrange("e (u k p) n -> e u p k n", p=P, k=2)

        @block.sync
        def _(sp):
            def load_unit(e, u):
                if u < KD:
                    return sp.dma_start(ring[:, u, :], w1_v[e, :, u, :])
                return sp.dma_start(ring[:, u, :].rearrange("p (k n) -> p k n", k=2), w2_v[e, u - KD])

            for t in range(NT):
                sp.dma_start(x_sb[:, t, :], x_d[0, t * P:(t + 1) * P, :]).then_inc(x_in[t], 16)
            sp.dma_start(gain[:, :], norm1_g[0].partition_broadcast(P)).then_inc(gain_in, 16)

            def load_group(i):
                c0, n = GROUPS[i]
                s = i % NSTREAM
                dst = stream[:, s, 0:KD * n].rearrange("p (k n) -> p k n", n=n)
                if i >= NSTREAM:
                    sp.wait_ge(*done("pe", GROUP_STEPS[i - NSTREAM]))
                sp.dma_start(dst, w_in[0, :, c0:c0 + n].rearrange("(k p) n -> p k n", p=P)).then_inc(stream_in[s], 16)

            for i in range(NSTREAM):
                load_group(i)
            sp.dma_start(scale_rows[:, :], pool_scale[0].rearrange("(g p) -> g p", p=P)).then_inc(scale_in, 16)
            sp.dma_start(rb_row[:, :], router_b[0:1, :]).then_inc(rb_in, 16)
            for i in range(NSTREAM, len(GROUPS)):
                load_group(i)
                if i < NSTREAM + KD:
                    load_unit(0, i - NSTREAM).then_inc(ring_in[i - NSTREAM], 16)
                if i == NSTREAM:
                    sp.wait_ge(*done("dve", "h1"))
                    sp.wait_ge(*done("pe", "hT3"))
                    sp.dma_start(poolw_sb, pool_w[0].rearrange("g c d -> c g d")).then_inc(pool_in, 16)
            G = len(GROUPS)
            sp.wait_ge(*done("pe", GROUP_STEPS[G - 3]))
            sp.dma_start(bp_sb, w_bp[0].rearrange("(c p) n -> p c n", p=P)).then_inc(branch_in[0], 16)
            sp.wait_ge(*done("pe", GROUP_STEPS[G - 1]))
            sp.dma_start(ba_sb, w_ba[0].rearrange("(c p) n -> p c n", p=P)).then_inc(branch_in[1], 16)
            wo_v = w_out[0].rearrange("(k p) n -> p k n", p=P)
            sp.wait_ge(*done("pe", "yp3"))
            sp.dma_start(wide[:, 0:4, :], wo_v[:, 0:4, :]).then_inc(wout_in[0], 16)
            sp.wait_ge(*done("pe", "ya3"))
            sp.dma_start(wide[:, 4:8, :], wo_v[:, 4:8, :]).then_inc(wout_in[1], 16)
            sp.wait_ge(*done("pool", "m3"))
            for u in range(KD, NRING):
                load_unit(0, u).then_inc(ring_in[u], 16)
            sp.wait_ge(*done("pe", "wout"))
            sp.dma_start(wide, ple_gate_w[0].rearrange("(k p) n -> p k n", p=P)).then_inc(plew_in, 16)
            sp.wait_ge(*done("dve", "iters"))
            n_it = sp.value_load(iters[0:1, 0:1], min_val=E, max_val=MAXIT)
            e_reg = sp.alloc_register("expert")
            with sp.Fori(1, n_it) as it:
                sp.reg_alu(e_reg, it, E - 1, ALU.bitwise_and)
                e = sp.snap(e_reg, min_val=0, max_val=E - 1)
                turn = sp.snap(it)
                for u in range(NRING):
                    sp.wait_ge(ring_used[u], turn)
                    load_unit(e, u).then_inc(ring_in[u], 16)
            for t in range(NT):
                sp.wait_ge(*done("dve", f"o{t}"))
                sp.dma_start(out_d[0, t * P:(t + 1) * P, :], hn[:, t, :]).then_inc(out_sem, 16)
            sp.wait_ge(out_sem, 16 * NT)

        @block.gpsimd
        def _(pool):
            g = nc.gpsimd
            g.memset(ident[:, :], 0.0).then_inc(*tell("pool", "ident0"))
            pool.wait_ge(*done("pool", "ident0"))
            g.affine_select(out=ident[:, :], in_=ident[:, :], compare_op=ALU.not_equal, fill=1.0, base=0,
                            pattern=[[-1, P]], channel_multiplier=1).then_inc(*tell("pool", "ident"))
            g.memset(tri[:, :], 1.0).then_inc(*tell("pool", "tri0"))
            pool.wait_ge(*done("pool", "tri0"))
            g.affine_select(out=tri[:, :], in_=tri[:, :], compare_op=ALU.is_gt, fill=0.0, base=0,
                            pattern=[[1, P]], channel_multiplier=-1).then_inc(*tell("pool", "tri"))
            g.memset(ones[:, :], 1.0).then_inc(*tell("pool", "ones"))
            g.iota(slot_no[:, :, :], [[0, 2], [1, SLOT]], base=0, channel_multiplier=0,
                   allow_small_or_imprecise_dtypes=True).then_inc(*tell("pool", "slot_no"))
            g.memset(uT[:, :, 0:PAD], 0.0).then_inc(*tell("pool", "pad"))
            g.iota(first_inv[:, :, :], [[0, NG], [1, PAD]], base=1, channel_multiplier=0,
                   allow_small_or_imprecise_dtypes=True).then_inc(*tell("pool", "iota"))
            pool.wait_ge(*done("pool", "iota"))
            for i, w in enumerate(WINDOWS):
                last = g.tensor_scalar(first_inv[:, i, :], first_inv[:, i, :], float(w), None, ALU.min)
            last.then_inc(*tell("pool", "inv_min"))
            for t in range(NT):
                pool.wait_ge(*done("dve", f"ix{t}"))
                g.affine_select(out=score[t], in_=score[t], compare_op=ALU.is_ge, fill=FILL, base=t * P,
                                pattern=[[-1, (t + 1) * P]], channel_multiplier=1).then_inc(*tell("pool", f"causal{t}"))
            W = PAD + S
            pool.wait_ge(*done("pool", "pad"))
            pool.wait_ge(*done("act", "u1"))
            g.tensor_tensor(s2[:, :, 1:W], uT[:, :, 1:W], uT[:, :, 0:W - 1], ALU.add).then_inc(*tell("pool", "s2"))
            pool.wait_ge(*done("pool", "s2"))
            g.tensor_tensor(s4[:, :, 3:W], s2[:, 1:, 3:W], s2[:, 1:, 1:W - 2], ALU.add).then_inc(*tell("pool", "s4"))
            pool.wait_ge(*done("pool", "s4"))
            g.tensor_tensor(s8[:, :, 7:W], s4[:, 1:, 7:W], s4[:, 1:, 3:W - 4], ALU.add).then_inc(*tell("pool", "s8"))
            pool.wait_ge(*done("pool", "s8"))
            g.tensor_tensor(s16[:, :, 15:W], s8[:, 1:, 15:W], s8[:, 1:, 7:W - 8], ALU.add).then_inc(*tell("pool", "s16"))
            pool.wait_ge(*done("pool", "s16"))
            sums = [s2[:, 0, :], s4[:, 0, :], s8[:, 0, :], s16[:, 0, :]]
            for i, w in enumerate(WINDOWS):
                g.tensor_scalar(mixed[:, i, :], sums[i][:, PAD:W], 1.0 / w, None, ALU.mult)\
                    .then_inc(*tell("pool", f"mx{i}"))
            pool.wait_ge(*done("pool", "mx3"))
            pool.wait_ge(*done("dve", "first_inv"))
            for i in range(NG):
                g.tensor_tensor(mixed[:, i, 0:PAD], sums[i][:, PAD:2 * PAD], first_inv[:, i, :], ALU.mult)\
                    .then_inc(*tell("pool", f"fix{i}"))
            pool.wait_ge(*done("pool", "fix3"))
            g.tensor_tensor(mixed[:, :, :], mixed[:, :, :], uT[:, :, PAD:W], ALU.subtract).then_inc(*tell("pool", "mixed"))
            for t in range(NT):
                pool.wait_ge(*done("dve", f"neg{t}"))
                g.affine_select(out=score[t], in_=score[t], compare_op=ALU.is_ge, fill=-1.0, base=t * P,
                                pattern=[[-1, (t + 1) * P]], channel_multiplier=1)\
                    .then_inc(*tell("pool", f"causal_neg{t}"))
            pool.wait_ge(*done("dve", "h1"))
            g.dma_start(gain[:, :], norm2_g[0].partition_broadcast(P)).then_inc(gain2_in, 16)
            for i in range(4):
                pool.wait_ge(*done("dve", f"ya{i}"))
                g.tensor_tensor(mT[:, 2 * i:2 * i + 2, :], mT[:, 2 * i:2 * i + 2, :],
                                mix_tmp[:, i, :].rearrange("p (c s) -> p c s", c=2), ALU.add)\
                    .then_inc(*tell("pool", f"m{i}"))
            g.memset(b1_sb, 0.0).then_inc(*tell("pool", "b1_zero"))
            g.dma_start(b2_rows, exp_b2[0]).then_inc(b2_in, 16)
            g.dma_start(p_sb, p_d[0, 0].rearrange("(t p) n -> p t n", p=P)).then_inc(p_in, 16)
            g.dma_start(router_sb[:, :, :], router_w[0].rearrange("(k p) e -> p k e", p=P)).then_inc(router_in, 16)
            pool.wait_ge(*done("pool", "b1_zero"))
            g.dma_start(work[0:E, 4096:4096 + 2 * F], exp_b1[0]).then_inc(b1_in, 16)
            g.memset(lpad[:, :, E:E + 4], FILL).then_inc(*tell("pool", "lpad"))
            g.memset(pos[:, :, MAXIT:MAXIT + 1], -1.0)
            g.memset(gate[:, :, MAXIT:MAXIT + 1], 0.0).then_inc(*tell("pool", "endcol"))
            pool.wait_ge(*done("pe", "wout"))
            g.dma_start(proj_sb, ple_proj_w[0].rearrange("(k p) n -> p k n", p=P)).then_inc(proj_in, 16)
            pool.wait_ge(*done("dve", "h21"))
            g.dma_start(gain[:, :], ple_norm_g[0].partition_broadcast(P)).then_inc(gain3_in, 16)
            pool.wait_ge(*done("pe", "ppj"))
            g.dma_start(final_gain, final_g.partition_broadcast(P)).then_inc(final_in, 16)

        @block.scalar
        def _(act):
            a = nc.scalar

            def norm_stats(names, source_ready):
                for t in range(NT):
                    act.wait_ge(*source_ready[t])
                    a.activation(hn[:, t, :], x_sb[:, t, :], ACT.Square, accum_out=ss[:, t:t + 1])\
                        .then_inc(*tell("act", names[t]))
                act.wait_ge(*done("dve", names[2]))
                a.activation(rstd[:, :], ss[:, :], ACT.Sqrt).then_inc(*tell("act", names[3]))

            def evacuate(name, dst, src, func=ACT.Copy, **kw):
                act.wait_ge(*done("pe", name))
                return a.activation(dst, src, func, **kw)

            norm_stats(["sq0", "sq1", "ms", "std"], [(x_in[0], 16), (x_in[1], 16)])
            for b in (0, 2):
                evacuate(f"hT{b}", hT[:, 2 * b:2 * b + 2, :], pair(b)).then_inc(*tell("act", f"hT{b}"))
            evacuate("scaleT", scale_col[:, :], bank[4][:, 0:NG]).then_inc(*tell("act", "scale"))
            evacuate("ki", kiT[0:DH, :], bank[4][0:DH, 0:S]).then_inc(*tell("act", "ki0"))
            evacuate("ki", kiT[DH:P, :], bank[4][0:DH, 0:S]).then_inc(*tell("act", "ki1"))
            evacuate("qi0", qiT[:, 0:2, :], pair(6)).then_inc(*tell("act", "qi0"))
            evacuate("qi1", qiT[:, 2:4, :], pair(7)).then_inc(*tell("act", "qi1"))
            evacuate("k", kT[0:DH, 0, :], bank[0][0:DH, 0:S]).then_inc(*tell("act", "k0"))
            evacuate("k", kT[DH:P, 0, :], bank[0][0:DH, 0:S]).then_inc(*tell("act", "k1"))
            for i, (name, b) in enumerate([("ix0e", 2), ("ix0o", 3), ("ix1a", 4), ("ix1b", 5), ("ix1c", 6), ("ix1d", 7)]):
                if i >= 2:
                    act.wait_ge(*done("dve", ["ix0h3", "ix0", "ix1h1", "ix1h3"][i - 2]))
                evacuate(name, relu[:, i % 2, :], bank[b][:, :], ACT.Relu, scale=DH ** -0.5)\
                    .then_inc(*tell("act", f"relu{i}"))
            for i in range(2):
                evacuate(f"q{i}", qT[:, 2 * i:2 * i + 2, :], pair(i)).then_inc(*tell("act", f"q{i}"))
            for i in range(2):
                evacuate(f"u{i}", uT[:, 2 * i:2 * i + 2, PAD:PAD + S],
                         pair(2 + i)).then_inc(*tell("act", f"u{i}"))

            def gates(i):
                b = 4 + i if i < 4 else 6 + i % 2
                evacuate(f"g{i}", sgT[:, 2 * i:2 * i + 2, :], pair(b),
                         ACT.Sigmoid).then_inc(*tell("act", f"sg{i}"))

            def exps(t, sm):
                act.wait_ge(*done("dve", f"nmax{t}"))
                for h in range(NH):
                    last = a.activation(sm[:, h, :], sm[:, h, :], ACT.Exp, bias=smax[:, h:h + 1],
                                        scale=DH ** -0.5, accum_out=ssum[:, h:h + 1])
                last.then_inc(*tell("act", f"exp{t}"))

            for i in range(4):
                gates(i)
            exps(0, sm0)
            gates(4)
            gates(5)
            exps(1, sm1)
            gates(6)
            gates(7)
            for i, n in enumerate("ab"):
                evacuate(f"PT0{n}", PT0[:, 4 * i:4 * i + 4, :], bank[i][:, :].rearrange("p (h s) -> p h s", s=P)).then_inc(*tell("act", f"PT0{n}"))
            for i, n in enumerate("abcd"):
                evacuate(f"PT1{n}", PT1[:, 2 * i:2 * i + 2, :, :].rearrange("p h k s -> p (h k s)"), bank[2 + i][:, :])\
                    .then_inc(*tell("act", f"PT1{n}"))
            for t in range(NT):
                evacuate(f"o{t}", oT[:, :, t * P:(t + 1) * P], bank[6 + t][:, :].rearrange("p (c s) -> p c s", s=P))\
                    .then_inc(*tell("act", f"o{t}"))
            norm_stats(["sq20", "sq21", "ms2", "std2"], [done("dve", "x1b"), done("dve", "x1d")])
            evacuate("pT", pT[:, :, :], pair(0)).then_inc(*tell("act", "pT"))
            for i in range(2):
                evacuate("ppj", ppj[:, 0, i * HALF:(i + 1) * HALF], bank[2 + i][:, :]).then_inc(*tell("act", f"ppj{i}"))
            for b in (0, 2):
                evacuate(f"h2T{b}", h2T[:, 2 * b:2 * b + 2, :], pair([6, 7, 0, 1][b]))\
                    .then_inc(*tell("act", f"h2T{b}"))
            for t in range(NT):
                act.wait_ge(*done("dve", "nm"))
                a.activation(expl[:, t, :], lpad[:, t, 0:E], ACT.Exp, bias=least[:, t:t + 1]).then_inc(*tell("act", f"rexp{t}"))
            evacuate("combT", combT, bank[3][0:E, 0:S]).then_inc(*tell("act", "combT"))
            act.wait_ge(gathered, 1)
            a.activation(xg_rows, xg_ps, ACT.Copy).then_inc(xg_ready, 1)
            act.wait_ge(xg_turned, 1)
            a.activation(xgT, xg_ps.rearrange("p (c q j) -> p c q j", q=2, j=SLOT), ACT.Copy).then_inc(xgT_ready, 1)

            act.wait_ge(*done("dve", "iters"))
            n_it = act.value_load(iters[0:1, 0:1], min_val=E, max_val=MAXIT)
            with act.Fori(0, n_it) as it:
                turn = act.snap(it + 1)
                turn_next = act.snap(it + 2)
                act.wait_ge(gsel_turned, turn)
                a.activation(gselT, y_ps[:, 0:S], ACT.Copy).then_inc(gselT_ready, 1)
                act.wait_ge(lin_ready, turn)
                a.activation(sigm, lin, ACT.Sigmoid, scale=1.702).then_inc(sig_ready, 1)
                act.wait_ge(gathered, turn_next)
                a.activation(xg_rows, xg_ps, ACT.Copy).then_inc(xg_ready, 1)
                act.wait_ge(act_turned, turn)
                a.activation(actT, y_ps.rearrange("p (c q j) -> p c q j", q=2, j=SLOT), ACT.Copy).then_inc(actT_ready, 1)
                act.wait_ge(xg_turned, turn_next)
                a.activation(xgT, xg_ps.rearrange("p (c q j) -> p c q j", q=2, j=SLOT), ACT.Copy).then_inc(xgT_ready, 1)

            norm_stats(["sq30", "sq31", "ms3", "std3"], [done("dve", "x2b"), done("dve", "x2d")])
            for b in (0, 2):
                evacuate(f"hpT{b}", hT[:, 2 * b:2 * b + 2, :], pair(b))\
                    .then_inc(*tell("act", f"hpT{b}"))
            for i in range(4):
                evacuate(f"pg{i}", sgate[:, i, :], bank[4 + i][:, :], ACT.Sigmoid).then_inc(*tell("act", f"sgp{i}"))
            norm_stats(["sqf0", "sqf1", "msf", "stdf"], [done("dve", "x31"), done("dve", "x33")])

        @block.vector
        def _(dve):
            v = nc.vector

            def rms(names, stats, std, gain_sem, gain_ap):
                dve.wait_ge(*done("act", stats))
                v.tensor_scalar(ss[:, :], ss[:, :], 1.0 / D, EPS, ALU.mult, ALU.add).then_inc(*tell("dve", names[0]))
                dve.wait_ge(*done("act", std))
                v.reciprocal(rstd[:, :], rstd[:, :]).then_inc(*tell("dve", names[1]))
                dve.wait_ge(*done("dve", names[1]))
                dve.wait_ge(gain_sem, 16)
                for t in range(NT):
                    v.scalar_tensor_tensor(hn[:, t, :], x_sb[:, t, :], rstd[:, t:t + 1], gain_ap, ALU.mult, ALU.mult)\
                        .then_inc(*tell("dve", names[2 + t]))

            rms(["ms", "rstd", "h0", "h1"], "sq1", "std", gain_in, gain[:, :])
            for b in (1, 3):
                dve.wait_ge(*done("pe", f"hT{b}"))
                v.tensor_copy(hT[:, 2 * b:2 * b + 2, :], pair(b))\
                    .then_inc(*tell("dve", f"hT{b}"))
            dve.wait_ge(*done("pool", "inv_min"))
            v.reciprocal(first_inv[:, :, :], first_inv[:, :, :]).then_inc(*tell("dve", "first_inv"))
            dve.wait_ge(*done("pe", "wi"))
            v.tensor_scalar(wi_sb[:, :, :], bank[5][:, 0:NT * NH].rearrange("p (t h) -> p t h", t=NT),
                            NH ** -0.5, None, ALU.mult).then_inc(*tell("dve", "wi"))
            dve.wait_ge(*done("pe", "k"))
            v.tensor_copy(kT[0:DH, 1, :], bank[0][DH:P, 0:S]).then_inc(*tell("dve", "k2"))
            v.tensor_copy(kT[DH:P, 1, :], bank[0][DH:P, 0:S]).then_inc(*tell("dve", "k3"))
            dve.wait_ge(*done("pe", "v"))
            v.tensor_copy(v_sb[:, :, :], bank[1][:, 0:NT * P].rearrange("p (t c) -> p t c", t=NT))\
                .then_inc(*tell("dve", "v"))
            dve.wait_ge(*done("dve", "wi"))
            for t in range(NT):
                n = (t + 1) * P
                per = HALF // n
                order = [0, 2, 4, 6, 1, 3, 5, 7] if t == 0 else [0, 2, 1, 3, 4, 6, 5, 7]
                for i, h in enumerate(order):
                    b = (0 if t == 0 else 2) + i // per
                    dve.wait_ge(*done("act", f"relu{b}"))
                    r = relu[:, b % 2, (i % per) * n:(i % per + 1) * n]
                    name = f"ix{t}" if i == NH - 1 else f"ix{t}h{i}"
                    if i == 0:
                        v.tensor_scalar(score[t], r, wi_sb[:, t, h:h + 1], None, ALU.mult).then_inc(*tell("dve", name))
                    else:
                        dve.wait_ge(*done("dve", f"ix{t}h{i - 1}"))
                        v.scalar_tensor_tensor(score[t], r, wi_sb[:, t, h:h + 1], score[t], ALU.mult, ALU.add)\
                            .then_inc(*tell("dve", name))
            for r in range(TOPK // 8):
                for t in range(NT):
                    dve.wait_ge(*(done("dve", f"tk{t}r{r - 1}") if r else done("pool", f"causal{t}")))
                    v.max(top8[:, t, :], score[t]).then_inc(*tell("dve", f"tk{t}m{r}"))
                for t in range(NT):
                    dve.wait_ge(*done("dve", f"tk{t}m{r}"))
                    v.match_replace(score[t], top8[:, t, :], score[t], TAKEN).then_inc(*tell("dve", f"tk{t}r{r}"))
            for t in range(NT):
                dve.wait_ge(*done("dve", f"tk{t}r{TOPK // 8 - 1}"))
                v.tensor_scalar(score[t], score[t], TAKEN, 1.0, ALU.is_equal, ALU.subtract).then_inc(*tell("dve", f"neg{t}"))

            def masked(t, name, pe_name, b, heads, sm):
                n = (t + 1) * P
                dve.wait_ge(*done("pe", pe_name))
                v.scalar_tensor_tensor(sm[:, heads, :], score[t].rearrange("p (o s) -> p o s", o=1).broadcast_to([P, HALF // n, n]),
                                       BIG, bank[b][:, :].rearrange("p (h s) -> p h s", s=n), ALU.mult, ALU.add)\
                    .then_inc(*tell("dve", name))

            def row_max(t, sm, last):
                dve.wait_ge(*done("dve", last))
                if t:
                    dve.wait_ge(*done("act", "exp0"))
                v.tensor_reduce(smax[:, :], sm, AX.X, ALU.max).then_inc(*tell("dve", f"max{t}"))
                dve.wait_ge(*done("dve", f"max{t}"))
                v.tensor_scalar(smax[:, :], smax[:, :], -(DH ** -0.5), None, ALU.mult).then_inc(*tell("dve", f"nmax{t}"))

            def normalise(t, sm):
                n = (t + 1) * P
                dve.wait_ge(*done("act", f"exp{t}"))
                v.reciprocal(ssum[:, :], ssum[:, :]).then_inc(*tell("dve", f"rcp{t}"))
                dve.wait_ge(*done("dve", f"rcp{t}"))
                v.tensor_tensor(sm, sm, ssum[:, :].rearrange("p (h o) -> p h o", o=1).broadcast_to([P, NH, n]), ALU.mult)\
                    .then_inc(*tell("dve", f"P{t}"))

            dve.wait_ge(*done("pool", "causal_neg0"))
            masked(0, "msk0e", "sc0e", 0, slice(0, NH, 2), sm0)
            masked(0, "msk0o", "sc0o", 1, slice(1, NH, 2), sm0)
            row_max(0, sm0, "msk0o")
            dve.wait_ge(*done("pool", "causal_neg1"))
            masked(1, "msk1a", "sc1a", 2, slice(0, 4, 2), sm1)
            masked(1, "msk1b", "sc1b", 3, slice(1, 4, 2), sm1)
            masked(1, "msk1c", "sc1c", 4, slice(4, NH, 2), sm1)
            masked(1, "msk1d", "sc1d", 5, slice(5, NH, 2), sm1)
            normalise(0, sm0)
            row_max(1, sm1, "msk1d")
            normalise(1, sm1)
            for i, n in enumerate("ab"):
                dve.wait_ge(*done("pe", f"y1{n}"))
                dve.wait_ge(*done("act", "scale"))
                v.tensor_tensor(y1T[:, 2 * i:2 * i + 2, :], pair(i),
                                scale_col[:, 2 * i:2 * i + 2].rearrange("p (c o) -> p c o", o=1).broadcast_to([P, 2, S]),
                                ALU.mult).then_inc(*tell("dve", f"y1{n}"))
            for i in range(4):
                dve.wait_ge(*done("pe", f"yp{i}"))
                v.tensor_tensor(mT[:, 2 * i:2 * i + 2, :], pair(2 + i),
                                sgT[:, 2 * i:2 * i + 2, :], ALU.mult).then_inc(*tell("dve", f"yp{i}"))
            dve.wait_ge(*done("pe", "o1"))
            for i in range(4):
                dve.wait_ge(*done("pe", f"ya{i}"))
                v.tensor_tensor(mix_tmp[:, i, :].rearrange("p (c s) -> p c s", c=2),
                                pair([6, 7, 0, 1][i]),
                                sgT[:, KD + 2 * i:KD + 2 * i + 2, :], ALU.mult).then_inc(*tell("dve", f"ya{i}"))

            def residual(names, banks):
                for i, b in enumerate(banks):
                    xs = x_sb[:, i // 2, (i % 2) * HALF:(i % 2 + 1) * HALF]
                    v.tensor_tensor(xs, xs, bank[b][:, :], ALU.add).then_inc(*tell("dve", names[i]))

            dve.wait_ge(*done("pe", "wout"))
            residual(["x1a", "x1b", "x1c", "x1d"], [2, 3, 4, 5])
            rms(["ms2", "rstd2", "h20", "h21"], "sq21", "std2", gain2_in, gain[:, :])
            for i in range(2):
                dve.wait_ge(*done("pe", "ppj"))
                v.tensor_copy(ppj[:, 1, i * HALF:(i + 1) * HALF], bank[4 + i][:, :]).then_inc(*tell("dve", f"ppj{2 + i}"))
            for b in (1, 3):
                dve.wait_ge(*done("pe", f"h2T{b}"))
                v.tensor_copy(h2T[:, 2 * b:2 * b + 2, :], pair([6, 7, 0, 1][b]))\
                    .then_inc(*tell("dve", f"h2T{b}"))

            dve.wait_ge(*done("pe", "logits"))
            dve.wait_ge(*done("pool", "endcol"))
            v.tensor_copy(lpad[:, :, 0:E], bank[2][:, 0:NT * E].rearrange("p (t e) -> p t e", t=NT)).then_inc(*tell("dve", "l"))
            dve.wait_ge(*done("dve", "l"))
            for t in range(NT):
                v.max(top4[:, t, :], lpad[:, t, :]).then_inc(*tell("dve", f"top{t}"))
            dve.wait_ge(*done("dve", "top1"))
            v.tensor_scalar(least[:, :], top4[:, :, 0], -1.0, None, ALU.mult).then_inc(*tell("dve", "nm"))
            v.memset(top4[:, :, TOPE:8], FILL).then_inc(*tell("dve", "t4"))
            dve.wait_ge(*done("dve", "t4"))
            dve.wait_ge(*done("act", "rexp1"))
            for t in range(NT):
                v.match_replace(lpad[:, t, :], top4[:, t, :], lpad[:, t, :], TAKEN).then_inc(*tell("dve", f"mr{t}"))
            dve.wait_ge(*done("dve", "mr1"))
            v.tensor_scalar(mask[:, :, :], lpad[:, :, 0:E], TAKEN, None, ALU.is_equal).then_inc(*tell("dve", "mask"))
            dve.wait_ge(*done("dve", "mask"))
            v.tensor_tensor(expl[:, :, :], expl[:, :, :], mask[:, :, :], ALU.mult).then_inc(*tell("dve", "em"))
            dve.wait_ge(*done("dve", "em"))
            v.tensor_reduce(gsum[:, :], expl[:, :, :], AX.X, ALU.add).then_inc(*tell("dve", "rs"))
            dve.wait_ge(*done("dve", "rs"))
            v.reciprocal(gsum[:, :], gsum[:, :]).then_inc(*tell("dve", "rr"))
            dve.wait_ge(*done("dve", "rr"))
            v.tensor_tensor(gate[:, :, 0:E], expl[:, :, :], gsum[:, :].rearrange("p (t o) -> p t o", o=1).broadcast_to([P, NT, E]),
                            ALU.mult).then_inc(*tell("dve", "gt"))
            dve.wait_ge(*done("pe", "count"))
            v.tensor_reduce(small[:, 3:4], bank[3][:, NT * E:(NT + 1) * E], AX.X, ALU.max).then_inc(*tell("dve", "cmax"))
            dve.wait_ge(*done("dve", "cmax"))
            for i in range(S // SLOT - 1):
                last = v.tensor_scalar(small[:, 4 + i:5 + i], small[:, 3:4], float(SLOT * (i + 1)), float(E), ALU.is_gt, ALU.mult)
            last.then_inc(*tell("dve", "over"))
            dve.wait_ge(*done("dve", "over"))
            v.tensor_reduce(small[:, 1:2], small[:, 4:4 + S // SLOT - 1], AX.X, ALU.add).then_inc(*tell("dve", "osum"))
            dve.wait_ge(*done("dve", "osum"))
            v.tensor_scalar(iters[:, :], small[:, 1:2], float(E), None, ALU.add).then_inc(*tell("dve", "iters"))
            v.scalar_tensor_tensor(pos[:, :, 0:E], bank[3][:, 0:NT * E].rearrange("p (t e) -> p t e", t=NT), 1.0,
                                   mask[:, :, :], ALU.add, ALU.mult).then_inc(*tell("dve", "p1"))
            dve.wait_ge(*done("dve", "p1"))
            v.tensor_scalar(pos[:, :, 0:E], pos[:, :, 0:E], 1.0, None, ALU.subtract).then_inc(*tell("dve", "p2"))
            dve.wait_ge(*done("dve", "p2"))
            for i in range(1, S // SLOT):
                v.tensor_scalar(pos[:, :, i * E:(i + 1) * E], pos[:, :, 0:E], float(SLOT * i), None, ALU.subtract)\
                    .then_inc(*tell("dve", f"pm{i}"))
                if i == 1:
                    dve.wait_ge(*done("dve", "gt"))
                v.tensor_copy(gate[:, :, i * E:(i + 1) * E], gate[:, :, 0:E]).then_inc(*tell("dve", f"gm{i}"))
            dve.wait_ge(*done("dve", f"gm{S // SLOT - 1}"))

            v.tensor_scalar(sel[:, 0, :], slot_no[:, 0, :], pos[:, 0, 0:1], None, ALU.is_equal)
            v.tensor_scalar(sel[:, 1, :], slot_no[:, 0, :], pos[:, 1, 0:1], None, ALU.is_equal).then_inc(*tell("dve", "sel_first"))
            v.tensor_copy(pick[:, :], ident[:, 0:1].broadcast_to([P, SLOT])).then_inc(picked, 1)

            dve.wait_ge(*done("dve", "iters"))
            n_it = dve.value_load(iters[0:1, 0:1], min_val=E, max_val=MAXIT)
            with dve.Fori(0, n_it) as it:
                turn = dve.snap(it + 1)
                e_next = turn & (E - 1)
                dve.wait_ge(gathered, turn)
                for t in range(NT):
                    last = v.tensor_scalar(gsel[:, t, :, :], slot_no[:, :, :], pos[:, t, bass.ds(it, 1)],
                                           gate[:, t, bass.ds(it, 1)], ALU.is_equal, ALU.mult)
                last.then_inc(gsel_ready, 1)
                for t in range(NT):
                    last = v.tensor_scalar(sel[:, t, :], slot_no[:, 0, :], pos[:, t, bass.ds(turn, 1)], None, ALU.is_equal)
                last.then_inc(sel_ready, 1)
                dve.wait_ge(ring_used[0], turn)
                v.tensor_copy(pick[:, :], ident[:, bass.ds(e_next, 1)].broadcast_to([P, SLOT])).then_inc(picked, 1)
                dve.wait_ge(ring_used[KD - 1], turn)
                v.tensor_scalar(lin, lin_ps, 7.0, None, ALU.min).then_inc(lin_ready, 1)
                v.tensor_scalar(up, up_ps, 7.0, -7.0, ALU.min, ALU.max).then_inc(up_ready, 1)
                dve.wait_ge(up_ready, turn)
                dve.wait_ge(lin_ready, turn)
                v.scalar_tensor_tensor(up, up, 1.0, lin, ALU.add, ALU.mult).then_inc(prod_ready, 1)
                dve.wait_ge(prod_ready, turn)
                dve.wait_ge(sig_ready, turn)
                v.tensor_tensor(act_rows, up, sigm, ALU.mult).then_inc(act_ready, 1)
                dve.wait_ge(ring_used[NRING - 1], turn)
                v.tensor_copy(y_sb, y_ps).then_inc(y_ready, 1)

            dve.wait_ge(scattered, n_it)
            residual(["x2a", "x2b", "x2c", "x2d"], [4, 5, 6, 7])
            rms(["ms3", "rstd3", "h30", "h31"], "sq31", "std3", gain3_in, gain[:, :])
            for b in (1, 3):
                dve.wait_ge(*done("pe", f"hpT{b}"))
                v.tensor_copy(hT[:, 2 * b:2 * b + 2, :], pair(b))\
                    .then_inc(*tell("dve", f"hpT{b}"))
            for i in range(4):
                dve.wait_ge(*done("act", f"sgp{i}"))
                v.tensor_tensor(sgate[:, i, :], sgate[:, i, :], ppj[:, i // 2, (i % 2) * HALF:(i % 2 + 1) * HALF], ALU.mult)\
                    .then_inc(*tell("dve", f"pl{i}"))
                dve.wait_ge(*done("dve", f"pl{i}"))
                xs = x_sb[:, i // 2, (i % 2) * HALF:(i % 2 + 1) * HALF]
                v.tensor_tensor(xs, xs, sgate[:, i, :], ALU.add).then_inc(*tell("dve", f"x3{i}"))
            rms(["msf", "rstdf", "o0", "o1"], "sqf1", "stdf", final_in, final_gain)

        @block.tensor
        def _(pe):
            mm = nc.tensor.matmul
            turn_ = nc.tensor.transpose

            pe.wait_ge(*done("pool", "ident"))

            def turn_rows(names, banks, free):
                for b in range(4):
                    if free[b] is not None:
                        pe.wait_ge(*free[b])
                    for i in range(4):
                        k, t = 2 * b + i // 2, i % 2
                        if b == 0:
                            pe.wait_ge(*done("dve", names[4 + t]))
                        last = turn_(bank[banks[b]][:, i * P:(i + 1) * P], hn[:, t, k * P:(k + 1) * P], ident[:, :])
                    last.then_inc(*tell("pe", names[b]))

            turn_rows(["hT0", "hT1", "hT2", "hT3", "h0", "h1"], [0, 1, 2, 3], [None] * 4)
            pe.wait_ge(scale_in, 16)
            turn_(bank[4][:, 0:NG], scale_rows[:, :], ident[0:NG, 0:NG]).then_inc(*tell("pe", "scaleT"))

            def group(i):
                c0, n = GROUPS[i]
                pe.wait_ge(stream_in[i % NSTREAM], 16 * (i // NSTREAM + 1))
                return stream[:, i % NSTREAM, 0:KD * n].rearrange("p (k n) -> p k n", n=n)

            def project_T(i, b, name):
                w = group(i)
                for c in range(GW // P):
                    for k in range(KD):
                        last = mm(bank[b][:, c * S:(c + 1) * S], w[:, k, c * P:(c + 1) * P], hT[:, k, :],
                                  start=(k == 0), stop=(k == KD - 1))
                last.then_inc(*tell("pe", name))

            w = group(0)
            pe.wait_ge(*done("act", "scale"))
            for k in range(KD):
                if k % 2 == 0:
                    pe.wait_ge(*done("act" if k // 2 % 2 == 0 else "dve", f"hT{k // 2}"))
                last = mm(bank[4][0:DH, 0:S], w[:, k, 0:DH], hT[:, k, :], start=(k == 0), stop=(k == KD - 1))
            last.then_inc(*tell("pe", "ki"))
            for t in range(NT):
                for k in range(KD):
                    last = mm(bank[5][:, t * NH:(t + 1) * NH], hT[:, k, t * P:(t + 1) * P], w[:, k, DH:DH + NH],
                              start=(k == 0), stop=(k == KD - 1))
            last.then_inc(*tell("pe", "wi"))
            project_T(1, 6, "qi0")
            project_T(2, 7, "qi1")
            w = group(3)
            for k in range(KD):
                last = mm(bank[0][:, 0:S], w[:, k, 0:P], hT[:, k, :], start=(k == 0), stop=(k == KD - 1))
            last.then_inc(*tell("pe", "k"))
            for t in range(NT):
                for k in range(KD):
                    last = mm(bank[1][:, t * P:(t + 1) * P], hT[:, k, t * P:(t + 1) * P], w[:, k, P:2 * P],
                              start=(k == 0), stop=(k == KD - 1))
            last.then_inc(*tell("pe", "v"))

            def head_products(t, qs, keys, heads, b, name):
                n = (t + 1) * P
                for i, h in enumerate(heads):
                    half = slice(DH * (h % 2), DH * (h % 2) + DH)
                    last = mm(bank[b][:, i * n:(i + 1) * n], qs[half, h // 2, t * P:(t + 1) * P], keys(h)[half, 0:n],
                              start=True, stop=True)
                last.then_inc(*tell("pe", name))

            pe.wait_ge(*done("act", "qi1"))
            pe.wait_ge(*done("dve", "wi"))
            index_keys = lambda h: kiT
            head_products(0, qiT, index_keys, [0, 2, 4, 6], 2, "ix0e")
            head_products(0, qiT, index_keys, [1, 3, 5, 7], 3, "ix0o")
            head_products(1, qiT, index_keys, [0, 2], 4, "ix1a")
            head_products(1, qiT, index_keys, [1, 3], 5, "ix1b")
            head_products(1, qiT, index_keys, [4, 6], 6, "ix1c")
            head_products(1, qiT, index_keys, [5, 7], 7, "ix1d")
            for i, (b, name, free) in enumerate([(0, "q0", ("dve", "k3")), (1, "q1", ("dve", "v")),
                                                 (2, "u0", ("act", "relu0")), (3, "u1", ("act", "relu1"))]):
                if i == 0:
                    pe.wait_ge(*done("act", "k1"))
                pe.wait_ge(*done(*free))
                project_T(4 + i, b, name)
            for i in range(4):
                pe.wait_ge(*done("act", f"relu{2 + i}"))
                project_T(8 + i, 4 + i, f"g{i}")
            head_keys = lambda h: kT[:, h // GROUP, :]
            pe.wait_ge(*done("act", "q1"))
            head_products(0, qT, head_keys, [0, 2, 4, 6], 0, "sc0e")
            head_products(0, qT, head_keys, [1, 3, 5, 7], 1, "sc0o")
            pe.wait_ge(*done("act", "u1"))
            head_products(1, qT, head_keys, [0, 2], 2, "sc1a")
            head_products(1, qT, head_keys, [1, 3], 3, "sc1b")
            pe.wait_ge(*done("act", "sg1"))
            head_products(1, qT, head_keys, [4, 6], 4, "sc1c")
            head_products(1, qT, head_keys, [5, 7], 5, "sc1d")
            for i in range(4, 8):
                pe.wait_ge(*done("act", f"sg{i - 2}"))
                project_T(8 + i, 6 + i % 2, f"g{i}")
            pe.wait_ge(pool_in, 16)
            pe.wait_ge(*done("pool", "mixed"))
            pe.wait_ge(*done("dve", "msk0o"))
            for i, n in enumerate("ab"):
                for c in range(2):
                    last = mm(bank[i][:, c * S:(c + 1) * S], poolw_sb[:, 2 * i + c, :], mixed[:, 2 * i + c, :],
                              start=True, stop=True)
                last.then_inc(*tell("pe", f"y1{n}"))
            pe.wait_ge(*done("dve", "P0"))
            for i, n in enumerate("ab"):
                pe.wait_ge(*done("dve", f"y1{n}"))
                for h in range(4):
                    last = turn_(bank[i][:, h * P:(h + 1) * P], sm0[:, 4 * i + h, :], ident[:, :])
                last.then_inc(*tell("pe", f"PT0{n}"))
            pe.wait_ge(*done("dve", "P1"))
            for i, n in enumerate("abcd"):
                for j in range(4):
                    h, kb = 2 * i + j // 2, j % 2
                    last = turn_(bank[2 + i][:, j * P:(j + 1) * P], sm1[:, h, kb * P:(kb + 1) * P], ident[:, :])
                last.then_inc(*tell("pe", f"PT1{n}"))
            for t in range(NT):
                pe.wait_ge(*done("act", f"sg{6 + t}"))
                pe.wait_ge(*done("act", "PT0b" if t == 0 else "PT1d"))
                for h in range(NH):
                    vh = h // GROUP
                    for kb in range(t + 1):
                        pt = PT0[:, h, :] if t == 0 else PT1[:, h, kb, :]
                        last = mm(bank[6 + t][DH * (h % 2):DH * (h % 2) + DH, (h // 2) * P:(h // 2 + 1) * P],
                                  v_sb[:, kb, vh * DH:(vh + 1) * DH], pt, start=(kb == 0), stop=(kb == t))
                last.then_inc(*tell("pe", f"o{t}"))
            pe.wait_ge(branch_in[0], 16)
            for i in range(4):
                for c in range(2):
                    j = 2 * i + c
                    for k in range(NG):
                        last = mm(bank[2 + i][:, c * S:(c + 1) * S], bp_sb[:, k, j * P:(j + 1) * P], y1T[:, k, :],
                                  start=(k == 0), stop=(k == NG - 1))
                last.then_inc(*tell("pe", f"yp{i}"))
            pe.wait_ge(branch_in[1], 16)
            pe.wait_ge(*done("act", "o1"))
            for i, b in enumerate([6, 7, 0, 1]):
                for c in range(2):
                    j = 2 * i + c
                    for k in range(AW // P):
                        last = mm(bank[b][:, c * S:(c + 1) * S], ba_sb[:, k, j * P:(j + 1) * P], oT[:, k, :],
                                  start=(k == 0), stop=(k == AW // P - 1))
                last.then_inc(*tell("pe", f"ya{i}"))
            pe.wait_ge(*done("dve", "yp3"))
            for k in range(KD):
                if k % 4 == 0:
                    pe.wait_ge(wout_in[k // 4], 16)
                if k % 2 == 0:
                    pe.wait_ge(*done("pool", f"m{k // 2}"))
                for t in range(NT):
                    for n in range(D // HALF):
                        last = mm(bank[2 + 2 * t + n][:, :], mT[:, k, t * P:(t + 1) * P], wide[:, k, n * HALF:(n + 1) * HALF],
                                  start=(k == 0), stop=(k == KD - 1))
            last.then_inc(*tell("pe", "wout"))
            pe.wait_ge(p_in, 16)
            for k in range(2):
                for t in range(NT):
                    last = turn_(bank[0][:, (2 * k + t) * P:(2 * k + t + 1) * P], p_sb[:, t, k * P:(k + 1) * P], ident[:, :])
            last.then_inc(*tell("pe", "pT"))
            pe.wait_ge(*done("act", "pT"))
            pe.wait_ge(proj_in, 16)
            pe.wait_ge(*done("dve", "x1d"))
            for t in range(NT):
                for n in range(D // HALF):
                    for k in range(2):
                        last = mm(bank[2 + 2 * t + n][:, :], pT[:, k, t * P:(t + 1) * P], proj_sb[:, k, n * HALF:(n + 1) * HALF],
                                  start=(k == 0), stop=(k == 1))
            last.then_inc(*tell("pe", "ppj"))
            turn_rows(["h2T0", "h2T1", "h2T2", "h2T3", "h20", "h21"], [6, 7, 0, 1],
                      [done("dve", "ya3"), None, None, None])
            pe.wait_ge(router_in, 16)
            pe.wait_ge(rb_in, 16)
            pe.wait_ge(*done("act", "ppj1"))
            for t in range(NT):
                mm(bank[2][:, t * E:(t + 1) * E], ones[0:1, :], rb_row[:, :], start=True, stop=False)
                for k in range(KD):
                    if t == 0 and k % 2 == 0:
                        pe.wait_ge(*done("act" if k // 2 % 2 == 0 else "dve", f"h2T{k // 2}"))
                    last = mm(bank[2][:, t * E:(t + 1) * E], h2T[:, k, t * P:(t + 1) * P], router_sb[:, k, :],
                              start=False, stop=(k == KD - 1))
            last.then_inc(*tell("pe", "logits"))
            pe.wait_ge(*done("dve", "mask"))
            mm(bank[3][:, 0:E], tri[:, :], mask[:, 0, :], start=True, stop=True)
            mm(bank[3][:, E:2 * E], ones[:, :], mask[:, 0, :], start=True, stop=False)
            mm(bank[3][:, E:2 * E], tri[:, :], mask[:, 1, :], start=False, stop=True).then_inc(*tell("pe", "pos"))
            mm(bank[3][:, 2 * E:3 * E], ones[:, :], mask[:, 0, :], start=True, stop=False)
            mm(bank[3][:, 2 * E:3 * E], ones[:, :], mask[:, 1, :], start=False, stop=True).then_inc(*tell("pe", "count"))
            pe.wait_ge(*done("dve", "p1"))
            pe.wait_ge(*done("dve", "gt"))
            for t in range(NT):
                last = turn_(bank[3][0:E, t * P:(t + 1) * P], gate[:, t, 0:E], ident[:, :])
            last.then_inc(*tell("pe", "combT"))

            def gather():
                for t in range(NT):
                    for q in range(2):
                        last = mm(xg_ps[q * SLOT:(q + 1) * SLOT, :], sel[:, t, :], hn[:, t, q * HALF:(q + 1) * HALF],
                                  start=(t == 0), stop=(t == NT - 1), skip_group_check=True)
                return last

            def turn_block(dst, src):
                for c in range(4):
                    last = turn_(dst[:, c * P:(c + 1) * P], src[:, c * P:(c + 1) * P], ident[:, :])
                return last

            pe.wait_ge(*done("dve", "sel_first"))
            gather().then_inc(gathered, 1)
            pe.wait_ge(*done("act", "combT"))
            pe.wait_ge(b2_in, 16)
            for t in range(NT):
                for n in range(D // HALF):
                    last = mm(acc[2 * t + n][:, :], combT[:, t * P:(t + 1) * P], b2_rows[:, n * HALF:(n + 1) * HALF],
                              start=True, stop=False, skip_group_check=True)
            last.then_inc(*tell("pe", "comb_b2"))
            pe.wait_ge(xg_ready, 1)
            turn_block(xg_ps, xg_rows).then_inc(xg_turned, 1)
            pe.wait_ge(b1_in, 16)
            pe.wait_ge(*done("dve", "iters"))

            n_it = pe.value_load(iters[0:1, 0:1], min_val=E, max_val=MAXIT)
            with pe.Fori(0, n_it) as it:
                turn = pe.snap(it + 1)
                turn_next = pe.snap(it + 2)
                arrived = pe.snap(it * 16 + 16)
                pe.wait_ge(gsel_ready, turn)
                for t in range(NT):
                    last = turn_(y_ps[:, t * P:(t + 1) * P], gsel[:, t, :, :], ident[:, :])
                last.then_inc(gsel_turned, 1)
                w1_parts = [(ps, q, 2 * i + q) for i, ps in enumerate((lin_ps, up_ps)) for q in range(2)]
                pe.wait_ge(picked, turn)
                for ps, q, n in w1_parts:
                    mm(ps[q * SLOT:(q + 1) * SLOT, :], pick[:, :], b1_sb[:, n * HALF:(n + 1) * HALF],
                       start=True, stop=False, skip_group_check=True)
                pe.wait_ge(xgT_ready, turn)
                for k in range(KD):
                    pe.wait_ge(ring_in[k], arrived)
                    for ps, q, n in w1_parts:
                        last = mm(ps[q * SLOT:(q + 1) * SLOT, :], xgT[:, k % 4, k // 4, :], ring[:, k, n * HALF:(n + 1) * HALF],
                                  start=False, stop=(k == KD - 1), skip_group_check=True)
                    last.then_inc(ring_used[k], 1)
                pe.wait_ge(sel_ready, turn)
                gather().then_inc(gathered, 1)
                pe.wait_ge(gselT_ready, turn)
                pe.wait_ge(act_ready, turn)
                turn_block(y_ps, act_rows).then_inc(act_turned, 1)
                pe.wait_ge(xg_ready, turn_next)
                turn_block(xg_ps, xg_rows).then_inc(xg_turned, 1)
                pe.wait_ge(actT_ready, turn)
                for k in range(KF):
                    u = KD + k // 2
                    if k % 2 == 0:
                        pe.wait_ge(ring_in[u], arrived)
                    w2u = ring[:, u, :].rearrange("p (k n) -> p k n", k=2)
                    for q in range(2):
                        last = mm(y_ps[q * SLOT:(q + 1) * SLOT, :], actT[:, k % 4, k // 4, :], w2u[:, k % 2, q * HALF:(q + 1) * HALF],
                                  start=(k == 0), stop=(k == KF - 1), skip_group_check=True)
                    if k % 2:
                        last.then_inc(ring_used[u], 1)
                pe.wait_ge(y_ready, turn)
                for t in range(NT):
                    for q in range(2):
                        rows = slice(q * SLOT, (q + 1) * SLOT)
                        last = mm(acc[2 * t + q][:, :], gselT[rows, t * P:(t + 1) * P], y_sb[rows, :],
                                  start=False, stop=False, skip_group_check=True)
                last.then_inc(scattered, 1)

            turn_rows(["hpT0", "hpT1", "hpT2", "hpT3", "h30", "h31"], [0, 1, 2, 3], [None] * 4)
            pe.wait_ge(plew_in, 16)
            for t in range(NT):
                for n in range(D // HALF):
                    for k in range(KD):
                        if t == 0 and n == 0 and k % 2 == 0:
                            pe.wait_ge(*done("act" if k // 2 % 2 == 0 else "dve", f"hpT{k // 2}"))
                        last = mm(bank[4 + 2 * t + n][:, :], hT[:, k, t * P:(t + 1) * P], wide[:, k, n * HALF:(n + 1) * HALF],
                                  start=(k == 0), stop=(k == KD - 1))
                    last.then_inc(*tell("pe", f"pg{2 * t + n}"))


_INS = ["x", "p", "norm1_g", "w_in", "pool_w", "pool_scale", "w_branch_pool", "w_branch_attn", "w_out",
        "norm2_g", "router_w", "router_b", "exp_w1", "exp_b1", "exp_w2", "exp_b2",
        "ple_norm_g", "ple_gate_w", "ple_proj_w", "final_g"]


def kernel(**inputs):
    import numpy as _np
    import concourse.bacc as _bacc
    from concourse import mybir as _mybir
    from concourse.bass_utils import run_bass_kernel_spmd as _run

    nc = _bacc.Bacc("TRN2", target_bir_lowering=False, num_devices=1)
    arrays, args = {}, []
    for name in _INS:
        a = _np.ascontiguousarray(inputs[name])
        arrays[f"in_{name}"] = a
        args.append(nc.dram_tensor(f"in_{name}", a.shape, _mybir.dt.from_np(a.dtype), kind="ExternalInput").ap())
    shape = inputs["x"].shape
    out = nc.dram_tensor("out_x", shape, _mybir.dt.float32, kind="ExternalOutput").ap()
    hybrid_block(nc, *args, out)
    r = _run(nc, [arrays], core_ids=[0])
    return r.results[0]["out_x"]
```

```python
import concourse.bass as bass
from concourse import mybir
from contextlib import ExitStack


def hybrid_block(nc, x_d, p_d, norm1_g, w_in, pool_w, pool_scale, w_bp, w_ba, w_out,
                 norm2_g, router_w, router_b, exp_w1, exp_b1, exp_w2, exp_b2,
                 ple_norm_g, ple_gate_w, ple_proj_w, final_g, out_d):
    f32 = mybir.dt.float32
    i32 = mybir.dt.int32
    ALU = mybir.AluOpType
    ACT = mybir.ActivationFunctionType
    AX = mybir.AxisListType

    P = 128
    S, D = x_d.shape[1], x_d.shape[2]
    NT = S // P
    KD = D // P
    HALF = 512
    PW = pool_scale.shape[1]
    NG = PW // P
    WINDOWS = (2, 4, 8, 16)
    PAD = 16
    NH, DH = 8, 64
    NKV = 2
    GROUP = NH // NKV
    AW = NH * DH
    TOPK = S // 4
    E = router_w.shape[2]
    F = exp_w2.shape[2]
    KF = F // P
    NU = 2 * KF
    TOPE = 4
    SLOT = 64
    MAXIT = E * (S // SLOT)
    EPS = 1e-6
    FILL, TAKEN, BIG = -1e38, -3e38, 1e30
    WARM_UP = 24

    C_U, C_Q = 0, PW
    C_K = C_Q + AW
    C_V = C_K + NKV * DH
    C_QI = C_V + NKV * DH
    C_KI = C_QI + NH * DH
    C_WI = C_KI + DH
    C_G = C_WI + NH

    GW = 256
    GROUPS = [(C_KI, DH + NH), (C_QI, GW), (C_QI + GW, GW), (C_K, GW), (C_Q, GW), (C_Q + GW, GW),
              (C_U, GW), (C_U + GW, GW)] + [(C_G + GW * i, GW) for i in range(2 * D // GW)]
    GROUP_STEPS = ["wi", "qi0", "qi1", "v", "q0", "q1", "u0", "u1"] + [f"g{i}" for i in range(2 * D // GW)]
    NSTREAM = 4
    SLOTF = KD * GW
    AHEAD = NSTREAM + 1
    NRING = 12

    ctx = ExitStack()
    with ctx:
        def sb(name, shape, dt=f32):
            return ctx.enter_context(nc.sbuf_tensor(name, shape, dt))

        def sem(name):
            return ctx.enter_context(nc.semaphore(name))

        ring = sb("ring", [P, NRING, SLOTF])
        stream = sb("stream", [P, NSTREAM, SLOTF])
        work = sb("work", [P, 12864])
        x_sb = sb("x_sb", [P, NT, D])
        hn = sb("hn", [P, NT, D])
        gain = sb("gain", [P, D])
        ident = sb("ident", [P, P])
        tri = sb("tri", [P, P])
        ones = sb("ones", [P, P])
        slot_no = sb("slot_no", [P, 2, SLOT])
        pos = sb("pos", [P, NT, MAXIT + 1])
        gate = sb("gate", [P, NT, MAXIT + 1])
        rb_row = sb("rb_row", [1, E])
        scale_rows = sb("scale_rows", [NG, P])
        scale_col = sb("scale_col", [P, NG])
        ss = sb("ss", [P, NT])
        half_ss = sb("half_ss", [P, 2 * NT])
        gate_rstd = sb("gate_rstd", [P, NT])
        rstd = sb("rstd", [P, NT])
        eps = sb("eps", [P, 1])
        top8 = sb("top8", [P, NT, 8])
        wi_sb = sb("wi_sb", [P, NT, NH])
        smax = sb("smax", [P, NH])
        ssum = sb("ssum", [P, NH])
        first_inv = sb("first_inv", [P, NG, PAD])
        lpad = sb("lpad", [P, NT, E + 4])
        top4 = sb("top4", [P, NT, 8])
        mask = sb("mask", [P, NT, E])
        expl = sb("expl", [P, NT, E])
        small = sb("small", [P, 8])
        least = sb("least", [P, NT])
        gsum = sb("gsum", [P, NT])
        iters = sb("iters", [P, 1], i32)

        sgT = ring[:, 8:10, :].rearrange("p a (c s) -> p (a c) s", s=S)
        sm1 = ring[:, 10, :].rearrange("p (h s) -> p h s", h=NH)
        PT1 = ring[:, 11, :].rearrange("p (h k s) -> p h k s", h=NH, k=NT)

        def cut(a, n):
            return work[:, a:a + n]

        hT = cut(0, 2048).rearrange("p (k s) -> p k s", k=KD)
        qiT = cut(2048, 1024).rearrange("p (c s) -> p c s", s=S)
        qT = cut(3072, 1024).rearrange("p (c s) -> p c s", s=S)
        kiT = cut(4096, 256)
        kT = cut(4352, 512).rearrange("p (v s) -> p v s", v=NKV)
        v_sb = cut(4864, 256).rearrange("p (t c) -> p t c", t=NT)
        relu = cut(5120, 1024).rearrange("p (b c) -> p b c", b=2)
        sm0 = cut(5120, 1024).rearrange("p (h s) -> p h s", h=NH)
        score = [cut(6144, P), cut(6272, 2 * P)]
        uT = cut(6656, NG * (PAD + S)).rearrange("p (g s) -> p g s", g=NG)
        PT0 = cut(6656, 1024).rearrange("p (h s) -> p h s", h=NH)
        mixed = cut(7744, 1024).rearrange("p (g s) -> p g s", g=NG)
        s2 = cut(8768, NG * (PAD + S)).rearrange("p (g s) -> p g s", g=NG)
        s4 = cut(8768 + NG * (PAD + S), (NG - 1) * (PAD + S)).rearrange("p (g s) -> p g s", g=NG - 1)
        s8 = cut(10816, (NG - 2) * (PAD + S)).rearrange("p (g s) -> p g s", g=NG - 2)
        s16 = cut(10816 + 544, PAD + S).rearrange("p (g s) -> p g s", g=1)
        mT = cut(8768, 2048).rearrange("p (k s) -> p k s", k=KD)
        y1T = cut(10816, 1024).rearrange("p (g s) -> p g s", g=NG)
        oT = cut(11840, 1024).rearrange("p (c s) -> p c s", s=S)
        mix_tmp = PT1.rearrange("p h k s -> p (h k s)").rearrange("p (b s) -> p b s", b=4)
        poolw_sb = hn[:, 0, 0:NG * P].rearrange("p (g d) -> p g d", g=NG)
        bp_sb = stream[:, 0:2, :].rearrange("p a (c n) -> p (a c) n", n=D)
        ba_sb = stream[:, 2:4, :].rearrange("p a (c n) -> p (a c) n", n=D)
        wide = stream[:, :, :].rearrange("p a (c n) -> p (a c) n", n=D)

        ppj = cut(2048, 2048).rearrange("p (t n) -> p t n", t=NT)
        combT = work[0:E, 7424:7424 + S]
        b2_halves = [work[0:E, 6144:6144 + HALF], work[0:E, 12352:12352 + HALF]]
        p_sb = cut(6144, 512).rearrange("p (t n) -> p t n", t=NT)
        pT = cut(6656, 512).rearrange("p (k s) -> p k s", k=2)
        proj_sb = cut(0, 2048).rearrange("p (k n) -> p k n", k=2)
        router_sb = cut(7168, KD * E).rearrange("p (k e) -> p k e", e=E)
        h2T = hT

        b1_sb = cut(4096, 2 * F)
        xg_rows = cut(0, HALF)
        xgT = cut(512, KD * SLOT).rearrange("p (c q j) -> p c q j", q=2, j=SLOT)
        sel = cut(1024, NT * SLOT).rearrange("p (t j) -> p t j", t=NT)
        gsel = cut(1152, NT * 2 * SLOT).rearrange("p (t q j) -> p t q j", t=NT, q=2)
        gselT = cut(1408, S)
        pick = cut(1664, SLOT)
        y_sb = cut(7168, HALF)
        lin = cut(7744, HALF)
        up = cut(8256, HALF)
        sigm = cut(10816, HALF)
        actT = cut(11328, HALF).rearrange("p (c q j) -> p c q j", q=2, j=SLOT)
        act_rows = cut(11840, HALF)

        ahead_unit = [stream[:, i, :] for i in range(NSTREAM)] + [cut(8768, SLOTF)]

        final_gain = cut(6144, D)
        sgate = cut(4096, 2048).rearrange("p (b n) -> p b n", b=4)

        bank = [ctx.enter_context(nc.psum_tensor(f"bank{i}", [P, HALF], f32)) for i in range(8)]
        lin_ps, up_ps, xg_ps, y_ps = [bank[i][:, :] for i in range(4)]

        def pair(b):
            return bank[b][:, :].rearrange("p (c s) -> p c s", c=2)

        acc = bank[4:8]

        gain_in, pool_in, scale_in = sem("gain_in"), sem("pool_in"), sem("scale_in")
        x_in = [sem(f"x_in{t}") for t in range(NT)]
        stream_in = [sem(f"stream_in{i}") for i in range(NSTREAM)]
        ring_in = [sem(f"ring_in{i}") for i in range(NRING)]
        ring_used = [sem(f"ring_used{i}") for i in range(NRING)]
        b2_high_in = sem("b2_high_in")
        rb_in, router_in, b1_in, b2_in, p_in, proj_in = sem("rb_in"), sem("router_in"), sem("b1_in"), sem("b2_in"), sem("p_in"), sem("proj_in")
        gain2_in, gain3_in, final_in, plew_in = sem("gain2_in"), sem("gain3_in"), sem("final_in"), sem("plew_in")
        branch_in = [sem("branch_pool_in"), sem("branch_attn_in")]
        wout_in = [sem("wout_low_in"), sem("wout_high_in")]
        out_sem, ahead_in = sem("out_written"), sem("ahead_in")

        STEPS = {
            "pe": (
                "hT10 hT11 hT12 hT13 ki wi qi0 qi1 k v ix0e ix0o ix1a ix1b ix1c ix1d q0 q1 u0 u1 g0 g1 g2 g3 sc0e "
                "sc0o sc1a sc1b sc1c sc1d g4 g5 g6 g7 scaleT y1a y1b PT0a PT0b PT1a PT1b PT1c PT1d o0 o1 pT yp0 "
                "yp1 yp2 yp3 ya0 ya1 ya2 ya3 wout_low wout ppj0 ppj1 ppj2 ppj3 hT20 hT21 hT22 hT23 logits pos "
                "count combT b2 ahead moe0 moe1 hT30 hT31 pg0 hT32 hT33 pg1 pg2 pg3").split(),
            "act": (
                "root_a sq10 std10 sq11 std11 hT10 hT12 ki0 ki1 qi0 qi1 k0 k1 relu0 relu1 relu2 relu3 relu4 relu5 "
                "q0 q1 u0 u1 sg0 sg1 sg2 sg3 exp0 sg4 sg5 exp1 sg6 sg7 scale PT0a PT0b PT1a PT1b PT1c PT1d o0 o1 "
                "pT root_b sq20 std20 sq21 std21 hT20 hT22 ppj0 ppj1 rexp0 rexp1 ppj2 combT hT30 hT31 sq30 std30 "
                "hT32 hT33 sq31 std31 sgp0 sqf0 sgp1 sqf1 stdf0 sgp2 sqf2 sgp3 root_c sqf3 stdf1").split(),
            "dve": (
                "rstd10 h10 rstd11 h11 hT11 hT13 first_inv wi k2 k3 v ix0h0 ix0h1 ix0h2 ix0h3 ix0h4 ix0h5 ix0h6 "
                "ix0 ix1h0 ix1h1 ix1h2 ix1h3 ix1h4 ix1h5 ix1h6 ix1 tk0m0 tk1m0 tk0r0 tk1r0 tk0m1 tk1m1 tk0r1 "
                "tk1r1 tk0m2 tk1m2 tk0r2 tk1r2 tk0m3 tk1m3 tk0r3 tk1r3 tk0m4 tk1m4 tk0r4 tk1r4 tk0m5 tk1m5 tk0r5 "
                "tk1r5 tk0m6 tk1m6 tk0r6 tk1r6 tk0m7 tk1m7 tk0r7 tk1r7 neg0 neg1 msk0e msk0o max0 nmax0 msk1a "
                "msk1b msk1c msk1d rcp0 P0 max1 nmax1 rcp1 P1 y1a y1b yp0 yp1 yp2 yp3 ya0 ya1 ya2 ya3 x1a x1b x1c "
                "x1d rstd20 h20 rstd21 h21 hT21 hT23 l top0 top1 nm t4 mr0 mr1 mask em rs rr gt cmax p1 p2 "
                "sel_first pm1 gm1 pm2 gm2 pm3 gm3 over osum iters ppj3 x2a h30 x2b h31 x2c h32 x2d h33 rstd30 "
                "rstd31 pl0 x30 pl1 x31 sum0 rstdf0 out00 out01 pl2 x32 pl3 x33 sum1 rstdf1 out10 out11").split(),
            "pool": (
                "eps ident0 ident tri0 tri ones slot_no pad iota inv_min causal0 causal1 s2 s4 s8 s16 mx0 mx1 mx2 "
                "mx3 fix0 fix1 fix2 fix3 mixed causal_neg0 causal_neg1 m0 m1 m2 m3 b1_zero lpad endcol").split(),
        }
        STEP_SEM = {e: sem(f"{e}_step") for e in STEPS}
        AT = {e: {n: i + 1 for i, n in enumerate(names)} for e, names in STEPS.items()}
        told = {e: [] for e in STEPS}

        def tell(engine, name):
            told[engine].append(name)
            assert STEPS[engine][len(told[engine]) - 1] == name, (engine, name, len(told[engine]))
            return STEP_SEM[engine], 1

        def done(engine, name):
            return STEP_SEM[engine], AT[engine][name]

        xg_ready, act_ready = sem("xg_ready"), sem("act_ready")
        sel_ready, gsel_ready = sem("sel_ready"), sem("gsel_ready")
        picked, xg_turned, xgT_ready = sem("picked"), sem("xg_turned"), sem("xgT_ready")
        act_turned, actT_ready = sem("act_turned"), sem("actT_ready")
        gathered, gsel_turned, gselT_ready = sem("gathered"), sem("gsel_turned"), sem("gselT_ready")
        lin_ready, up_ready = sem("lin_ready"), sem("up_ready")
        sig_ready, prod_ready = sem("sig_ready"), sem("prod_ready")
        y_ready = sem("y_ready")

        block = ctx.enter_context(nc.Block())

        w1_v = exp_w1[0].rearrange("e (k p) n -> e p k n", p=P)
        w2_v = exp_w2[0].rearrange("e (u k p) n -> e u p k n", p=P, k=2)

        @block.sync
        def _(sp):
            def load_unit(e, u):
                if u < KD:
                    return sp.dma_start(ring[:, u, :], w1_v[e, :, u, :])
                return sp.dma_start(ring[:, u, :].rearrange("p (k n) -> p k n", k=2), w2_v[e, u - KD])

            for t in range(NT):
                sp.dma_start(x_sb[:, t, :], x_d[0, t * P:(t + 1) * P, :]).then_inc(x_in[t], 16)
            sp.dma_start(gain[:, :], norm1_g[0].partition_broadcast(P)).then_inc(gain_in, 16)

            def load_group(i):
                c0, n = GROUPS[i]
                s = i % NSTREAM
                dst = stream[:, s, 0:KD * n].rearrange("p (k n) -> p k n", n=n)
                if i >= NSTREAM:
                    sp.wait_ge(*done("pe", GROUP_STEPS[i - NSTREAM]))
                sp.dma_start(dst, w_in[0, :, c0:c0 + n].rearrange("(k p) n -> p k n", p=P)).then_inc(stream_in[s], 16)

            for i in range(NSTREAM):
                load_group(i)
            sp.dma_start(scale_rows[:, :], pool_scale[0].rearrange("(g p) -> g p", p=P)).then_inc(scale_in, 16)
            sp.dma_start(rb_row[:, :], router_b[0:1, :]).then_inc(rb_in, 16)
            for i in range(NSTREAM, len(GROUPS)):
                load_group(i)
                if i < NSTREAM + KD:
                    load_unit(0, i - NSTREAM).then_inc(ring_in[i - NSTREAM], 16)
                if i == NSTREAM:
                    sp.wait_ge(*done("dve", "h11"))
                    sp.wait_ge(*done("pe", "hT13"))
                    sp.dma_start(poolw_sb, pool_w[0].rearrange("g c d -> c g d")).then_inc(pool_in, 16)
            G = len(GROUPS)
            sp.wait_ge(*done("pe", GROUP_STEPS[G - 3]))
            sp.dma_start(bp_sb, w_bp[0].rearrange("(c p) n -> p c n", p=P)).then_inc(branch_in[0], 16)
            sp.wait_ge(*done("pe", GROUP_STEPS[G - 1]))
            sp.dma_start(ba_sb, w_ba[0].rearrange("(c p) n -> p c n", p=P)).then_inc(branch_in[1], 16)
            wo_v = w_out[0].rearrange("(k p) n -> p k n", p=P)
            sp.wait_ge(*done("pe", "yp3"))
            sp.dma_start(wide[:, 0:4, :], wo_v[:, 0:4, :]).then_inc(wout_in[0], 16)
            sp.wait_ge(*done("pe", "ya3"))
            sp.dma_start(wide[:, 4:8, :], wo_v[:, 4:8, :]).then_inc(wout_in[1], 16)
            sp.wait_ge(*done("pool", "m3"))
            for u in range(KD, NRING):
                load_unit(0, u).then_inc(ring_in[u], 16)
            for u in range(NSTREAM):
                sp.wait_ge(*done("pe", "wout_low" if u < NSTREAM // 2 else "wout"))
                sp.dma_start(ahead_unit[u], w1_v[1, :, u, :]).then_inc(stream_in[u], 16)
            sp.dma_start(ahead_unit[NSTREAM], w1_v[1, :, NSTREAM, :]).then_inc(ahead_in, 16)
            for e, units in ((2, range(AHEAD)), (1, range(AHEAD, NRING)), (2, range(AHEAD, NRING))):
                for u in units:
                    sp.wait_ge(ring_used[u], 1 if u < AHEAD else e)
                    load_unit(e, u).then_inc(ring_in[u], 16)
            sp.wait_ge(*done("dve", "iters"))
            n_it = sp.value_load(iters[0:1, 0:1], min_val=E, max_val=MAXIT)
            e_reg = sp.alloc_register("expert")
            with sp.Fori(3, n_it) as it:
                sp.reg_alu(e_reg, it, E - 1, ALU.bitwise_and)
                e = sp.snap(e_reg, min_val=0, max_val=E - 1)
                turn, turn_low = sp.snap(it), sp.snap(it - 1)
                for u in range(NRING):
                    sp.wait_ge(ring_used[u], turn_low if u < AHEAD else turn)
                    load_unit(e, u).then_inc(ring_in[u], 16)
            sp.wait_ge(*done("pe", "ahead"))
            sp.dma_start(wide, ple_gate_w[0].rearrange("(k p) n -> p k n", p=P)).then_inc(plew_in, 16)
            for t in range(NT):
                for n in range(2):
                    half = slice(n * HALF, (n + 1) * HALF)
                    sp.wait_ge(*done("dve", f"out{t}{n}"))
                    sp.dma_start(out_d[0, t * P:(t + 1) * P, half], hn[:, t, half]).then_inc(out_sem, 16)
            sp.wait_ge(out_sem, 16 * NT * 2)

        @block.gpsimd
        def _(pool):
            g = nc.gpsimd
            g.memset(eps[:, :], EPS).then_inc(*tell("pool", "eps"))
            g.memset(ident[:, :], 0.0).then_inc(*tell("pool", "ident0"))
            pool.wait_ge(*done("pool", "ident0"))
            g.affine_select(out=ident[:, :], in_=ident[:, :], compare_op=ALU.not_equal, fill=1.0, base=0,
                            pattern=[[-1, P]], channel_multiplier=1).then_inc(*tell("pool", "ident"))
            g.memset(tri[:, :], 1.0).then_inc(*tell("pool", "tri0"))
            pool.wait_ge(*done("pool", "tri0"))
            g.affine_select(out=tri[:, :], in_=tri[:, :], compare_op=ALU.is_gt, fill=0.0, base=0,
                            pattern=[[1, P]], channel_multiplier=-1).then_inc(*tell("pool", "tri"))
            g.memset(ones[:, :], 1.0).then_inc(*tell("pool", "ones"))
            g.iota(slot_no[:, :, :], [[0, 2], [1, SLOT]], base=0, channel_multiplier=0,
                   allow_small_or_imprecise_dtypes=True).then_inc(*tell("pool", "slot_no"))
            g.memset(uT[:, :, 0:PAD], 0.0).then_inc(*tell("pool", "pad"))
            g.iota(first_inv[:, :, :], [[0, NG], [1, PAD]], base=1, channel_multiplier=0,
                   allow_small_or_imprecise_dtypes=True).then_inc(*tell("pool", "iota"))
            pool.wait_ge(*done("pool", "iota"))
            for i, w in enumerate(WINDOWS):
                last = g.tensor_scalar(first_inv[:, i, :], first_inv[:, i, :], float(w), None, ALU.min)
            last.then_inc(*tell("pool", "inv_min"))
            for t in range(NT):
                pool.wait_ge(*done("dve", f"ix{t}"))
                g.affine_select(out=score[t], in_=score[t], compare_op=ALU.is_ge, fill=FILL, base=t * P,
                                pattern=[[-1, (t + 1) * P]], channel_multiplier=1).then_inc(*tell("pool", f"causal{t}"))
            W = PAD + S
            pool.wait_ge(*done("pool", "pad"))
            pool.wait_ge(*done("act", "u1"))
            g.tensor_tensor(s2[:, :, 1:W], uT[:, :, 1:W], uT[:, :, 0:W - 1], ALU.add).then_inc(*tell("pool", "s2"))
            pool.wait_ge(*done("pool", "s2"))
            g.tensor_tensor(s4[:, :, 3:W], s2[:, 1:, 3:W], s2[:, 1:, 1:W - 2], ALU.add).then_inc(*tell("pool", "s4"))
            pool.wait_ge(*done("pool", "s4"))
            g.tensor_tensor(s8[:, :, 7:W], s4[:, 1:, 7:W], s4[:, 1:, 3:W - 4], ALU.add).then_inc(*tell("pool", "s8"))
            pool.wait_ge(*done("pool", "s8"))
            g.tensor_tensor(s16[:, :, 15:W], s8[:, 1:, 15:W], s8[:, 1:, 7:W - 8], ALU.add).then_inc(*tell("pool", "s16"))
            pool.wait_ge(*done("pool", "s16"))
            sums = [s2[:, 0, :], s4[:, 0, :], s8[:, 0, :], s16[:, 0, :]]
            for i, w in enumerate(WINDOWS):
                g.tensor_scalar(mixed[:, i, :], sums[i][:, PAD:W], 1.0 / w, None, ALU.mult)\
                    .then_inc(*tell("pool", f"mx{i}"))
            pool.wait_ge(*done("pool", "mx3"))
            pool.wait_ge(*done("dve", "first_inv"))
            for i in range(NG):
                g.tensor_tensor(mixed[:, i, 0:PAD], sums[i][:, PAD:2 * PAD], first_inv[:, i, :], ALU.mult)\
                    .then_inc(*tell("pool", f"fix{i}"))
            pool.wait_ge(*done("pool", "fix3"))
            g.tensor_tensor(mixed[:, :, :], mixed[:, :, :], uT[:, :, PAD:W], ALU.subtract).then_inc(*tell("pool", "mixed"))
            for t in range(NT):
                pool.wait_ge(*done("dve", f"neg{t}"))
                g.affine_select(out=score[t], in_=score[t], compare_op=ALU.is_ge, fill=-1.0, base=t * P,
                                pattern=[[-1, (t + 1) * P]], channel_multiplier=1)\
                    .then_inc(*tell("pool", f"causal_neg{t}"))
            pool.wait_ge(*done("dve", "h11"))
            g.dma_start(gain[:, :], norm2_g[0].partition_broadcast(P)).then_inc(gain2_in, 16)
            pool.wait_ge(*done("dve", "msk1d"))
            g.dma_start(p_sb, p_d[0, 0].rearrange("(t p) n -> p t n", p=P)).then_inc(p_in, 16)
            pool.wait_ge(*done("pe", GROUP_STEPS[-1]))
            g.dma_start(proj_sb, ple_proj_w[0].rearrange("(k p) n -> p k n", p=P)).then_inc(proj_in, 16)
            for i in range(4):
                pool.wait_ge(*done("dve", f"ya{i}"))
                g.tensor_tensor(mT[:, 2 * i:2 * i + 2, :], mT[:, 2 * i:2 * i + 2, :],
                                mix_tmp[:, i, :].rearrange("p (c s) -> p c s", c=2), ALU.add)\
                    .then_inc(*tell("pool", f"m{i}"))
            g.memset(b1_sb, 0.0).then_inc(*tell("pool", "b1_zero"))
            pool.wait_ge(*done("pe", "pT"))
            g.dma_start(b2_halves[0], exp_b2[0, :, 0:HALF]).then_inc(b2_in, 16)
            g.dma_start(b2_halves[1], exp_b2[0, :, HALF:D]).then_inc(b2_high_in, 16)
            g.dma_start(router_sb[:, :, :], router_w[0].rearrange("(k p) e -> p k e", p=P)).then_inc(router_in, 16)
            pool.wait_ge(*done("pool", "b1_zero"))
            g.dma_start(work[0:E, 4096:4096 + 2 * F], exp_b1[0]).then_inc(b1_in, 16)
            g.memset(lpad[:, :, E:E + 4], FILL).then_inc(*tell("pool", "lpad"))
            g.memset(pos[:, :, MAXIT:MAXIT + 1], -1.0)
            g.memset(gate[:, :, MAXIT:MAXIT + 1], 0.0).then_inc(*tell("pool", "endcol"))
            pool.wait_ge(*done("dve", "h21"))
            g.dma_start(gain[:, :], ple_norm_g[0].partition_broadcast(P)).then_inc(gain3_in, 16)
            pool.wait_ge(*done("pe", "b2"))
            g.dma_start(final_gain, final_g.partition_broadcast(P)).then_inc(final_in, 16)

        @block.scalar
        def _(act):
            a = nc.scalar

            def norm_stats(n, source_ready):
                for t in range(NT):
                    act.wait_ge(*source_ready[t])
                    a.activation(hn[:, t, :], x_sb[:, t, :], ACT.Square, accum_out=ss[:, t:t + 1])\
                        .then_inc(*tell("act", f"sq{n}{t}"))
                    act.wait_ge(*done("act", f"sq{n}{t}"))
                    a.activation(rstd[:, t:t + 1], ss[:, t:t + 1], ACT.Sqrt, bias=eps[:, :], scale=1.0 / D)\
                        .then_inc(*tell("act", f"std{n}{t}"))

            def evacuate_turned(n, i, dst, b):
                evacuate(f"hT{n}{i}", dst[:, 4 * (i % 2):4 * (i % 2) + 4, (i // 2) * P:(i // 2 + 1) * P],
                         bank[b][:, :].rearrange("p (k s) -> p k s", s=P)).then_inc(*tell("act", f"hT{n}{i}"))

            def evacuate(name, dst, src, func=ACT.Copy, **kw):
                act.wait_ge(*done("pe", name))
                return a.activation(dst, src, func, **kw)

            act.wait_ge(*done("pool", "eps"))
            a.activation(small[:, 0:1], eps[:, :], ACT.Sqrt).then_inc(*tell("act", "root_a"))
            norm_stats(1, [(x_in[0], 16), (x_in[1], 16)])
            for i in (0, 2):
                evacuate_turned(1, i, hT, i)
            evacuate("ki", kiT[0:DH, :], bank[4][0:DH, 0:S]).then_inc(*tell("act", "ki0"))
            evacuate("ki", kiT[DH:P, :], bank[4][0:DH, 0:S]).then_inc(*tell("act", "ki1"))
            evacuate("qi0", qiT[:, 0:2, :], pair(6)).then_inc(*tell("act", "qi0"))
            evacuate("qi1", qiT[:, 2:4, :], pair(7)).then_inc(*tell("act", "qi1"))
            evacuate("k", kT[0:DH, 0, :], bank[0][0:DH, 0:S]).then_inc(*tell("act", "k0"))
            evacuate("k", kT[DH:P, 0, :], bank[0][0:DH, 0:S]).then_inc(*tell("act", "k1"))
            for i, (name, b) in enumerate([("ix0e", 2), ("ix0o", 3), ("ix1a", 4), ("ix1b", 5), ("ix1c", 6), ("ix1d", 7)]):
                if i >= 2:
                    act.wait_ge(*done("dve", ["ix0h3", "ix0", "ix1h1", "ix1h3"][i - 2]))
                evacuate(name, relu[:, i % 2, :], bank[b][:, :], ACT.Relu, scale=DH ** -0.5)\
                    .then_inc(*tell("act", f"relu{i}"))
            for i in range(2):
                evacuate(f"q{i}", qT[:, 2 * i:2 * i + 2, :], pair(i)).then_inc(*tell("act", f"q{i}"))
            for i in range(2):
                evacuate(f"u{i}", uT[:, 2 * i:2 * i + 2, PAD:PAD + S],
                         pair(2 + i)).then_inc(*tell("act", f"u{i}"))

            def gates(i):
                b = 4 + i if i < 4 else 6 + i % 2
                evacuate(f"g{i}", sgT[:, 2 * i:2 * i + 2, :], pair(b),
                         ACT.Sigmoid).then_inc(*tell("act", f"sg{i}"))

            def exps(t, sm):
                act.wait_ge(*done("dve", f"nmax{t}"))
                for h in range(NH):
                    last = a.activation(sm[:, h, :], sm[:, h, :], ACT.Exp, bias=smax[:, h:h + 1],
                                        scale=DH ** -0.5, accum_out=ssum[:, h:h + 1])
                last.then_inc(*tell("act", f"exp{t}"))

            for i in range(4):
                gates(i)
            exps(0, sm0)
            gates(4)
            gates(5)
            exps(1, sm1)
            gates(6)
            gates(7)
            evacuate("scaleT", scale_col[:, :], bank[1][:, 0:NG]).then_inc(*tell("act", "scale"))
            for i, n in enumerate("ab"):
                evacuate(f"PT0{n}", PT0[:, 4 * i:4 * i + 4, :], bank[i][:, :].rearrange("p (h s) -> p h s", s=P)).then_inc(*tell("act", f"PT0{n}"))
            for i, n in enumerate("abcd"):
                evacuate(f"PT1{n}", PT1[:, 2 * i:2 * i + 2, :, :].rearrange("p h k s -> p (h k s)"), bank[2 + i][:, :])\
                    .then_inc(*tell("act", f"PT1{n}"))
            for t in range(NT):
                evacuate(f"o{t}", oT[:, :, t * P:(t + 1) * P], bank[6 + t][:, :].rearrange("p (c s) -> p c s", s=P))\
                    .then_inc(*tell("act", f"o{t}"))
            evacuate("pT", pT[:, :, :], pair(0)).then_inc(*tell("act", "pT"))
            a.activation(small[:, 0:1], eps[:, :], ACT.Sqrt).then_inc(*tell("act", "root_b"))
            norm_stats(2, [done("dve", "x1b"), done("dve", "x1d")])
            for i in (0, 2):
                evacuate_turned(2, i, h2T, 2 + i)
            for i in range(2):
                evacuate(f"ppj{i}", ppj[:, 0, i * HALF:(i + 1) * HALF], bank[6 + i][:, :]).then_inc(*tell("act", f"ppj{i}"))
            for t in range(NT):
                act.wait_ge(*done("dve", "nm"))
                a.activation(expl[:, t, :], lpad[:, t, 0:E], ACT.Exp, bias=least[:, t:t + 1]).then_inc(*tell("act", f"rexp{t}"))
            evacuate("ppj2", ppj[:, 1, 0:HALF], bank[0][:, :]).then_inc(*tell("act", "ppj2"))
            evacuate("combT", combT, bank[3][0:E, 0:S]).then_inc(*tell("act", "combT"))
            act.wait_ge(gathered, 1)
            a.activation(xg_rows, xg_ps, ACT.Copy).then_inc(xg_ready, 1)
            act.wait_ge(xg_turned, 1)
            a.activation(xgT, xg_ps.rearrange("p (c q j) -> p c q j", q=2, j=SLOT), ACT.Copy).then_inc(xgT_ready, 1)


            def expert(turn, turn_next):
                act.wait_ge(lin_ready, turn)
                a.activation(sigm, lin, ACT.Sigmoid, scale=1.702).then_inc(sig_ready, 1)
                act.wait_ge(gathered, turn_next)
                a.activation(xg_rows, xg_ps, ACT.Copy).then_inc(xg_ready, 1)
                act.wait_ge(act_turned, turn)
                a.activation(actT, y_ps.rearrange("p (c q j) -> p c q j", q=2, j=SLOT), ACT.Copy).then_inc(actT_ready, 1)
                act.wait_ge(xg_turned, turn_next)
                a.activation(xgT, xg_ps.rearrange("p (c q j) -> p c q j", q=2, j=SLOT), ACT.Copy).then_inc(xgT_ready, 1)

            expert(1, 2)
            expert(2, 3)
            act.wait_ge(*done("dve", "iters"))
            n_it = act.value_load(iters[0:1, 0:1], min_val=E, max_val=MAXIT)
            with act.Fori(2, n_it) as it:
                expert(act.snap(it + 1), act.snap(it + 2))

            for t in range(NT):
                for b in range(2):
                    evacuate_turned(3, 2 * t + b, hT, 2 * t + b)
                act.wait_ge(*done("dve", f"x2{'bd'[t]}"))
                a.activation(sgate[:, 2 * t:2 * t + 2, :], x_sb[:, t, :].rearrange("p (b n) -> p b n", b=2), ACT.Square,
                             accum_out=ss[:, t:t + 1]).then_inc(*tell("act", f"sq3{t}"))
                act.wait_ge(*done("act", f"sq3{t}"))
                a.activation(rstd[:, t:t + 1], ss[:, t:t + 1], ACT.Sqrt, bias=eps[:, :], scale=1.0 / D)\
                    .then_inc(*tell("act", f"std3{t}"))
            for i in range(4):
                if i == 0:
                    act.wait_ge(*done("dve", "rstd31"))
                evacuate(f"pg{i}", sgate[:, i, :], bank[4 + i][:, :], ACT.Sigmoid, scale=gate_rstd[:, i // 2:i // 2 + 1])\
                    .then_inc(*tell("act", f"sgp{i}"))
                if i == 3:
                    a.activation(small[:, 0:1], eps[:, :], ACT.Sqrt).then_inc(*tell("act", "root_c"))
                act.wait_ge(*done("pe", "hT33"))
                act.wait_ge(*done("dve", f"x3{i}"))
                half = slice((i % 2) * HALF, (i % 2 + 1) * HALF)
                a.activation(hn[:, i // 2, half], x_sb[:, i // 2, half], ACT.Square, accum_out=half_ss[:, i:i + 1])\
                    .then_inc(*tell("act", f"sqf{i}"))
                if i % 2:
                    t = i // 2
                    act.wait_ge(*done("dve", f"sum{t}"))
                    a.activation(rstd[:, t:t + 1], ss[:, t:t + 1], ACT.Sqrt, bias=eps[:, :], scale=1.0 / D)\
                        .then_inc(*tell("act", f"stdf{t}"))

        @block.vector
        def _(dve):
            v = nc.vector

            def rms(n, gain_sem, gain_ap):
                dve.wait_ge(gain_sem, 16)
                for t in range(NT):
                    dve.wait_ge(*done("act", f"std{n}{t}"))
                    v.reciprocal(rstd[:, t:t + 1], rstd[:, t:t + 1]).then_inc(*tell("dve", f"rstd{n}{t}"))
                    dve.wait_ge(*done("dve", f"rstd{n}{t}"))
                    v.scalar_tensor_tensor(hn[:, t, :], x_sb[:, t, :], rstd[:, t:t + 1], gain_ap, ALU.mult, ALU.mult)\
                        .then_inc(*tell("dve", f"h{n}{t}"))

            def evacuate_turned(n, i, dst, b):
                dve.wait_ge(*done("pe", f"hT{n}{i}"))
                v.tensor_copy(dst[:, 4 * (i % 2):4 * (i % 2) + 4, (i // 2) * P:(i // 2 + 1) * P],
                              bank[b][:, :].rearrange("p (k s) -> p k s", s=P)).then_inc(*tell("dve", f"hT{n}{i}"))

            rms(1, gain_in, gain[:, :])
            for i in (1, 3):
                evacuate_turned(1, i, hT, i)
            dve.wait_ge(*done("pool", "inv_min"))
            v.reciprocal(first_inv[:, :, :], first_inv[:, :, :]).then_inc(*tell("dve", "first_inv"))
            dve.wait_ge(*done("pe", "wi"))
            v.tensor_scalar(wi_sb[:, :, :], bank[5][:, 0:NT * NH].rearrange("p (t h) -> p t h", t=NT),
                            NH ** -0.5, None, ALU.mult).then_inc(*tell("dve", "wi"))
            dve.wait_ge(*done("pe", "k"))
            v.tensor_copy(kT[0:DH, 1, :], bank[0][DH:P, 0:S]).then_inc(*tell("dve", "k2"))
            v.tensor_copy(kT[DH:P, 1, :], bank[0][DH:P, 0:S]).then_inc(*tell("dve", "k3"))
            dve.wait_ge(*done("pe", "v"))
            v.tensor_copy(v_sb[:, :, :], bank[1][:, 0:NT * P].rearrange("p (t c) -> p t c", t=NT))\
                .then_inc(*tell("dve", "v"))
            dve.wait_ge(*done("dve", "wi"))
            for t in range(NT):
                n = (t + 1) * P
                per = HALF // n
                order = [0, 2, 4, 6, 1, 3, 5, 7] if t == 0 else [0, 2, 1, 3, 4, 6, 5, 7]
                for i, h in enumerate(order):
                    b = (0 if t == 0 else 2) + i // per
                    dve.wait_ge(*done("act", f"relu{b}"))
                    r = relu[:, b % 2, (i % per) * n:(i % per + 1) * n]
                    name = f"ix{t}" if i == NH - 1 else f"ix{t}h{i}"
                    if i == 0:
                        v.tensor_scalar(score[t], r, wi_sb[:, t, h:h + 1], None, ALU.mult).then_inc(*tell("dve", name))
                    else:
                        dve.wait_ge(*done("dve", f"ix{t}h{i - 1}"))
                        v.scalar_tensor_tensor(score[t], r, wi_sb[:, t, h:h + 1], score[t], ALU.mult, ALU.add)\
                            .then_inc(*tell("dve", name))
            for r in range(TOPK // 8):
                for t in range(NT):
                    dve.wait_ge(*(done("dve", f"tk{t}r{r - 1}") if r else done("pool", f"causal{t}")))
                    v.max(top8[:, t, :], score[t]).then_inc(*tell("dve", f"tk{t}m{r}"))
                for t in range(NT):
                    dve.wait_ge(*done("dve", f"tk{t}m{r}"))
                    v.match_replace(score[t], top8[:, t, :], score[t], TAKEN).then_inc(*tell("dve", f"tk{t}r{r}"))
            for t in range(NT):
                dve.wait_ge(*done("dve", f"tk{t}r{TOPK // 8 - 1}"))
                v.tensor_scalar(score[t], score[t], TAKEN, 1.0, ALU.is_equal, ALU.subtract).then_inc(*tell("dve", f"neg{t}"))

            def masked(t, name, pe_name, b, heads, sm):
                n = (t + 1) * P
                dve.wait_ge(*done("pe", pe_name))
                v.scalar_tensor_tensor(sm[:, heads, :], score[t].rearrange("p (o s) -> p o s", o=1).broadcast_to([P, HALF // n, n]),
                                       BIG, bank[b][:, :].rearrange("p (h s) -> p h s", s=n), ALU.mult, ALU.add)\
                    .then_inc(*tell("dve", name))

            def row_max(t, sm, last):
                dve.wait_ge(*done("dve", last))
                if t:
                    dve.wait_ge(*done("act", "exp0"))
                v.tensor_reduce(smax[:, :], sm, AX.X, ALU.max).then_inc(*tell("dve", f"max{t}"))
                dve.wait_ge(*done("dve", f"max{t}"))
                v.tensor_scalar(smax[:, :], smax[:, :], -(DH ** -0.5), None, ALU.mult).then_inc(*tell("dve", f"nmax{t}"))

            def normalise(t, sm):
                n = (t + 1) * P
                dve.wait_ge(*done("act", f"exp{t}"))
                v.reciprocal(ssum[:, :], ssum[:, :]).then_inc(*tell("dve", f"rcp{t}"))
                dve.wait_ge(*done("dve", f"rcp{t}"))
                v.tensor_tensor(sm, sm, ssum[:, :].rearrange("p (h o) -> p h o", o=1).broadcast_to([P, NH, n]), ALU.mult)\
                    .then_inc(*tell("dve", f"P{t}"))

            dve.wait_ge(*done("pool", "causal_neg0"))
            masked(0, "msk0e", "sc0e", 0, slice(0, NH, 2), sm0)
            masked(0, "msk0o", "sc0o", 1, slice(1, NH, 2), sm0)
            row_max(0, sm0, "msk0o")
            dve.wait_ge(*done("pool", "causal_neg1"))
            masked(1, "msk1a", "sc1a", 2, slice(0, 4, 2), sm1)
            masked(1, "msk1b", "sc1b", 3, slice(1, 4, 2), sm1)
            masked(1, "msk1c", "sc1c", 4, slice(4, NH, 2), sm1)
            masked(1, "msk1d", "sc1d", 5, slice(5, NH, 2), sm1)
            normalise(0, sm0)
            row_max(1, sm1, "msk1d")
            normalise(1, sm1)
            for i, n in enumerate("ab"):
                dve.wait_ge(*done("pe", f"y1{n}"))
                dve.wait_ge(*done("act", "scale"))
                v.tensor_tensor(y1T[:, 2 * i:2 * i + 2, :], pair(i),
                                scale_col[:, 2 * i:2 * i + 2].rearrange("p (c o) -> p c o", o=1).broadcast_to([P, 2, S]),
                                ALU.mult).then_inc(*tell("dve", f"y1{n}"))
            for i in range(4):
                dve.wait_ge(*done("pe", f"yp{i}"))
                v.tensor_tensor(mT[:, 2 * i:2 * i + 2, :], pair(2 + i),
                                sgT[:, 2 * i:2 * i + 2, :], ALU.mult).then_inc(*tell("dve", f"yp{i}"))
            dve.wait_ge(*done("pe", "o1"))
            for i in range(4):
                dve.wait_ge(*done("pe", f"ya{i}"))
                v.tensor_tensor(mix_tmp[:, i, :].rearrange("p (c s) -> p c s", c=2),
                                pair([6, 7, 0, 1][i]),
                                sgT[:, KD + 2 * i:KD + 2 * i + 2, :], ALU.mult).then_inc(*tell("dve", f"ya{i}"))

            def residual(names, banks):
                for i, b in enumerate(banks):
                    xs = x_sb[:, i // 2, (i % 2) * HALF:(i % 2 + 1) * HALF]
                    v.tensor_tensor(xs, xs, bank[b][:, :], ALU.add).then_inc(*tell("dve", names[i]))

            dve.wait_ge(*done("pe", "wout"))
            residual(["x1a", "x1b", "x1c", "x1d"], [2, 3, 4, 5])
            rms(2, gain2_in, gain[:, :])
            for i in (1, 3):
                evacuate_turned(2, i, h2T, 2 + i)

            dve.wait_ge(*done("pe", "logits"))
            dve.wait_ge(*done("pool", "endcol"))
            v.tensor_copy(lpad[:, :, 0:E], bank[2][:, 0:NT * E].rearrange("p (t e) -> p t e", t=NT)).then_inc(*tell("dve", "l"))
            dve.wait_ge(*done("dve", "l"))
            for t in range(NT):
                v.max(top4[:, t, :], lpad[:, t, :]).then_inc(*tell("dve", f"top{t}"))
            dve.wait_ge(*done("dve", "top1"))
            v.tensor_scalar(least[:, :], top4[:, :, 0], -1.0, None, ALU.mult).then_inc(*tell("dve", "nm"))
            v.memset(top4[:, :, TOPE:8], FILL).then_inc(*tell("dve", "t4"))
            dve.wait_ge(*done("dve", "t4"))
            dve.wait_ge(*done("act", "rexp1"))
            for t in range(NT):
                v.match_replace(lpad[:, t, :], top4[:, t, :], lpad[:, t, :], TAKEN).then_inc(*tell("dve", f"mr{t}"))
            dve.wait_ge(*done("dve", "mr1"))
            v.tensor_scalar(mask[:, :, :], lpad[:, :, 0:E], TAKEN, None, ALU.is_equal).then_inc(*tell("dve", "mask"))
            dve.wait_ge(*done("dve", "mask"))
            v.tensor_tensor(expl[:, :, :], expl[:, :, :], mask[:, :, :], ALU.mult).then_inc(*tell("dve", "em"))
            dve.wait_ge(*done("dve", "em"))
            v.tensor_reduce(gsum[:, :], expl[:, :, :], AX.X, ALU.add).then_inc(*tell("dve", "rs"))
            dve.wait_ge(*done("dve", "rs"))
            v.reciprocal(gsum[:, :], gsum[:, :]).then_inc(*tell("dve", "rr"))
            dve.wait_ge(*done("dve", "rr"))
            v.tensor_tensor(gate[:, :, 0:E], expl[:, :, :], gsum[:, :].rearrange("p (t o) -> p t o", o=1).broadcast_to([P, NT, E]),
                            ALU.mult).then_inc(*tell("dve", "gt"))
            dve.wait_ge(*done("pe", "count"))
            v.tensor_reduce(small[:, 3:4], bank[3][:, NT * E:(NT + 1) * E], AX.X, ALU.max).then_inc(*tell("dve", "cmax"))
            v.scalar_tensor_tensor(pos[:, :, 0:E], bank[3][:, 0:NT * E].rearrange("p (t e) -> p t e", t=NT), 1.0,
                                   mask[:, :, :], ALU.add, ALU.mult).then_inc(*tell("dve", "p1"))
            dve.wait_ge(*done("dve", "p1"))
            v.tensor_scalar(pos[:, :, 0:E], pos[:, :, 0:E], 1.0, None, ALU.subtract).then_inc(*tell("dve", "p2"))
            dve.wait_ge(*done("dve", "p2"))
            v.tensor_scalar(sel[:, 0, :], slot_no[:, 0, :], pos[:, 0, 0:1], None, ALU.is_equal)
            v.tensor_scalar(sel[:, 1, :], slot_no[:, 0, :], pos[:, 1, 0:1], None, ALU.is_equal).then_inc(*tell("dve", "sel_first"))
            v.tensor_copy(pick[:, :], ident[:, 0:1].broadcast_to([P, SLOT])).then_inc(picked, 1)

            for i in range(1, S // SLOT):
                v.tensor_scalar(pos[:, :, i * E:(i + 1) * E], pos[:, :, 0:E], float(SLOT * i), None, ALU.subtract)\
                    .then_inc(*tell("dve", f"pm{i}"))
                if i == 1:
                    dve.wait_ge(*done("dve", "gt"))
                v.tensor_copy(gate[:, :, i * E:(i + 1) * E], gate[:, :, 0:E]).then_inc(*tell("dve", f"gm{i}"))

            dve.wait_ge(*done("dve", "cmax"))
            for i in range(S // SLOT - 1):
                last = v.tensor_scalar(small[:, 4 + i:5 + i], small[:, 3:4], float(SLOT * (i + 1)), float(E), ALU.is_gt, ALU.mult)
            last.then_inc(*tell("dve", "over"))
            dve.wait_ge(*done("dve", "over"))
            v.tensor_reduce(small[:, 1:2], small[:, 4:4 + S // SLOT - 1], AX.X, ALU.add).then_inc(*tell("dve", "osum"))
            dve.wait_ge(*done("dve", "osum"))
            v.tensor_scalar(iters[:, :], small[:, 1:2], float(E), None, ALU.add).then_inc(*tell("dve", "iters"))
            dve.wait_ge(*done("pe", "ppj3"))
            v.tensor_copy(ppj[:, 1, HALF:D], bank[1][:, :]).then_inc(*tell("dve", "ppj3"))

            def expert(turn, last_turn, it, e_next):
                if last_turn is not None:
                    dve.wait_ge(gsel_turned, last_turn)
                    v.tensor_copy(gselT, xg_ps[:, 0:S]).then_inc(gselT_ready, 1)
                for t in range(NT):
                    last = v.tensor_scalar(gsel[:, t, :, :], slot_no[:, :, :], pos[:, t, bass.ds(it, 1)],
                                           gate[:, t, bass.ds(it, 1)], ALU.is_equal, ALU.mult)
                last.then_inc(gsel_ready, 1)
                dve.wait_ge(gathered, turn)
                for t in range(NT):
                    last = v.tensor_scalar(sel[:, t, :], slot_no[:, 0, :], pos[:, t, bass.ds(turn, 1)], None, ALU.is_equal)
                last.then_inc(sel_ready, 1)
                dve.wait_ge(ring_used[AHEAD], turn)
                v.tensor_copy(pick[:, :], ident[:, bass.ds(e_next, 1)].broadcast_to([P, SLOT])).then_inc(picked, 1)
                dve.wait_ge(ring_used[KD - 1], turn)
                v.tensor_scalar(lin, lin_ps, 7.0, None, ALU.min).then_inc(lin_ready, 1)
                v.tensor_scalar(up, up_ps, 7.0, -7.0, ALU.min, ALU.max).then_inc(up_ready, 1)
                dve.wait_ge(up_ready, turn)
                dve.wait_ge(lin_ready, turn)
                v.scalar_tensor_tensor(up, up, 1.0, lin, ALU.add, ALU.mult).then_inc(prod_ready, 1)
                dve.wait_ge(prod_ready, turn)
                dve.wait_ge(sig_ready, turn)
                v.tensor_tensor(act_rows, up, sigm, ALU.mult).then_inc(act_ready, 1)
                dve.wait_ge(ring_used[NRING - 1], turn)
                v.tensor_copy(y_sb, y_ps).then_inc(y_ready, 1)

            expert(1, None, 0, 1)
            dve.wait_ge(*done("dve", "iters"))
            n_it = dve.value_load(iters[0:1, 0:1], min_val=E, max_val=MAXIT)
            with dve.Fori(1, n_it) as it:
                turn = dve.snap(it + 1)
                expert(turn, it, it, turn & (E - 1))
            dve.wait_ge(gsel_turned, n_it)
            v.tensor_copy(gselT, xg_ps[:, 0:S]).then_inc(gselT_ready, 1)

            dve.wait_ge(gain3_in, 16)
            for i in range(4):
                t, half = i // 2, slice((i % 2) * HALF, (i % 2 + 1) * HALF)
                dve.wait_ge(*done("pe", f"moe{t}"))
                v.tensor_tensor(x_sb[:, t, half], x_sb[:, t, half], acc[i][:, :], ALU.add).then_inc(*tell("dve", f"x2{'abcd'[i]}"))
                dve.wait_ge(*done("dve", f"x2{'abcd'[i]}"))
                v.tensor_tensor(hn[:, t, half], x_sb[:, t, half], gain[:, half], ALU.mult).then_inc(*tell("dve", f"h3{i}"))
            for t in range(NT):
                dve.wait_ge(*done("act", f"std3{t}"))
                v.reciprocal(gate_rstd[:, t:t + 1], rstd[:, t:t + 1]).then_inc(*tell("dve", f"rstd3{t}"))
            dve.wait_ge(final_in, 16)
            for i in range(4):
                t, half = i // 2, slice((i % 2) * HALF, (i % 2 + 1) * HALF)
                dve.wait_ge(*done("act", f"sgp{i}"))
                v.tensor_tensor(sgate[:, i, :], sgate[:, i, :], ppj[:, t, half], ALU.mult).then_inc(*tell("dve", f"pl{i}"))
                dve.wait_ge(*done("dve", f"pl{i}"))
                v.tensor_tensor(x_sb[:, t, half], x_sb[:, t, half], sgate[:, i, :], ALU.add).then_inc(*tell("dve", f"x3{i}"))
                if i % 2:
                    dve.wait_ge(*done("act", f"sqf{i}"))
                    v.tensor_tensor(ss[:, t:t + 1], half_ss[:, i - 1:i], half_ss[:, i:i + 1], ALU.add)\
                        .then_inc(*tell("dve", f"sum{t}"))
                    dve.wait_ge(*done("act", f"stdf{t}"))
                    v.reciprocal(rstd[:, t:t + 1], rstd[:, t:t + 1]).then_inc(*tell("dve", f"rstdf{t}"))
                    dve.wait_ge(*done("dve", f"rstdf{t}"))
                    for n in range(2):
                        half = slice(n * HALF, (n + 1) * HALF)
                        v.scalar_tensor_tensor(hn[:, t, half], x_sb[:, t, half], rstd[:, t:t + 1], final_gain[:, half],
                                               ALU.mult, ALU.mult).then_inc(*tell("dve", f"out{t}{n}"))

        @block.tensor
        def _(pe):
            mm = nc.tensor.matmul
            turn_ = nc.tensor.transpose

            pe.wait_ge(*done("pool", "ident"))

            pe.wait_ge(*done("pool", "ones"))
            for i in range(WARM_UP):
                last = mm(bank[7][:, 0:P], ones[:, :], tri[:, :], start=True, stop=True)

            def turn_tile(n, t, banks):
                pe.wait_ge(*done("dve", f"h{n}{t}"))
                for b in range(2):
                    for i in range(4):
                        k = 4 * b + i
                        last = turn_(bank[banks[b]][:, i * P:(i + 1) * P], hn[:, t, k * P:(k + 1) * P], ident[:, :])
                    last.then_inc(*tell("pe", f"hT{n}{2 * t + b}"))

            def turned(n, k, tiles=range(NT)):
                if k % 4 == 0:
                    for t in tiles:
                        pe.wait_ge(*done("act" if k == 0 else "dve", f"hT{n}{2 * t + k // 4}"))

            turn_tile(1, 0, [0, 1])
            turn_tile(1, 1, [2, 3])

            def group(i):
                c0, n = GROUPS[i]
                pe.wait_ge(stream_in[i % NSTREAM], 16 * (i // NSTREAM + 1))
                return stream[:, i % NSTREAM, 0:KD * n].rearrange("p (k n) -> p k n", n=n)

            def project_T(i, b, name):
                w = group(i)
                for c in range(GW // P):
                    for k in range(KD):
                        last = mm(bank[b][:, c * S:(c + 1) * S], w[:, k, c * P:(c + 1) * P], hT[:, k, :],
                                  start=(k == 0), stop=(k == KD - 1))
                last.then_inc(*tell("pe", name))

            w = group(0)
            for k in range(KD):
                turned(1, k)
                last = mm(bank[4][0:DH, 0:S], w[:, k, 0:DH], hT[:, k, :], start=(k == 0), stop=(k == KD - 1))
            last.then_inc(*tell("pe", "ki"))
            for t in range(NT):
                for k in range(KD):
                    last = mm(bank[5][:, t * NH:(t + 1) * NH], hT[:, k, t * P:(t + 1) * P], w[:, k, DH:DH + NH],
                              start=(k == 0), stop=(k == KD - 1))
            last.then_inc(*tell("pe", "wi"))
            project_T(1, 6, "qi0")
            project_T(2, 7, "qi1")
            w = group(3)
            for k in range(KD):
                last = mm(bank[0][:, 0:S], w[:, k, 0:P], hT[:, k, :], start=(k == 0), stop=(k == KD - 1))
            last.then_inc(*tell("pe", "k"))
            for t in range(NT):
                for k in range(KD):
                    last = mm(bank[1][:, t * P:(t + 1) * P], hT[:, k, t * P:(t + 1) * P], w[:, k, P:2 * P],
                              start=(k == 0), stop=(k == KD - 1))
            last.then_inc(*tell("pe", "v"))

            def head_products(t, qs, keys, heads, b, name):
                n = (t + 1) * P
                for i, h in enumerate(heads):
                    half = slice(DH * (h % 2), DH * (h % 2) + DH)
                    last = mm(bank[b][:, i * n:(i + 1) * n], qs[half, h // 2, t * P:(t + 1) * P], keys(h)[half, 0:n],
                              start=True, stop=True)
                last.then_inc(*tell("pe", name))

            pe.wait_ge(*done("act", "qi1"))
            pe.wait_ge(*done("dve", "wi"))
            index_keys = lambda h: kiT
            head_products(0, qiT, index_keys, [0, 2, 4, 6], 2, "ix0e")
            head_products(0, qiT, index_keys, [1, 3, 5, 7], 3, "ix0o")
            head_products(1, qiT, index_keys, [0, 2], 4, "ix1a")
            head_products(1, qiT, index_keys, [1, 3], 5, "ix1b")
            head_products(1, qiT, index_keys, [4, 6], 6, "ix1c")
            head_products(1, qiT, index_keys, [5, 7], 7, "ix1d")
            for i, (b, name, free) in enumerate([(0, "q0", ("dve", "k3")), (1, "q1", ("dve", "v")),
                                                 (2, "u0", ("act", "relu0")), (3, "u1", ("act", "relu1"))]):
                if i == 0:
                    pe.wait_ge(*done("act", "k1"))
                pe.wait_ge(*done(*free))
                project_T(4 + i, b, name)
            for i in range(4):
                pe.wait_ge(*done("act", f"relu{2 + i}"))
                project_T(8 + i, 4 + i, f"g{i}")
            head_keys = lambda h: kT[:, h // GROUP, :]
            pe.wait_ge(*done("act", "q1"))
            head_products(0, qT, head_keys, [0, 2, 4, 6], 0, "sc0e")
            head_products(0, qT, head_keys, [1, 3, 5, 7], 1, "sc0o")
            pe.wait_ge(*done("act", "u1"))
            head_products(1, qT, head_keys, [0, 2], 2, "sc1a")
            head_products(1, qT, head_keys, [1, 3], 3, "sc1b")
            pe.wait_ge(*done("act", "sg1"))
            head_products(1, qT, head_keys, [4, 6], 4, "sc1c")
            head_products(1, qT, head_keys, [5, 7], 5, "sc1d")
            for i in range(4, 8):
                pe.wait_ge(*done("act", f"sg{i - 2}"))
                project_T(8 + i, 6 + i % 2, f"g{i}")
            pe.wait_ge(scale_in, 16)
            pe.wait_ge(*done("dve", "msk0o"))
            turn_(bank[1][:, 0:NG], scale_rows[:, :], ident[0:NG, 0:NG]).then_inc(*tell("pe", "scaleT"))
            pe.wait_ge(pool_in, 16)
            pe.wait_ge(*done("pool", "mixed"))
            for i, n in enumerate("ab"):
                if i == 1:
                    pe.wait_ge(*done("act", "scale"))
                for c in range(2):
                    last = mm(bank[i][:, c * S:(c + 1) * S], poolw_sb[:, 2 * i + c, :], mixed[:, 2 * i + c, :],
                              start=True, stop=True)
                last.then_inc(*tell("pe", f"y1{n}"))
            pe.wait_ge(*done("dve", "P0"))
            for i, n in enumerate("ab"):
                pe.wait_ge(*done("dve", f"y1{n}"))
                for h in range(4):
                    last = turn_(bank[i][:, h * P:(h + 1) * P], sm0[:, 4 * i + h, :], ident[:, :])
                last.then_inc(*tell("pe", f"PT0{n}"))
            pe.wait_ge(*done("dve", "P1"))
            for i, n in enumerate("abcd"):
                for j in range(4):
                    h, kb = 2 * i + j // 2, j % 2
                    last = turn_(bank[2 + i][:, j * P:(j + 1) * P], sm1[:, h, kb * P:(kb + 1) * P], ident[:, :])
                last.then_inc(*tell("pe", f"PT1{n}"))
            for t in range(NT):
                pe.wait_ge(*done("act", f"sg{6 + t}"))
                pe.wait_ge(*done("act", "PT0b" if t == 0 else "PT1d"))
                for h in range(NH):
                    vh = h // GROUP
                    for kb in range(t + 1):
                        pt = PT0[:, h, :] if t == 0 else PT1[:, h, kb, :]
                        last = mm(bank[6 + t][DH * (h % 2):DH * (h % 2) + DH, (h // 2) * P:(h // 2 + 1) * P],
                                  v_sb[:, kb, vh * DH:(vh + 1) * DH], pt, start=(kb == 0), stop=(kb == t))
                last.then_inc(*tell("pe", f"o{t}"))
            pe.wait_ge(p_in, 16)
            for k in range(2):
                for t in range(NT):
                    last = turn_(bank[0][:, (2 * k + t) * P:(2 * k + t + 1) * P], p_sb[:, t, k * P:(k + 1) * P], ident[:, :])
            last.then_inc(*tell("pe", "pT"))
            pe.wait_ge(branch_in[0], 16)
            for i in range(4):
                for c in range(2):
                    j = 2 * i + c
                    for k in range(NG):
                        last = mm(bank[2 + i][:, c * S:(c + 1) * S], bp_sb[:, k, j * P:(j + 1) * P], y1T[:, k, :],
                                  start=(k == 0), stop=(k == NG - 1))
                last.then_inc(*tell("pe", f"yp{i}"))
            pe.wait_ge(branch_in[1], 16)
            pe.wait_ge(*done("act", "o1"))
            for i, b in enumerate([6, 7, 0, 1]):
                if i == 2:
                    pe.wait_ge(*done("act", "pT"))
                for c in range(2):
                    j = 2 * i + c
                    for k in range(AW // P):
                        last = mm(bank[b][:, c * S:(c + 1) * S], ba_sb[:, k, j * P:(j + 1) * P], oT[:, k, :],
                                  start=(k == 0), stop=(k == AW // P - 1))
                last.then_inc(*tell("pe", f"ya{i}"))
            pe.wait_ge(*done("dve", "yp3"))
            for k in range(KD):
                if k == 4:
                    last.then_inc(*tell("pe", "wout_low"))
                if k % 4 == 0:
                    pe.wait_ge(wout_in[k // 4], 16)
                if k % 2 == 0:
                    pe.wait_ge(*done("pool", f"m{k // 2}"))
                for t in range(NT):
                    for n in range(D // HALF):
                        last = mm(bank[2 + 2 * t + n][:, :], mT[:, k, t * P:(t + 1) * P], wide[:, k, n * HALF:(n + 1) * HALF],
                                  start=(k == 0), stop=(k == KD - 1))
            last.then_inc(*tell("pe", "wout"))
            pe.wait_ge(proj_in, 16)
            pe.wait_ge(*done("dve", "ya3"))

            for i, b in enumerate([6, 7, 0, 1]):
                t, n = i // 2, i % 2
                for k in range(2):
                    last = mm(bank[b][:, :], pT[:, k, t * P:(t + 1) * P], proj_sb[:, k, n * HALF:(n + 1) * HALF],
                              start=(k == 0), stop=(k == 1))
                last.then_inc(*tell("pe", f"ppj{i}"))

            turn_tile(2, 0, [2, 3])
            turn_tile(2, 1, [4, 5])
            pe.wait_ge(router_in, 16)
            pe.wait_ge(rb_in, 16)
            pe.wait_ge(*done("act", "hT20"))
            pe.wait_ge(*done("dve", "hT21"))
            for t in range(NT):
                mm(bank[2][:, t * E:(t + 1) * E], ones[0:1, :], rb_row[:, :], start=True, stop=False)
                for k in range(KD):
                    turned(2, k, [t])
                    last = mm(bank[2][:, t * E:(t + 1) * E], h2T[:, k, t * P:(t + 1) * P], router_sb[:, k, :],
                              start=False, stop=(k == KD - 1))
            last.then_inc(*tell("pe", "logits"))
            pe.wait_ge(*done("dve", "mask"))
            mm(bank[3][:, 0:E], tri[:, :], mask[:, 0, :], start=True, stop=True)
            mm(bank[3][:, E:2 * E], ones[:, :], mask[:, 0, :], start=True, stop=False)
            mm(bank[3][:, E:2 * E], tri[:, :], mask[:, 1, :], start=False, stop=True).then_inc(*tell("pe", "pos"))
            mm(bank[3][:, 2 * E:3 * E], ones[:, :], mask[:, 0, :], start=True, stop=False)
            mm(bank[3][:, 2 * E:3 * E], ones[:, :], mask[:, 1, :], start=False, stop=True).then_inc(*tell("pe", "count"))
            pe.wait_ge(*done("dve", "p1"))
            pe.wait_ge(*done("dve", "gt"))
            for t in range(NT):
                last = turn_(bank[3][0:E, t * P:(t + 1) * P], gate[:, t, 0:E], ident[:, :])
            last.then_inc(*tell("pe", "combT"))

            def gather():
                for t in range(NT):
                    for q in range(2):
                        last = mm(xg_ps[q * SLOT:(q + 1) * SLOT, :], sel[:, t, :], hn[:, t, q * HALF:(q + 1) * HALF],
                                  start=(t == 0), stop=(t == NT - 1), skip_group_check=True)
                return last

            def turn_block(dst, src):
                for c in range(4):
                    last = turn_(dst[:, c * P:(c + 1) * P], src[:, c * P:(c + 1) * P], ident[:, :])
                return last

            pe.wait_ge(*done("dve", "sel_first"))
            gather().then_inc(gathered, 1)
            pe.wait_ge(xg_ready, 1)
            turn_block(xg_ps, xg_rows).then_inc(xg_turned, 1)
            pe.wait_ge(b1_in, 16)
            pe.wait_ge(*done("act", "combT"))
            pe.wait_ge(*done("dve", "ppj3"))

            def scatter(t):
                for q in range(2):
                    rows = slice(q * SLOT, (q + 1) * SLOT)
                    last = mm(acc[2 * t + q][:, :], gselT[rows, t * P:(t + 1) * P], y_sb[rows, :],
                              start=False, stop=False, skip_group_check=True)
                return last

            def turn_gates():
                for t in range(NT):
                    last = turn_(xg_ps[:, t * P:(t + 1) * P], gsel[:, t, :, :], ident[:, :])
                return last

            def expert(turn, turn_next, arrived, arrived_low, last_turn, ahead=False):
                if last_turn is not None:
                    pe.wait_ge(xgT_ready, turn)
                    pe.wait_ge(gsel_ready, last_turn)
                    turn_gates().then_inc(gsel_turned, 1)
                w1_parts = [(ps, q, 2 * i + q) for i, ps in enumerate((lin_ps, up_ps)) for q in range(2)]
                pe.wait_ge(picked, turn)
                for ps, q, n in w1_parts:
                    mm(ps[q * SLOT:(q + 1) * SLOT, :], pick[:, :], b1_sb[:, n * HALF:(n + 1) * HALF],
                       start=True, stop=False, skip_group_check=True)
                pe.wait_ge(xgT_ready, turn)
                for k in range(KD):
                    if ahead and k < AHEAD:
                        rows = ahead_unit[k]
                        if k < NSTREAM:
                            pe.wait_ge(stream_in[k], 16 * (len(GROUPS) // NSTREAM + 1))
                        else:
                            pe.wait_ge(ahead_in, 16)
                    else:
                        rows = ring[:, k, :]
                        pe.wait_ge(ring_in[k], arrived_low if k < AHEAD else arrived)
                    for ps, q, n in w1_parts:
                        last = mm(ps[q * SLOT:(q + 1) * SLOT, :], xgT[:, k % 4, k // 4, :], rows[:, n * HALF:(n + 1) * HALF],
                                  start=False, stop=(k == KD - 1), skip_group_check=True)
                    if not ahead or k >= AHEAD:
                        last.then_inc(ring_used[k], 1)
                    elif k == NSTREAM - 1:
                        last.then_inc(*tell("pe", "ahead"))
                pe.wait_ge(sel_ready, turn)
                if last_turn is not None:
                    pe.wait_ge(gselT_ready, last_turn)
                gather().then_inc(gathered, 1)
                if last_turn is not None:
                    pe.wait_ge(y_ready, last_turn)
                    for t in range(NT):
                        scatter(t)
                else:
                    pe.wait_ge(b2_in, 16)
                    pe.wait_ge(b2_high_in, 16)
                    for t in range(NT):
                        for n in range(D // HALF):
                            last = mm(acc[2 * t + n][:, :], combT[:, t * P:(t + 1) * P], b2_halves[n],
                                      start=True, stop=False, skip_group_check=True)
                    last.then_inc(*tell("pe", "b2"))
                pe.wait_ge(act_ready, turn)
                turn_block(y_ps, act_rows).then_inc(act_turned, 1)
                pe.wait_ge(xg_ready, turn_next)
                turn_block(xg_ps, xg_rows).then_inc(xg_turned, 1)
                pe.wait_ge(actT_ready, turn)
                for k in range(KF):
                    u = KD + k // 2
                    if k % 2 == 0:
                        pe.wait_ge(ring_in[u], arrived)
                    w2u = ring[:, u, :].rearrange("p (k n) -> p k n", k=2)
                    for q in range(2):
                        last = mm(y_ps[q * SLOT:(q + 1) * SLOT, :], actT[:, k % 4, k // 4, :], w2u[:, k % 2, q * HALF:(q + 1) * HALF],
                                  start=(k == 0), stop=(k == KF - 1), skip_group_check=True)
                    if k % 2:
                        last.then_inc(ring_used[u], 1)

            expert(1, 2, 16, 16, None)
            expert(2, 3, 32, None, 1, ahead=True)
            pe.wait_ge(*done("dve", "iters"))
            n_it = pe.value_load(iters[0:1, 0:1], min_val=E, max_val=MAXIT)
            with pe.Fori(2, n_it) as it:
                expert(pe.snap(it + 1), pe.snap(it + 2), pe.snap(it * 16 + 16), pe.snap(it * 16), pe.snap(it))
            pe.wait_ge(xgT_ready, pe.snap(n_it + 1))
            pe.wait_ge(gsel_ready, n_it)
            turn_gates().then_inc(gsel_turned, 1)
            pe.wait_ge(gselT_ready, n_it)
            pe.wait_ge(y_ready, n_it)
            for t in range(NT):
                scatter(t).then_inc(*tell("pe", f"moe{t}"))

            def turn_half(i, b):
                pe.wait_ge(*done("dve", f"h3{i}"))
                for c in range(4):
                    k = 4 * (i % 2) + c
                    last = turn_(bank[b][:, c * P:(c + 1) * P], hn[:, i // 2, k * P:(k + 1) * P], ident[:, :])
                last.then_inc(*tell("pe", f"hT3{i}"))

            def gate_part(t, n, ks):
                for k in ks:
                    last = mm(bank[4 + 2 * t + n][:, :], hT[:, k, t * P:(t + 1) * P], wide[:, k, n * HALF:(n + 1) * HALF],
                              start=(k == 0), stop=(k == KD - 1), skip_group_check=True)
                if k == KD - 1:
                    last.then_inc(*tell("pe", f"pg{2 * t + n}"))

            low, high = range(KD // 2), range(KD // 2, KD)
            for i in range(2):
                turn_half(i, i)
            pe.wait_ge(plew_in, 16)
            pe.wait_ge(*done("act", "hT30"))
            gate_part(0, 0, low)
            pe.wait_ge(*done("dve", "x2b"))
            gate_part(0, 1, low)
            pe.wait_ge(*done("act", "hT31"))
            gate_part(0, 0, high)
            for i in range(2, 4):
                turn_half(i, i)
            gate_part(0, 1, high)
            pe.wait_ge(*done("act", "hT33"))
            gate_part(1, 0, range(KD))
            gate_part(1, 1, range(KD))


_INS = ["x", "p", "norm1_g", "w_in", "pool_w", "pool_scale", "w_branch_pool", "w_branch_attn", "w_out",
        "norm2_g", "router_w", "router_b", "exp_w1", "exp_b1", "exp_w2", "exp_b2",
        "ple_norm_g", "ple_gate_w", "ple_proj_w", "final_g"]


def kernel(**inputs):
    import numpy as _np
    import concourse.bacc as _bacc
    from concourse import mybir as _mybir
    from concourse.bass_utils import run_bass_kernel_spmd as _run

    nc = _bacc.Bacc("TRN2", target_bir_lowering=False, num_devices=1)
    arrays, args = {}, []
    for name in _INS:
        a = _np.ascontiguousarray(inputs[name])
        arrays[f"in_{name}"] = a
        args.append(nc.dram_tensor(f"in_{name}", a.shape, _mybir.dt.from_np(a.dtype), kind="ExternalInput").ap())
    shape = inputs["x"].shape
    out = nc.dram_tensor("out_x", shape, _mybir.dt.float32, kind="ExternalOutput").ap()
    hybrid_block(nc, *args, out)
    r = _run(nc, [arrays], core_ids=[0])
    return r.results[0]["out_x"]
```

```python
import concourse.bass as bass
from concourse import mybir
from contextlib import ExitStack


def hybrid_block(nc, x_d, p_d, norm1_g, w_in, pool_w, pool_scale, w_bp, w_ba, w_out,
                 norm2_g, router_w, router_b, exp_w1, exp_b1, exp_w2, exp_b2,
                 ple_norm_g, ple_gate_w, ple_proj_w, final_g, out_d):
    f32 = mybir.dt.float32
    f32r = mybir.dt.float32r
    i32 = mybir.dt.int32
    ALU = mybir.AluOpType
    ACT = mybir.ActivationFunctionType
    AX = mybir.AxisListType

    P = 128
    S, D = x_d.shape[1], x_d.shape[2]
    NT = S // P
    KD = D // P
    HALF = 512
    PW = pool_scale.shape[1]
    NG = PW // P
    WINDOWS = (2, 4, 8, 16)
    PAD = 16
    NH, DH = 8, 64
    NKV = 2
    GROUP = NH // NKV
    AW = NH * DH
    TOPK = S // 4
    E = router_w.shape[2]
    F = exp_w2.shape[2]
    KF = F // P
    TOPE = 4
    SLOT = 64
    MAXIT = E * (S // SLOT)
    EPS = 1e-6
    FILL, TAKEN, BIG = -1e38, -3e38, 1e30
    WARM_UP = 24

    C_U, C_Q = 0, PW
    C_K = C_Q + AW
    C_V = C_K + NKV * DH
    C_QI = C_V + NKV * DH
    C_KI = C_QI + NH * DH
    C_WI = C_KI + DH
    C_G = C_WI + NH

    GW = 256
    GROUPS = [(C_KI, DH + NH), (C_QI, GW), (C_QI + GW, GW), (C_K, GW), (C_Q, GW), (C_Q + GW, GW),
              (C_U, GW), (C_U + GW, GW)] + [(C_G + GW * i, GW) for i in range(2 * D // GW)]
    GROUP_STEPS = ["wi", "qi0", "qi1", "v", "q0", "q1", "u0", "u1"] + [f"g{i}" for i in range(2 * D // GW)]
    SPLIT = [i for i, name in enumerate(GROUP_STEPS) if name not in ("wi", "v")]
    NSPLIT = 3
    REST_ON_POOL = (5,)
    NSTREAM = 4
    SLOTF = KD * GW
    ODD = NSTREAM + 1
    NRING = 12

    ctx = ExitStack()
    with ctx:
        def sb(name, shape, dt=f32):
            return ctx.enter_context(nc.sbuf_tensor(name, shape, dt))

        def sem(name):
            return ctx.enter_context(nc.semaphore(name))

        with ExitStack() as early:
            parts = early.enter_context(nc.sbuf_tensor("parts", [P, NRING, SLOTF], f32r))
        ring = sb("ring", [P, NRING, SLOTF])
        stream = sb("stream", [P, NSTREAM, SLOTF])
        work = sb("work", [P, 12864])
        x_sb = sb("x_sb", [P, NT, D])
        hn = sb("hn", [P, NT, D])
        gain = sb("gain", [P, D])
        ident = sb("ident", [P, P])
        tri = sb("tri", [P, P])
        ones = sb("ones", [P, P])
        slot_no = sb("slot_no", [P, 2, SLOT])
        pos = sb("pos", [P, NT, MAXIT + 1])
        gate = sb("gate", [P, NT, MAXIT + 1])
        rb_all = sb("rb_all", [P, E])
        scale_rows = sb("scale_rows", [NG, P])
        scale_col = sb("scale_col", [P, NG])
        ss = sb("ss", [P, NT])
        half_ss = sb("half_ss", [P, 2 * NT])
        gate_rstd = sb("gate_rstd", [P, NT])
        rstd = sb("rstd", [P, NT])
        eps = sb("eps", [P, 1])
        top8 = sb("top8", [P, NT, 8])
        wi_sb = sb("wi_sb", [P, NT, NH])
        smax = sb("smax", [P, NH])
        ssum = sb("ssum", [P, NH])
        first_inv = sb("first_inv", [P, NG, PAD])
        lpad = sb("lpad", [P, NT, E + 4])
        top4 = sb("top4", [P, NT, 8])
        mask = sb("mask", [P, NT, E])
        expl = sb("expl", [P, NT, E])
        small = sb("small", [P, 8])
        least = sb("least", [P, NT])
        gsum = sb("gsum", [P, NT])
        pairs = sb("pairs", [P, 1], i32)

        sgT = ring[:, 8:10, :].rearrange("p a (c s) -> p (a c) s", s=S)
        sm1 = ring[:, 10, :].rearrange("p (h s) -> p h s", h=NH)
        PT1 = ring[:, 11, :].rearrange("p (h k s) -> p h k s", h=NH, k=NT)

        h_hi, h_lo = [parts[:, i, :].rearrange("p (k s) -> p k s", k=KD) for i in range(2)]

        gate_parts = [parts[:, 4 * i:4 * i + 4, :].rearrange("p a (c n) -> p (a c) n", n=D) for i in range(2)]
        hp_parts = [parts[:, KD + i, :].rearrange("p (k s) -> p k s", k=KD) for i in range(2)]

        def w_parts(s):
            i = 2 + 2 * (s % NSPLIT)
            return parts[:, i, :], parts[:, i + 1, :]

        def rest_done(s):
            return done("pool" if s in REST_ON_POOL else "dve", f"rest{s}")

        def gate_rest(k):
            return "pool" if k % 2 else "dve"

        def cut(a, n):
            return work[:, a:a + n]

        hT = cut(0, 2048).rearrange("p (k s) -> p k s", k=KD)
        qiT = cut(2048, 1024).rearrange("p (c s) -> p c s", s=S)
        qT = cut(3072, 1024).rearrange("p (c s) -> p c s", s=S)
        kiT = cut(4096, 256)
        kT = cut(4352, 512).rearrange("p (v s) -> p v s", v=NKV)
        v_sb = cut(4864, 256).rearrange("p (t c) -> p t c", t=NT)
        relu = cut(5120, 1024).rearrange("p (b c) -> p b c", b=2)
        sm0 = cut(5120, 1024).rearrange("p (h s) -> p h s", h=NH)
        score = [cut(6144, P), cut(6272, 2 * P)]
        uT = cut(6656, NG * (PAD + S)).rearrange("p (g s) -> p g s", g=NG)
        PT0 = cut(6656, 1024).rearrange("p (h s) -> p h s", h=NH)
        mixed = cut(7744, 1024).rearrange("p (g s) -> p g s", g=NG)
        s2 = cut(8768, NG * (PAD + S)).rearrange("p (g s) -> p g s", g=NG)
        s4 = cut(8768 + NG * (PAD + S), (NG - 1) * (PAD + S)).rearrange("p (g s) -> p g s", g=NG - 1)
        s8 = cut(10816, (NG - 2) * (PAD + S)).rearrange("p (g s) -> p g s", g=NG - 2)
        s16 = cut(10816 + 544, PAD + S).rearrange("p (g s) -> p g s", g=1)
        mT = cut(8768, 2048).rearrange("p (k s) -> p k s", k=KD)
        y1T = cut(10816, 1024).rearrange("p (g s) -> p g s", g=NG)
        oT = cut(11840, 1024).rearrange("p (c s) -> p c s", s=S)
        mix_tmp = PT1.rearrange("p h k s -> p (h k s)").rearrange("p (b s) -> p b s", b=4)
        poolw_sb = hn[:, 0, 0:NG * P].rearrange("p (g d) -> p g d", g=NG)
        bp_sb = stream[:, 0:2, :].rearrange("p a (c n) -> p (a c) n", n=D)
        ba_sb = stream[:, 2:4, :].rearrange("p a (c n) -> p (a c) n", n=D)
        wide = stream[:, :, :].rearrange("p a (c n) -> p (a c) n", n=D)

        ppj = cut(2048, 2048).rearrange("p (t n) -> p t n", t=NT)
        combT = work[0:E, 7424:7424 + S]
        b2_halves = [work[0:E, 6144:6144 + HALF], work[0:E, 12352:12352 + HALF]]
        p_sb = cut(6144, 512).rearrange("p (t n) -> p t n", t=NT)
        pT = cut(6656, 512).rearrange("p (k s) -> p k s", k=2)
        proj_sb = cut(10816, 2048).rearrange("p (k n) -> p k n", k=2)
        router_sb = cut(7168, KD * E).rearrange("p (k e) -> p k e", e=E)
        h2T = cut(8768, 2048).rearrange("p (k s) -> p k s", k=KD)
        square_dump = cut(7744, D)

        b1_sb = cut(4096, 2 * F)
        xg_rows = cut(0, HALF)
        xgT = cut(512, KD * SLOT).rearrange("p (c q j) -> p c q j", q=2, j=SLOT)
        sel = cut(1024, NT * SLOT).rearrange("p (t j) -> p t j", t=NT)
        gsel = cut(1152, NT * 2 * SLOT).rearrange("p (t q j) -> p t q j", t=NT, q=2)
        gselT = cut(1408, S)
        pick = cut(1664, SLOT)
        y_sb = cut(7168, HALF)
        lin = cut(7744, HALF)
        up = cut(8256, HALF)
        sigm = cut(10816, HALF)
        actT = cut(11328, HALF).rearrange("p (c q j) -> p c q j", q=2, j=SLOT)
        act_rows = cut(11840, HALF)

        odd_unit = [stream[:, i, :] for i in range(NSTREAM)] + [cut(8768, SLOTF)]

        final_gain = cut(6144, D)
        sgate = cut(4096, 2048).rearrange("p (b n) -> p b n", b=4)

        bank = [ctx.enter_context(nc.psum_tensor(f"bank{i}", [P, HALF], f32)) for i in range(8)]
        lin_ps, up_ps, xg_ps, y_ps = [bank[i][:, :] for i in range(4)]

        def pair(b):
            return bank[b][:, :].rearrange("p (c s) -> p c s", c=2)

        acc = bank[4:8]

        gain_in, pool_in, scale_in = sem("gain_in"), sem("pool_in"), sem("scale_in")
        x_in = [sem(f"x_in{t}") for t in range(NT)]
        stream_in = [sem(f"stream_in{i}") for i in range(NSTREAM)]
        ring_in = [sem(f"ring_in{i}") for i in range(NRING)]
        ring_used = [sem(f"ring_used{i}") for i in range(NRING)]
        b2_high_in = sem("b2_high_in")
        rb_in, router_in, b1_in, b2_in, p_in, proj_in = sem("rb_in"), sem("router_in"), sem("b1_in"), sem("b2_in"), sem("p_in"), sem("proj_in")
        gain2_in, gain3_in, final_in = sem("gain2_in"), sem("gain3_in"), sem("final_in")
        plew_in = [sem("plew_low_in"), sem("plew_high_in")]
        branch_in = [sem("branch_pool_in"), sem("branch_attn_in")]
        wout_in = [sem("wout_low_in"), sem("wout_high_in")]
        out_sem = sem("out_written")
        odd_in = [sem(f"odd_in{i}") for i in range(ODD)]
        odd_used = [sem(f"odd_used{i}") for i in range(ODD)]

        STEPS = {
            "pe": (
                "hT10 hT11 hT12 hT13 ki wi qi0 qi1 k v ix0e ix0o ix1a ix1b ix1c ix1d q0 q1 u0 u1 g0 g1 g2 g3 sc0e "
                "sc0o sc1a sc1b sc1c sc1d g4 g5 g6 g7 scaleT y1a y1b PT0a PT0b PT1a PT1b PT1c PT1d o0 o1 pT yp0 "
                "yp1 yp2 yp3 ya0 ya1 ya2 ya3 wout0 wout_low hT20 hT21 wout1 hT22 hT23 logits ppj0 pos count ppj1 "
                "combT ppj2 ppj3 b2 moe0 moe1 hT30 hT31 pg0 hT32 hT33 pg1 pg2 pg3").split(),
            "act": (
                "root_a sq10 std10 sq11 std11 hT10 hT12 h_hi round0 ki0 ki1 round1 qi0 round2 round3 qi1 round4 "
                "k0 k1 relu0 relu1 relu2 relu3 relu4 relu5 q0 round5 q1 round6 u0 round7 u1 round8 sg0 round9 sg1 "
                "round10 sg2 round11 sg3 round12 exp0 sg4 round13 sg5 exp1 sg6 sg7 scale PT0a PT0b PT1a PT1b PT1c "
                "PT1d o0 o1 pT root_b hT20 sq20 std20 hT22 sq21 std21 rexp0 rexp1 combT ppj0 ppj1 ppj2 ppj3 "
                "gate_round0 gate_round1 gate_round2 gate_round3 hT30 hT31 gate_round4 gate_round5 gate_round6 "
                "gate_round7 sq30 std30 hT32 hT33 sq31 std31 sgp0 sqf0 sgp1 sqf1 stdf0 sgp2 sqf2 sgp3 root_c sqf3 "
                "stdf1").split(),
            "dve": (
                "rstd10 h10 rstd11 h11 hT11 hT13 h_lo rest0 first_inv wi rest1 rest2 rest3 k2 k3 v rest4 ix0h0 "
                "ix0h1 ix0h2 ix0h3 ix0h4 ix0h5 ix0h6 ix0 ix1h0 ix1h1 ix1h2 ix1h3 ix1h4 ix1h5 ix1h6 ix1 tk0m0 "
                "tk1m0 tk0r0 tk1r0 tk0m1 tk1m1 tk0r1 tk1r1 tk0m2 tk1m2 tk0r2 tk1r2 tk0m3 tk1m3 tk0r3 tk1r3 tk0m4 "
                "tk1m4 tk0r4 tk1r4 tk0m5 tk1m5 tk0r5 tk1r5 tk0m6 tk1m6 tk0r6 tk1r6 tk0m7 tk1m7 tk0r7 tk1r7 neg0 "
                "neg1 rest6 rest7 rest8 rest9 rest10 rest11 msk0e msk0o max0 nmax0 msk1a msk1b msk1c msk1d rest12 "
                "rcp0 P0 max1 nmax1 rest13 rcp1 P1 y1a y1b yp0 yp1 yp2 yp3 ya0 ya1 ya2 ya3 x1a h20 x1b h21 hT21 "
                "rstd20 x1c h22 x1d h23 hT23 rstd21 l0 l1 top0 top1 nm t4 mr0 mr1 mask em rs rr gt cmax p1 p2 "
                "sel_first pm1 gm1 pm2 gm2 pm3 gm3 over osum pairs gate_rest0 x2a h30 x2b h31 hp_rest0 gate_rest2 "
                "hp_rest1 x2c h32 gate_rest4 x2d h33 gate_rest6 hp_rest2 hp_rest3 rstd30 rstd31 pl0 x30 pl1 x31 "
                "sum0 rstdf0 out00 out01 pl2 x32 pl3 x33 sum1 rstdf1 out10 out11").split(),
            "pool": (
                "eps ident0 ident tri0 tri ones slot_no pad iota inv_min causal0 causal1 rest5 s2 s4 s8 s16 mx0 "
                "mx1 mx2 mx3 fix0 fix1 fix2 fix3 mixed causal_neg0 causal_neg1 m0 m1 m2 m3 b1_zero lpad endcol "
                "gate_rest1 gate_rest3 gate_rest5 gate_rest7").split(),
        }
        STEP_SEM = {e: sem(f"{e}_step") for e in STEPS}
        AT = {e: {n: i + 1 for i, n in enumerate(names)} for e, names in STEPS.items()}
        told = {e: [] for e in STEPS}

        def tell(engine, name):
            told[engine].append(name)
            assert STEPS[engine][len(told[engine]) - 1] == name, (engine, name, len(told[engine]))
            return STEP_SEM[engine], 1

        def done(engine, name):
            return STEP_SEM[engine], AT[engine][name]

        xg_ready, act_ready = sem("xg_ready"), sem("act_ready")
        sel_ready, gsel_ready = sem("sel_ready"), sem("gsel_ready")
        picked, xg_turned, xgT_ready = sem("picked"), sem("xg_turned"), sem("xgT_ready")
        act_turned, actT_ready = sem("act_turned"), sem("actT_ready")
        gathered, gsel_turned, gselT_ready = sem("gathered"), sem("gsel_turned"), sem("gselT_ready")
        lin_ready, up_ready = sem("lin_ready"), sem("up_ready")
        sig_ready, prod_ready = sem("sig_ready"), sem("prod_ready")
        y_ready = sem("y_ready")

        block = ctx.enter_context(nc.Block())

        w1_v = exp_w1[0].rearrange("e (k p) n -> e p k n", p=P)
        w2_v = exp_w2[0].rearrange("e (u k p) n -> e u p k n", p=P, k=2)

        @block.sync
        def _(sp):
            def load_unit(e, u, odd=False):
                if odd and u < ODD:
                    sp.dma_start(odd_unit[u], w1_v[e, :, u, :]).then_inc(odd_in[u], 16)
                elif u < KD:
                    sp.dma_start(ring[:, u, :], w1_v[e, :, u, :]).then_inc(ring_in[u], 16)
                else:
                    sp.dma_start(ring[:, u, :].rearrange("p (k n) -> p k n", k=2), w2_v[e, u - KD]).then_inc(ring_in[u], 16)

            for t in range(NT):
                sp.dma_start(x_sb[:, t, :], x_d[0, t * P:(t + 1) * P, :]).then_inc(x_in[t], 16)
            sp.dma_start(gain[:, :], norm1_g[0].partition_broadcast(P)).then_inc(gain_in, 16)

            def group_used(i):
                return rest_done(SPLIT.index(i)) if i in SPLIT else done("pe", GROUP_STEPS[i])

            def load_group(i):
                c0, n = GROUPS[i]
                s = i % NSTREAM
                dst = stream[:, s, 0:KD * n].rearrange("p (k n) -> p k n", n=n)
                if i >= NSTREAM:
                    sp.wait_ge(*group_used(i - NSTREAM))
                sp.dma_start(dst, w_in[0, :, c0:c0 + n].rearrange("(k p) n -> p k n", p=P)).then_inc(stream_in[s], 16)

            for i in range(NSTREAM):
                load_group(i)
            sp.dma_start(scale_rows[:, :], pool_scale[0].rearrange("(g p) -> g p", p=P)).then_inc(scale_in, 16)
            sp.dma_start(rb_all[:, :], router_b[0].partition_broadcast(P)).then_inc(rb_in, 16)
            for i in range(NSTREAM, len(GROUPS)):
                load_group(i)
                if i == NSTREAM:
                    sp.wait_ge(*done("dve", "h11"))
                    sp.wait_ge(*done("pe", "hT13"))
                    sp.dma_start(poolw_sb, pool_w[0].rearrange("g c d -> c g d")).then_inc(pool_in, 16)
            G = len(GROUPS)
            for i in (4, 3):
                sp.wait_ge(*group_used(G - i))
            sp.dma_start(bp_sb, w_bp[0].rearrange("(c p) n -> p c n", p=P)).then_inc(branch_in[0], 16)
            for i in (2, 1):
                sp.wait_ge(*group_used(G - i))
            sp.dma_start(ba_sb, w_ba[0].rearrange("(c p) n -> p c n", p=P)).then_inc(branch_in[1], 16)
            sp.wait_ge(*done("pe", GROUP_STEPS[-1]))
            for u in range(KD):
                load_unit(0, u)
            wo_v = w_out[0].rearrange("(k p) n -> p k n", p=P)
            sp.wait_ge(*done("pe", "yp3"))
            sp.dma_start(wide[:, 0:4, :], wo_v[:, 0:4, :]).then_inc(wout_in[0], 16)
            sp.wait_ge(*done("pe", "ya3"))
            sp.dma_start(wide[:, 4:8, :], wo_v[:, 4:8, :]).then_inc(wout_in[1], 16)
            sp.wait_ge(*done("pool", "m3"))
            for u in range(KD, NRING):
                load_unit(0, u)
            for u in range(ODD):
                sp.wait_ge(*done("pe", "wout_low" if u < NSTREAM // 2 else "wout1" if u < NSTREAM else "logits"))
                load_unit(1, u, odd=True)
            for u in range(ODD):
                sp.wait_ge(ring_used[u], 1)
                load_unit(2, u)
            for u in range(ODD, NRING):
                sp.wait_ge(ring_used[u], 1)
                load_unit(1, u)
            for u in range(ODD):
                sp.wait_ge(odd_used[u], 1)
                load_unit(3, u, odd=True)
            for e in (2, 3):
                for u in range(ODD, NRING):
                    sp.wait_ge(ring_used[u], e)
                    load_unit(e, u)
            sp.wait_ge(*done("dve", "pairs"))
            n_pairs = sp.value_load(pairs[0:1, 0:1], min_val=E // 2, max_val=MAXIT // 2)
            e_reg = sp.alloc_register("pair_of_experts")
            with sp.Fori(2, n_pairs) as j:
                sp.reg_alu(e_reg, j, E // 2 - 1, ALU.bitwise_and)
                sp.reg_alu(e_reg, e_reg, 1, ALU.logical_shift_left)
                e_even = sp.snap(e_reg, min_val=0, max_val=E - 2)
                sp.reg_alu(e_reg, e_reg, 1, ALU.add)
                e_odd = sp.snap(e_reg, min_val=1, max_val=E - 1)
                turn, turn_even, turn_odd = sp.snap(j), sp.snap(j * 2), sp.snap(j * 2 + 1)
                for u in range(NRING):
                    sp.wait_ge(ring_used[u], turn if u < ODD else turn_even)
                    load_unit(e_even, u)
                for u in range(ODD):
                    sp.wait_ge(odd_used[u], turn)
                    load_unit(e_odd, u, odd=True)
                for u in range(ODD, NRING):
                    sp.wait_ge(ring_used[u], turn_odd)
                    load_unit(e_odd, u)
            pg_v = ple_gate_w[0].rearrange("(k p) n -> p k n", p=P)
            for i in range(2):
                for u in range(2 * i, 2 * i + 2):
                    sp.wait_ge(odd_used[u], n_pairs)
                sp.dma_start(wide[:, 4 * i:4 * i + 4, :], pg_v[:, 4 * i:4 * i + 4, :]).then_inc(plew_in[i], 16)
            for t in range(NT):
                for n in range(2):
                    half = slice(n * HALF, (n + 1) * HALF)
                    sp.wait_ge(*done("dve", f"out{t}{n}"))
                    sp.dma_start(out_d[0, t * P:(t + 1) * P, half], hn[:, t, half]).then_inc(out_sem, 16)
            sp.wait_ge(out_sem, 16 * NT * 2)

        @block.gpsimd
        def _(pool):
            g = nc.gpsimd
            g.memset(eps[:, :], EPS).then_inc(*tell("pool", "eps"))
            g.memset(ident[:, :], 0.0).then_inc(*tell("pool", "ident0"))
            pool.wait_ge(*done("pool", "ident0"))
            g.affine_select(out=ident[:, :], in_=ident[:, :], compare_op=ALU.not_equal, fill=1.0, base=0,
                            pattern=[[-1, P]], channel_multiplier=1).then_inc(*tell("pool", "ident"))
            g.memset(tri[:, :], 1.0).then_inc(*tell("pool", "tri0"))
            pool.wait_ge(*done("pool", "tri0"))
            g.affine_select(out=tri[:, :], in_=tri[:, :], compare_op=ALU.is_gt, fill=0.0, base=0,
                            pattern=[[1, P]], channel_multiplier=-1).then_inc(*tell("pool", "tri"))
            g.memset(ones[:, :], 1.0).then_inc(*tell("pool", "ones"))
            g.iota(slot_no[:, :, :], [[0, 2], [1, SLOT]], base=0, channel_multiplier=0,
                   allow_small_or_imprecise_dtypes=True).then_inc(*tell("pool", "slot_no"))
            g.memset(uT[:, :, 0:PAD], 0.0).then_inc(*tell("pool", "pad"))
            g.iota(first_inv[:, :, :], [[0, NG], [1, PAD]], base=1, channel_multiplier=0,
                   allow_small_or_imprecise_dtypes=True).then_inc(*tell("pool", "iota"))
            pool.wait_ge(*done("pool", "iota"))
            for i, w in enumerate(WINDOWS):
                last = g.tensor_scalar(first_inv[:, i, :], first_inv[:, i, :], float(w), None, ALU.min)
            last.then_inc(*tell("pool", "inv_min"))
            for t in range(NT):
                pool.wait_ge(*done("dve", f"ix{t}"))
                g.affine_select(out=score[t], in_=score[t], compare_op=ALU.is_ge, fill=FILL, base=t * P,
                                pattern=[[-1, (t + 1) * P]], channel_multiplier=1).then_inc(*tell("pool", f"causal{t}"))
            for i in REST_ON_POOL:
                w_hi, w_lo = w_parts(i)
                pool.wait_ge(*done("act", f"round{i}"))
                g.tensor_tensor(w_lo, stream[:, SPLIT[i] % NSTREAM, :], w_hi.bitcast(f32), ALU.subtract)\
                    .then_inc(*tell("pool", f"rest{i}"))
            W = PAD + S
            pool.wait_ge(*done("pool", "pad"))
            pool.wait_ge(*done("act", "u1"))
            g.tensor_tensor(s2[:, :, 1:W], uT[:, :, 1:W], uT[:, :, 0:W - 1], ALU.add).then_inc(*tell("pool", "s2"))
            pool.wait_ge(*done("pool", "s2"))
            g.tensor_tensor(s4[:, :, 3:W], s2[:, 1:, 3:W], s2[:, 1:, 1:W - 2], ALU.add).then_inc(*tell("pool", "s4"))
            pool.wait_ge(*done("pool", "s4"))
            g.tensor_tensor(s8[:, :, 7:W], s4[:, 1:, 7:W], s4[:, 1:, 3:W - 4], ALU.add).then_inc(*tell("pool", "s8"))
            pool.wait_ge(*done("pool", "s8"))
            g.tensor_tensor(s16[:, :, 15:W], s8[:, 1:, 15:W], s8[:, 1:, 7:W - 8], ALU.add).then_inc(*tell("pool", "s16"))
            pool.wait_ge(*done("pool", "s16"))
            sums = [s2[:, 0, :], s4[:, 0, :], s8[:, 0, :], s16[:, 0, :]]
            for i, w in enumerate(WINDOWS):
                g.tensor_scalar(mixed[:, i, :], sums[i][:, PAD:W], 1.0 / w, None, ALU.mult)\
                    .then_inc(*tell("pool", f"mx{i}"))
            pool.wait_ge(*done("pool", "mx3"))
            pool.wait_ge(*done("dve", "first_inv"))
            for i in range(NG):
                g.tensor_tensor(mixed[:, i, 0:PAD], sums[i][:, PAD:2 * PAD], first_inv[:, i, :], ALU.mult)\
                    .then_inc(*tell("pool", f"fix{i}"))
            pool.wait_ge(*done("pool", "fix3"))
            g.tensor_tensor(mixed[:, :, :], mixed[:, :, :], uT[:, :, PAD:W], ALU.subtract).then_inc(*tell("pool", "mixed"))
            for t in range(NT):
                pool.wait_ge(*done("dve", f"neg{t}"))
                g.affine_select(out=score[t], in_=score[t], compare_op=ALU.is_ge, fill=-1.0, base=t * P,
                                pattern=[[-1, (t + 1) * P]], channel_multiplier=1)\
                    .then_inc(*tell("pool", f"causal_neg{t}"))
            pool.wait_ge(*done("dve", "h11"))
            g.dma_start(gain[:, :], norm2_g[0].partition_broadcast(P)).then_inc(gain2_in, 16)
            pool.wait_ge(*done("dve", "msk1d"))
            g.dma_start(p_sb, p_d[0, 0].rearrange("(t p) n -> p t n", p=P)).then_inc(p_in, 16)
            for i in range(4):
                pool.wait_ge(*done("dve", f"ya{i}"))
                g.tensor_tensor(mT[:, 2 * i:2 * i + 2, :], mT[:, 2 * i:2 * i + 2, :],
                                mix_tmp[:, i, :].rearrange("p (c s) -> p c s", c=2), ALU.add)\
                    .then_inc(*tell("pool", f"m{i}"))
            g.dma_start(proj_sb, ple_proj_w[0].rearrange("(k p) n -> p k n", p=P)).then_inc(proj_in, 16)
            g.memset(b1_sb, 0.0).then_inc(*tell("pool", "b1_zero"))
            pool.wait_ge(*done("pe", "pT"))
            g.dma_start(b2_halves[0], exp_b2[0, :, 0:HALF]).then_inc(b2_in, 16)
            g.dma_start(router_sb[:, :, :], router_w[0].rearrange("(k p) e -> p k e", p=P)).then_inc(router_in, 16)
            pool.wait_ge(*done("pool", "b1_zero"))
            g.dma_start(work[0:E, 4096:4096 + 2 * F], exp_b1[0]).then_inc(b1_in, 16)
            g.memset(lpad[:, :, E:E + 4], FILL).then_inc(*tell("pool", "lpad"))
            g.memset(pos[:, :, MAXIT:MAXIT + 1], -1.0)
            g.memset(gate[:, :, MAXIT:MAXIT + 1], 0.0).then_inc(*tell("pool", "endcol"))
            pool.wait_ge(*done("dve", "h23"))
            g.dma_start(gain[:, :], ple_norm_g[0].partition_broadcast(P)).then_inc(gain3_in, 16)
            pool.wait_ge(*done("pe", "ppj3"))
            g.dma_start(b2_halves[1], exp_b2[0, :, HALF:D]).then_inc(b2_high_in, 16)
            pool.wait_ge(*done("pe", "b2"))
            g.dma_start(final_gain, final_g.partition_broadcast(P)).then_inc(final_in, 16)
            for k in range(1, KD, 2):
                pool.wait_ge(*done("act", f"gate_round{k}"))
                g.tensor_tensor(gate_parts[1][:, k, :], wide[:, k, :], gate_parts[0][:, k, :].bitcast(f32), ALU.subtract)\
                    .then_inc(*tell("pool", f"gate_rest{k}"))

        @block.scalar
        def _(act):
            a = nc.scalar

            def norm_stats(n, t, dump):
                a.activation(dump, x_sb[:, t, :], ACT.Square, accum_out=ss[:, t:t + 1]).then_inc(*tell("act", f"sq{n}{t}"))
                act.wait_ge(*done("act", f"sq{n}{t}"))
                a.activation(rstd[:, t:t + 1], ss[:, t:t + 1], ACT.Sqrt, bias=eps[:, :], scale=1.0 / D)\
                    .then_inc(*tell("act", f"std{n}{t}"))

            def evacuate_turned(n, i, dst, b):
                evacuate(f"hT{n}{i}", dst[:, 4 * (i % 2):4 * (i % 2) + 4, (i // 2) * P:(i // 2 + 1) * P],
                         bank[b][:, :].rearrange("p (k s) -> p k s", s=P)).then_inc(*tell("act", f"hT{n}{i}"))

            def evacuate(name, dst, src, func=ACT.Copy, **kw):
                act.wait_ge(*done("pe", name))
                return a.activation(dst, src, func, **kw)

            act.wait_ge(*done("pool", "eps"))
            a.activation(small[:, 0:1], eps[:, :], ACT.Sqrt).then_inc(*tell("act", "root_a"))
            for t in range(NT):
                act.wait_ge(x_in[t], 16)
                norm_stats(1, t, hn[:, t, :])
            def round_group(s):
                if s >= NSPLIT:
                    act.wait_ge(*done("pe", GROUP_STEPS[SPLIT[s - NSPLIT]]))
                i = SPLIT[s]
                act.wait_ge(stream_in[i % NSTREAM], 16 * (i // NSTREAM + 1))
                a.activation(w_parts(s)[0], stream[:, i % NSTREAM, :], ACT.Copy).then_inc(*tell("act", f"round{s}"))

            for i in (0, 2):
                evacuate_turned(1, i, hT, i)
            act.wait_ge(*done("act", "hT12"))
            act.wait_ge(*done("dve", "hT13"))
            a.activation(h_hi, hT, ACT.Copy).then_inc(*tell("act", "h_hi"))
            round_group(0)
            evacuate("ki", kiT[0:DH, :], bank[4][0:DH, 0:S]).then_inc(*tell("act", "ki0"))
            evacuate("ki", kiT[DH:P, :], bank[4][0:DH, 0:S]).then_inc(*tell("act", "ki1"))
            round_group(1)
            evacuate("qi0", qiT[:, 0:2, :], pair(6)).then_inc(*tell("act", "qi0"))
            round_group(2)
            round_group(3)
            evacuate("qi1", qiT[:, 2:4, :], pair(7)).then_inc(*tell("act", "qi1"))
            round_group(4)
            evacuate("k", kT[0:DH, 0, :], bank[0][0:DH, 0:S]).then_inc(*tell("act", "k0"))
            evacuate("k", kT[DH:P, 0, :], bank[0][0:DH, 0:S]).then_inc(*tell("act", "k1"))
            for i, (name, b) in enumerate([("ix0e", 2), ("ix0o", 3), ("ix1a", 4), ("ix1b", 5), ("ix1c", 6), ("ix1d", 7)]):
                if i >= 2:
                    act.wait_ge(*done("dve", ["ix0h3", "ix0", "ix1h1", "ix1h3"][i - 2]))
                evacuate(name, relu[:, i % 2, :], bank[b][:, :], ACT.Relu, scale=DH ** -0.5)\
                    .then_inc(*tell("act", f"relu{i}"))
            for i in range(2):
                evacuate(f"q{i}", qT[:, 2 * i:2 * i + 2, :], pair(i)).then_inc(*tell("act", f"q{i}"))
                round_group(5 + i)
            for i in range(2):
                evacuate(f"u{i}", uT[:, 2 * i:2 * i + 2, PAD:PAD + S],
                         pair(2 + i)).then_inc(*tell("act", f"u{i}"))
                round_group(7 + i)

            def gates(i):
                b = 4 + i if i < 4 else 6 + i % 2
                evacuate(f"g{i}", sgT[:, 2 * i:2 * i + 2, :], pair(b),
                         ACT.Sigmoid).then_inc(*tell("act", f"sg{i}"))
                if 9 + i < len(SPLIT):
                    round_group(9 + i)

            def exps(t, sm):
                act.wait_ge(*done("dve", f"nmax{t}"))
                for h in range(NH):
                    last = a.activation(sm[:, h, :], sm[:, h, :], ACT.Exp, bias=smax[:, h:h + 1],
                                        scale=DH ** -0.5, accum_out=ssum[:, h:h + 1])
                last.then_inc(*tell("act", f"exp{t}"))

            for i in range(4):
                gates(i)
            exps(0, sm0)
            gates(4)
            gates(5)
            exps(1, sm1)
            gates(6)
            gates(7)
            evacuate("scaleT", scale_col[:, :], bank[1][:, 0:NG]).then_inc(*tell("act", "scale"))
            for i, n in enumerate("ab"):
                evacuate(f"PT0{n}", PT0[:, 4 * i:4 * i + 4, :], bank[i][:, :].rearrange("p (h s) -> p h s", s=P)).then_inc(*tell("act", f"PT0{n}"))
            for i, n in enumerate("abcd"):
                evacuate(f"PT1{n}", PT1[:, 2 * i:2 * i + 2, :, :].rearrange("p h k s -> p (h k s)"), bank[2 + i][:, :])\
                    .then_inc(*tell("act", f"PT1{n}"))
            for t in range(NT):
                evacuate(f"o{t}", oT[:, :, t * P:(t + 1) * P], bank[6 + t][:, :].rearrange("p (c s) -> p c s", s=P))\
                    .then_inc(*tell("act", f"o{t}"))
            evacuate("pT", pT[:, :, :], pair(0)).then_inc(*tell("act", "pT"))
            a.activation(small[:, 0:1], eps[:, :], ACT.Sqrt).then_inc(*tell("act", "root_b"))
            for t in range(NT):
                evacuate_turned(2, 2 * t, h2T, [6, 2][t])
                act.wait_ge(*done("dve", f"x1{'bd'[t]}"))
                if t:
                    act.wait_ge(*done("act", "sq20"))
                norm_stats(2, t, square_dump)
            for t in range(NT):
                act.wait_ge(*done("dve", "nm"))
                a.activation(expl[:, t, :], lpad[:, t, 0:E], ACT.Exp, bias=least[:, t:t + 1]).then_inc(*tell("act", f"rexp{t}"))
            act.wait_ge(gathered, 1)
            a.activation(xg_rows, xg_ps, ACT.Copy).then_inc(xg_ready, 1)
            evacuate("combT", combT, bank[1][0:E, 0:S]).then_inc(*tell("act", "combT"))
            act.wait_ge(xg_turned, 1)
            a.activation(xgT, xg_ps.rearrange("p (c q j) -> p c q j", q=2, j=SLOT), ACT.Copy).then_inc(xgT_ready, 1)
            for i in range(4):
                evacuate(f"ppj{i}", ppj[:, i // 2, (i % 2) * HALF:(i % 2 + 1) * HALF], bank[[6, 7, 4, 5][i]][:, :])\
                    .then_inc(*tell("act", f"ppj{i}"))

            def expert(turn, turn_next):
                act.wait_ge(lin_ready, turn)
                a.activation(sigm, lin, ACT.Sigmoid, scale=1.702).then_inc(sig_ready, 1)
                act.wait_ge(gathered, turn_next)
                a.activation(xg_rows, xg_ps, ACT.Copy).then_inc(xg_ready, 1)
                act.wait_ge(act_turned, turn)
                a.activation(actT, y_ps.rearrange("p (c q j) -> p c q j", q=2, j=SLOT), ACT.Copy).then_inc(actT_ready, 1)
                act.wait_ge(xg_turned, turn_next)
                a.activation(xgT, xg_ps.rearrange("p (c q j) -> p c q j", q=2, j=SLOT), ACT.Copy).then_inc(xgT_ready, 1)

            expert(1, 2)
            expert(2, 3)
            act.wait_ge(*done("dve", "pairs"))
            n_pairs = act.value_load(pairs[0:1, 0:1], min_val=E // 2, max_val=MAXIT // 2)
            with act.Fori(1, n_pairs) as j:
                for parity in range(2):
                    expert(act.snap(j * 2 + parity + 1), act.snap(j * 2 + parity + 2))

            act.wait_ge(ring_used[NRING - 1], act.snap(n_pairs * 2))
            for t in range(NT):
                act.wait_ge(plew_in[t], 16)
                for k in range(4 * t, 4 * t + 4):
                    a.activation(gate_parts[0][:, k, :], wide[:, k, :], ACT.Copy).then_inc(*tell("act", f"gate_round{k}"))
                if t == 0:
                    for i in range(2):
                        evacuate_turned(3, i, hp_parts[0], i)
            for t in range(NT):
                if t:
                    for i in range(2, 4):
                        evacuate_turned(3, i, hp_parts[0], i)
                act.wait_ge(*done("dve", f"x2{'bd'[t]}"))
                norm_stats(3, t, sgate[:, 2 * t:2 * t + 2, :].rearrange("p b n -> p (b n)"))
            for i in range(4):
                if i == 0:
                    act.wait_ge(*done("dve", "rstd31"))
                evacuate(f"pg{i}", sgate[:, i, :], bank[4 + i][:, :], ACT.Sigmoid, scale=gate_rstd[:, i // 2:i // 2 + 1])\
                    .then_inc(*tell("act", f"sgp{i}"))
                if i == 3:
                    a.activation(small[:, 0:1], eps[:, :], ACT.Sqrt).then_inc(*tell("act", "root_c"))
                act.wait_ge(*done("pe", "hT33"))
                act.wait_ge(*done("dve", f"x3{i}"))
                half = slice((i % 2) * HALF, (i % 2 + 1) * HALF)
                a.activation(hn[:, i // 2, half], x_sb[:, i // 2, half], ACT.Square, accum_out=half_ss[:, i:i + 1])\
                    .then_inc(*tell("act", f"sqf{i}"))
                if i % 2:
                    t = i // 2
                    act.wait_ge(*done("dve", f"sum{t}"))
                    a.activation(rstd[:, t:t + 1], ss[:, t:t + 1], ACT.Sqrt, bias=eps[:, :], scale=1.0 / D)\
                        .then_inc(*tell("act", f"stdf{t}"))

        @block.vector
        def _(dve):
            v = nc.vector

            dve.wait_ge(gain_in, 16)
            for t in range(NT):
                dve.wait_ge(*done("act", f"std1{t}"))
                v.reciprocal(rstd[:, t:t + 1], rstd[:, t:t + 1]).then_inc(*tell("dve", f"rstd1{t}"))
                dve.wait_ge(*done("dve", f"rstd1{t}"))
                v.scalar_tensor_tensor(hn[:, t, :], x_sb[:, t, :], rstd[:, t:t + 1], gain[:, :], ALU.mult, ALU.mult)\
                    .then_inc(*tell("dve", f"h1{t}"))

            def evacuate_turned(n, i, dst, b):
                dve.wait_ge(*done("pe", f"hT{n}{i}"))
                v.tensor_copy(dst[:, 4 * (i % 2):4 * (i % 2) + 4, (i // 2) * P:(i // 2 + 1) * P],
                              bank[b][:, :].rearrange("p (k s) -> p k s", s=P)).then_inc(*tell("dve", f"hT{n}{i}"))

            for i in (1, 3):
                evacuate_turned(1, i, hT, i)
            def rest(*groups):
                for s in groups:
                    w_hi, w_lo = w_parts(s)
                    dve.wait_ge(*done("act", f"round{s}"))
                    v.tensor_tensor(w_lo, stream[:, SPLIT[s] % NSTREAM, :], w_hi.bitcast(f32), ALU.subtract)\
                        .then_inc(*tell("dve", f"rest{s}"))

            dve.wait_ge(*done("dve", "hT13"))
            dve.wait_ge(*done("act", "h_hi"))
            v.tensor_tensor(h_lo, hT, h_hi.bitcast(f32), ALU.subtract).then_inc(*tell("dve", "h_lo"))
            rest(0)
            dve.wait_ge(*done("pool", "inv_min"))
            v.reciprocal(first_inv[:, :, :], first_inv[:, :, :]).then_inc(*tell("dve", "first_inv"))
            dve.wait_ge(*done("pe", "wi"))
            v.tensor_scalar(wi_sb[:, :, :], bank[5][:, 0:NT * NH].rearrange("p (t h) -> p t h", t=NT),
                            NH ** -0.5, None, ALU.mult).then_inc(*tell("dve", "wi"))
            rest(1, 2, 3)
            dve.wait_ge(*done("pe", "k"))
            v.tensor_copy(kT[0:DH, 1, :], bank[0][DH:P, 0:S]).then_inc(*tell("dve", "k2"))
            v.tensor_copy(kT[DH:P, 1, :], bank[0][DH:P, 0:S]).then_inc(*tell("dve", "k3"))
            dve.wait_ge(*done("pe", "v"))
            v.tensor_copy(v_sb[:, :, :], bank[1][:, 0:NT * P].rearrange("p (t c) -> p t c", t=NT))\
                .then_inc(*tell("dve", "v"))
            rest(4)
            dve.wait_ge(*done("dve", "wi"))
            for t in range(NT):
                n = (t + 1) * P
                per = HALF // n
                order = [0, 2, 4, 6, 1, 3, 5, 7] if t == 0 else [0, 2, 1, 3, 4, 6, 5, 7]
                for i, h in enumerate(order):
                    b = (0 if t == 0 else 2) + i // per
                    dve.wait_ge(*done("act", f"relu{b}"))
                    r = relu[:, b % 2, (i % per) * n:(i % per + 1) * n]
                    name = f"ix{t}" if i == NH - 1 else f"ix{t}h{i}"
                    if i == 0:
                        v.tensor_scalar(score[t], r, wi_sb[:, t, h:h + 1], None, ALU.mult).then_inc(*tell("dve", name))
                    else:
                        dve.wait_ge(*done("dve", f"ix{t}h{i - 1}"))
                        v.scalar_tensor_tensor(score[t], r, wi_sb[:, t, h:h + 1], score[t], ALU.mult, ALU.add)\
                            .then_inc(*tell("dve", name))
            for r in range(TOPK // 8):
                for t in range(NT):
                    dve.wait_ge(*(done("dve", f"tk{t}r{r - 1}") if r else done("pool", f"causal{t}")))
                    v.max(top8[:, t, :], score[t]).then_inc(*tell("dve", f"tk{t}m{r}"))
                for t in range(NT):
                    dve.wait_ge(*done("dve", f"tk{t}m{r}"))
                    v.match_replace(score[t], top8[:, t, :], score[t], TAKEN).then_inc(*tell("dve", f"tk{t}r{r}"))
            for t in range(NT):
                dve.wait_ge(*done("dve", f"tk{t}r{TOPK // 8 - 1}"))
                v.tensor_scalar(score[t], score[t], TAKEN, 1.0, ALU.is_equal, ALU.subtract).then_inc(*tell("dve", f"neg{t}"))

            rest(6, 7, 8, 9, 10, 11)

            def masked(t, name, pe_name, b, heads, sm):
                n = (t + 1) * P
                dve.wait_ge(*done("pe", pe_name))
                v.scalar_tensor_tensor(sm[:, heads, :], score[t].rearrange("p (o s) -> p o s", o=1).broadcast_to([P, HALF // n, n]),
                                       BIG, bank[b][:, :].rearrange("p (h s) -> p h s", s=n), ALU.mult, ALU.add)\
                    .then_inc(*tell("dve", name))

            def row_max(t, sm, last):
                dve.wait_ge(*done("dve", last))
                if t:
                    dve.wait_ge(*done("act", "exp0"))
                v.tensor_reduce(smax[:, :], sm, AX.X, ALU.max).then_inc(*tell("dve", f"max{t}"))
                dve.wait_ge(*done("dve", f"max{t}"))
                v.tensor_scalar(smax[:, :], smax[:, :], -(DH ** -0.5), None, ALU.mult).then_inc(*tell("dve", f"nmax{t}"))

            def normalise(t, sm):
                n = (t + 1) * P
                dve.wait_ge(*done("act", f"exp{t}"))
                v.reciprocal(ssum[:, :], ssum[:, :]).then_inc(*tell("dve", f"rcp{t}"))
                dve.wait_ge(*done("dve", f"rcp{t}"))
                v.tensor_tensor(sm, sm, ssum[:, :].rearrange("p (h o) -> p h o", o=1).broadcast_to([P, NH, n]), ALU.mult)\
                    .then_inc(*tell("dve", f"P{t}"))

            dve.wait_ge(*done("pool", "causal_neg0"))
            masked(0, "msk0e", "sc0e", 0, slice(0, NH, 2), sm0)
            masked(0, "msk0o", "sc0o", 1, slice(1, NH, 2), sm0)
            row_max(0, sm0, "msk0o")
            dve.wait_ge(*done("pool", "causal_neg1"))
            masked(1, "msk1a", "sc1a", 2, slice(0, 4, 2), sm1)
            masked(1, "msk1b", "sc1b", 3, slice(1, 4, 2), sm1)
            masked(1, "msk1c", "sc1c", 4, slice(4, NH, 2), sm1)
            masked(1, "msk1d", "sc1d", 5, slice(5, NH, 2), sm1)
            rest(12)
            normalise(0, sm0)
            row_max(1, sm1, "msk1d")
            rest(13)
            normalise(1, sm1)
            for i, n in enumerate("ab"):
                dve.wait_ge(*done("pe", f"y1{n}"))
                dve.wait_ge(*done("act", "scale"))
                v.tensor_tensor(y1T[:, 2 * i:2 * i + 2, :], pair(i),
                                scale_col[:, 2 * i:2 * i + 2].rearrange("p (c o) -> p c o", o=1).broadcast_to([P, 2, S]),
                                ALU.mult).then_inc(*tell("dve", f"y1{n}"))
            for i in range(4):
                dve.wait_ge(*done("pe", f"yp{i}"))
                v.tensor_tensor(mT[:, 2 * i:2 * i + 2, :], pair(2 + i),
                                sgT[:, 2 * i:2 * i + 2, :], ALU.mult).then_inc(*tell("dve", f"yp{i}"))
            dve.wait_ge(*done("pe", "o1"))
            for i in range(4):
                dve.wait_ge(*done("pe", f"ya{i}"))
                v.tensor_tensor(mix_tmp[:, i, :].rearrange("p (c s) -> p c s", c=2),
                                pair([6, 7, 0, 1][i]),
                                sgT[:, KD + 2 * i:KD + 2 * i + 2, :], ALU.mult).then_inc(*tell("dve", f"ya{i}"))

            dve.wait_ge(gain2_in, 16)
            for i in range(4):
                t, half = i // 2, slice((i % 2) * HALF, (i % 2 + 1) * HALF)
                dve.wait_ge(*done("pe", f"wout{t}"))
                v.tensor_tensor(x_sb[:, t, half], x_sb[:, t, half], bank[2 + i][:, :], ALU.add).then_inc(*tell("dve", f"x1{'abcd'[i]}"))
                dve.wait_ge(*done("dve", f"x1{'abcd'[i]}"))
                v.tensor_tensor(hn[:, t, half], x_sb[:, t, half], gain[:, half], ALU.mult).then_inc(*tell("dve", f"h2{i}"))
                if i % 2:
                    evacuate_turned(2, i, h2T, [7, 3][t])
                    dve.wait_ge(*done("act", f"std2{t}"))
                    v.reciprocal(rstd[:, t:t + 1], rstd[:, t:t + 1]).then_inc(*tell("dve", f"rstd2{t}"))

            dve.wait_ge(*done("pe", "logits"))
            dve.wait_ge(*done("pool", "endcol"))
            dve.wait_ge(rb_in, 16)
            dve.wait_ge(*done("dve", "rstd21"))
            for t in range(NT):
                v.scalar_tensor_tensor(lpad[:, t, 0:E], bank[0][:, t * E:(t + 1) * E], rstd[:, t:t + 1], rb_all[:, :],
                                       ALU.mult, ALU.add).then_inc(*tell("dve", f"l{t}"))
            dve.wait_ge(*done("dve", "l1"))
            for t in range(NT):
                v.max(top4[:, t, :], lpad[:, t, :]).then_inc(*tell("dve", f"top{t}"))
            dve.wait_ge(*done("dve", "top1"))
            v.tensor_scalar(least[:, :], top4[:, :, 0], -1.0, None, ALU.mult).then_inc(*tell("dve", "nm"))
            v.memset(top4[:, :, TOPE:8], FILL).then_inc(*tell("dve", "t4"))
            dve.wait_ge(*done("dve", "t4"))
            dve.wait_ge(*done("act", "rexp1"))
            for t in range(NT):
                v.match_replace(lpad[:, t, :], top4[:, t, :], lpad[:, t, :], TAKEN).then_inc(*tell("dve", f"mr{t}"))
            dve.wait_ge(*done("dve", "mr1"))
            v.tensor_scalar(mask[:, :, :], lpad[:, :, 0:E], TAKEN, None, ALU.is_equal).then_inc(*tell("dve", "mask"))
            dve.wait_ge(*done("dve", "mask"))
            v.tensor_tensor(expl[:, :, :], expl[:, :, :], mask[:, :, :], ALU.mult).then_inc(*tell("dve", "em"))
            dve.wait_ge(*done("dve", "em"))
            v.tensor_reduce(gsum[:, :], expl[:, :, :], AX.X, ALU.add).then_inc(*tell("dve", "rs"))
            dve.wait_ge(*done("dve", "rs"))
            v.reciprocal(gsum[:, :], gsum[:, :]).then_inc(*tell("dve", "rr"))
            dve.wait_ge(*done("dve", "rr"))
            v.tensor_tensor(gate[:, :, 0:E], expl[:, :, :], gsum[:, :].rearrange("p (t o) -> p t o", o=1).broadcast_to([P, NT, E]),
                            ALU.mult).then_inc(*tell("dve", "gt"))
            dve.wait_ge(*done("pe", "count"))
            v.tensor_reduce(small[:, 3:4], bank[1][:, NT * E:(NT + 1) * E], AX.X, ALU.max).then_inc(*tell("dve", "cmax"))
            v.scalar_tensor_tensor(pos[:, :, 0:E], bank[1][:, 0:NT * E].rearrange("p (t e) -> p t e", t=NT), 1.0,
                                   mask[:, :, :], ALU.add, ALU.mult).then_inc(*tell("dve", "p1"))
            dve.wait_ge(*done("dve", "p1"))
            v.tensor_scalar(pos[:, :, 0:E], pos[:, :, 0:E], 1.0, None, ALU.subtract).then_inc(*tell("dve", "p2"))
            dve.wait_ge(*done("dve", "p2"))
            for t in range(NT):
                last = v.tensor_scalar(sel[:, t, :], slot_no[:, 0, :], pos[:, t, 0:1], rstd[:, t:t + 1], ALU.is_equal, ALU.mult)
            last.then_inc(*tell("dve", "sel_first"))
            v.tensor_copy(pick[:, :], ident[:, 0:1].broadcast_to([P, SLOT])).then_inc(picked, 1)

            for i in range(1, S // SLOT):
                v.tensor_scalar(pos[:, :, i * E:(i + 1) * E], pos[:, :, 0:E], float(SLOT * i), None, ALU.subtract)\
                    .then_inc(*tell("dve", f"pm{i}"))
                if i == 1:
                    dve.wait_ge(*done("dve", "gt"))
                v.tensor_copy(gate[:, :, i * E:(i + 1) * E], gate[:, :, 0:E]).then_inc(*tell("dve", f"gm{i}"))

            dve.wait_ge(*done("dve", "cmax"))
            for i in range(S // SLOT - 1):
                last = v.tensor_scalar(small[:, 4 + i:5 + i], small[:, 3:4], float(SLOT * (i + 1)), float(E // 2), ALU.is_gt, ALU.mult)
            last.then_inc(*tell("dve", "over"))
            dve.wait_ge(*done("dve", "over"))
            v.tensor_reduce(small[:, 1:2], small[:, 4:4 + S // SLOT - 1], AX.X, ALU.add).then_inc(*tell("dve", "osum"))
            dve.wait_ge(*done("dve", "osum"))
            v.tensor_scalar(pairs[:, :], small[:, 1:2], float(E // 2), None, ALU.add).then_inc(*tell("dve", "pairs"))

            def expert(turn, last_turn, it, e_next):
                if last_turn is not None:
                    dve.wait_ge(gsel_turned, last_turn)
                    v.tensor_copy(gselT, xg_ps[:, 0:S]).then_inc(gselT_ready, 1)
                for t in range(NT):
                    last = v.tensor_scalar(gsel[:, t, :, :], slot_no[:, :, :], pos[:, t, bass.ds(it, 1)],
                                           gate[:, t, bass.ds(it, 1)], ALU.is_equal, ALU.mult)
                last.then_inc(gsel_ready, 1)
                dve.wait_ge(gathered, turn)
                for t in range(NT):
                    last = v.tensor_scalar(sel[:, t, :], slot_no[:, 0, :], pos[:, t, bass.ds(turn, 1)], rstd[:, t:t + 1],
                                           ALU.is_equal, ALU.mult)
                last.then_inc(sel_ready, 1)
                dve.wait_ge(ring_used[ODD], turn)
                v.tensor_copy(pick[:, :], ident[:, bass.ds(e_next, 1)].broadcast_to([P, SLOT])).then_inc(picked, 1)
                dve.wait_ge(ring_used[KD - 1], turn)
                v.tensor_scalar(lin, lin_ps, 7.0, None, ALU.min).then_inc(lin_ready, 1)
                v.tensor_scalar(up, up_ps, 7.0, -7.0, ALU.min, ALU.max).then_inc(up_ready, 1)
                dve.wait_ge(up_ready, turn)
                dve.wait_ge(lin_ready, turn)
                v.scalar_tensor_tensor(up, up, 1.0, lin, ALU.add, ALU.mult).then_inc(prod_ready, 1)
                dve.wait_ge(prod_ready, turn)
                dve.wait_ge(sig_ready, turn)
                v.tensor_tensor(act_rows, up, sigm, ALU.mult).then_inc(act_ready, 1)
                dve.wait_ge(ring_used[NRING - 1], turn)
                v.tensor_copy(y_sb, y_ps).then_inc(y_ready, 1)

            expert(1, None, 0, 1)
            expert(2, 1, 1, 2)
            dve.wait_ge(*done("dve", "pairs"))
            n_pairs = dve.value_load(pairs[0:1, 0:1], min_val=E // 2, max_val=MAXIT // 2)
            with dve.Fori(1, n_pairs) as j:
                for parity in range(2):
                    it, turn = dve.snap(j * 2 + parity), dve.snap(j * 2 + parity + 1)
                    expert(turn, it, it, turn & (E - 1))
            dve.wait_ge(gsel_turned, dve.snap(n_pairs * 2))
            v.tensor_copy(gselT, xg_ps[:, 0:S]).then_inc(gselT_ready, 1)

            def gate_remainder(k):
                dve.wait_ge(*done("act", f"gate_round{k}"))
                v.tensor_tensor(gate_parts[1][:, k, :], wide[:, k, :], gate_parts[0][:, k, :].bitcast(f32), ALU.subtract)\
                    .then_inc(*tell("dve", f"gate_rest{k}"))

            def rows(i):
                t, half = i // 2, slice((i % 2) * HALF, (i % 2 + 1) * HALF)
                dve.wait_ge(*done("pe", f"moe{t}"))
                v.tensor_tensor(x_sb[:, t, half], x_sb[:, t, half], acc[i][:, :], ALU.add).then_inc(*tell("dve", f"x2{'abcd'[i]}"))
                dve.wait_ge(*done("dve", f"x2{'abcd'[i]}"))
                v.tensor_tensor(hn[:, t, half], x_sb[:, t, half], gain[:, half], ALU.mult).then_inc(*tell("dve", f"h3{i}"))

            def rows_remainder(i):
                dve.wait_ge(*done("act", f"hT3{i}"))
                part = (slice(None), slice(4 * (i % 2), 4 * (i % 2) + 4), slice((i // 2) * P, (i // 2 + 1) * P))
                v.tensor_tensor(hp_parts[1][part], bank[i][:, :].rearrange("p (k s) -> p k s", s=P),
                                hp_parts[0][part].bitcast(f32), ALU.subtract).then_inc(*tell("dve", f"hp_rest{i}"))

            dve.wait_ge(gain3_in, 16)
            gate_remainder(0)
            rows(0)
            rows(1)
            rows_remainder(0)
            gate_remainder(2)
            rows_remainder(1)
            rows(2)
            gate_remainder(4)
            rows(3)
            gate_remainder(6)
            rows_remainder(2)
            rows_remainder(3)
            for t in range(NT):
                dve.wait_ge(*done("act", f"std3{t}"))
                v.reciprocal(gate_rstd[:, t:t + 1], rstd[:, t:t + 1]).then_inc(*tell("dve", f"rstd3{t}"))
            dve.wait_ge(final_in, 16)
            for i in range(4):
                t, half = i // 2, slice((i % 2) * HALF, (i % 2 + 1) * HALF)
                dve.wait_ge(*done("act", f"sgp{i}"))
                v.tensor_tensor(sgate[:, i, :], sgate[:, i, :], ppj[:, t, half], ALU.mult).then_inc(*tell("dve", f"pl{i}"))
                dve.wait_ge(*done("dve", f"pl{i}"))
                v.tensor_tensor(x_sb[:, t, half], x_sb[:, t, half], sgate[:, i, :], ALU.add).then_inc(*tell("dve", f"x3{i}"))
                if i % 2:
                    dve.wait_ge(*done("act", f"sqf{i}"))
                    v.tensor_tensor(ss[:, t:t + 1], half_ss[:, i - 1:i], half_ss[:, i:i + 1], ALU.add)\
                        .then_inc(*tell("dve", f"sum{t}"))
                    dve.wait_ge(*done("act", f"stdf{t}"))
                    v.reciprocal(rstd[:, t:t + 1], rstd[:, t:t + 1]).then_inc(*tell("dve", f"rstdf{t}"))
                    dve.wait_ge(*done("dve", f"rstdf{t}"))
                    for n in range(2):
                        half = slice(n * HALF, (n + 1) * HALF)
                        v.scalar_tensor_tensor(hn[:, t, half], x_sb[:, t, half], rstd[:, t:t + 1], final_gain[:, half],
                                               ALU.mult, ALU.mult).then_inc(*tell("dve", f"out{t}{n}"))

        @block.tensor
        def _(pe):
            mm = nc.tensor.matmul
            turn_ = nc.tensor.transpose

            pe.wait_ge(*done("pool", "ident"))

            pe.wait_ge(*done("pool", "ones"))
            for i in range(WARM_UP):
                last = mm(bank[7][:, 0:P], ones[:, :], tri[:, :], start=True, stop=True)

            for t in range(NT):
                pe.wait_ge(*done("dve", f"h1{t}"))
                for b in range(2):
                    for c in range(4):
                        k = 4 * b + c
                        last = turn_(bank[2 * t + b][:, c * P:(c + 1) * P], hn[:, t, k * P:(k + 1) * P], ident[:, :])
                    last.then_inc(*tell("pe", f"hT1{2 * t + b}"))

            def group(i):
                c0, n = GROUPS[i]
                pe.wait_ge(stream_in[i % NSTREAM], 16 * (i // NSTREAM + 1))
                return stream[:, i % NSTREAM, 0:KD * n].rearrange("p (k n) -> p k n", n=n)

            def project_T(i, b, name):
                s = SPLIT.index(i)
                w_hi, w_lo = [w.rearrange("p (k n) -> p k n", n=GW) for w in w_parts(s)]
                pe.wait_ge(*rest_done(s))
                for c in range(GW // P):
                    cols = slice(c * P, (c + 1) * P)
                    for k in range(KD):
                        for n, (w, h) in enumerate([(w_hi, h_hi), (w_hi, h_lo), (w_lo, h_hi)]):
                            last = mm(bank[b][:, c * S:(c + 1) * S], w[:, k, cols], h[:, k, :],
                                      start=(k == 0 and n == 0), stop=(k == KD - 1 and n == 2))
                last.then_inc(*tell("pe", name))

            w = group(0)
            for k in range(KD):
                if k % 4 == 0:
                    for t in range(NT):
                        pe.wait_ge(*done("act" if k == 0 else "dve", f"hT1{2 * t + k // 4}"))
                last = mm(bank[4][0:DH, 0:S], w[:, k, 0:DH], hT[:, k, :], start=(k == 0), stop=(k == KD - 1))
            last.then_inc(*tell("pe", "ki"))
            for t in range(NT):
                for k in range(KD):
                    last = mm(bank[5][:, t * NH:(t + 1) * NH], hT[:, k, t * P:(t + 1) * P], w[:, k, DH:DH + NH],
                              start=(k == 0), stop=(k == KD - 1))
            last.then_inc(*tell("pe", "wi"))
            project_T(1, 6, "qi0")
            project_T(2, 7, "qi1")
            w = group(3)
            for k in range(KD):
                last = mm(bank[0][:, 0:S], w[:, k, 0:P], hT[:, k, :], start=(k == 0), stop=(k == KD - 1))
            last.then_inc(*tell("pe", "k"))
            for t in range(NT):
                for k in range(KD):
                    last = mm(bank[1][:, t * P:(t + 1) * P], hT[:, k, t * P:(t + 1) * P], w[:, k, P:2 * P],
                              start=(k == 0), stop=(k == KD - 1))
            last.then_inc(*tell("pe", "v"))

            def head_products(t, qs, keys, heads, b, name):
                n = (t + 1) * P
                for i, h in enumerate(heads):
                    half = slice(DH * (h % 2), DH * (h % 2) + DH)
                    last = mm(bank[b][:, i * n:(i + 1) * n], qs[half, h // 2, t * P:(t + 1) * P], keys(h)[half, 0:n],
                              start=True, stop=True)
                last.then_inc(*tell("pe", name))

            pe.wait_ge(*done("act", "qi1"))
            pe.wait_ge(*done("dve", "wi"))
            index_keys = lambda h: kiT
            head_products(0, qiT, index_keys, [0, 2, 4, 6], 2, "ix0e")
            head_products(0, qiT, index_keys, [1, 3, 5, 7], 3, "ix0o")
            head_products(1, qiT, index_keys, [0, 2], 4, "ix1a")
            head_products(1, qiT, index_keys, [1, 3], 5, "ix1b")
            head_products(1, qiT, index_keys, [4, 6], 6, "ix1c")
            head_products(1, qiT, index_keys, [5, 7], 7, "ix1d")
            for i, (b, name, free) in enumerate([(0, "q0", ("dve", "k3")), (1, "q1", ("dve", "v")),
                                                 (2, "u0", ("act", "relu0")), (3, "u1", ("act", "relu1"))]):
                if i == 0:
                    pe.wait_ge(*done("act", "k1"))
                pe.wait_ge(*done(*free))
                project_T(4 + i, b, name)
            for i in range(4):
                pe.wait_ge(*done("act", f"relu{2 + i}"))
                project_T(8 + i, 4 + i, f"g{i}")
            head_keys = lambda h: kT[:, h // GROUP, :]
            pe.wait_ge(*done("act", "q1"))
            head_products(0, qT, head_keys, [0, 2, 4, 6], 0, "sc0e")
            head_products(0, qT, head_keys, [1, 3, 5, 7], 1, "sc0o")
            pe.wait_ge(*done("act", "u1"))
            head_products(1, qT, head_keys, [0, 2], 2, "sc1a")
            head_products(1, qT, head_keys, [1, 3], 3, "sc1b")
            pe.wait_ge(*done("act", "sg1"))
            head_products(1, qT, head_keys, [4, 6], 4, "sc1c")
            head_products(1, qT, head_keys, [5, 7], 5, "sc1d")
            for i in range(4, 8):
                pe.wait_ge(*done("act", f"sg{i - 2}"))
                project_T(8 + i, 6 + i % 2, f"g{i}")
            pe.wait_ge(scale_in, 16)
            pe.wait_ge(*done("dve", "msk0o"))
            turn_(bank[1][:, 0:NG], scale_rows[:, :], ident[0:NG, 0:NG]).then_inc(*tell("pe", "scaleT"))
            pe.wait_ge(pool_in, 16)
            pe.wait_ge(*done("pool", "mixed"))
            for i, n in enumerate("ab"):
                if i == 1:
                    pe.wait_ge(*done("act", "scale"))
                for c in range(2):
                    last = mm(bank[i][:, c * S:(c + 1) * S], poolw_sb[:, 2 * i + c, :], mixed[:, 2 * i + c, :],
                              start=True, stop=True)
                last.then_inc(*tell("pe", f"y1{n}"))
            pe.wait_ge(*done("dve", "P0"))
            for i, n in enumerate("ab"):
                pe.wait_ge(*done("dve", f"y1{n}"))
                for h in range(4):
                    last = turn_(bank[i][:, h * P:(h + 1) * P], sm0[:, 4 * i + h, :], ident[:, :])
                last.then_inc(*tell("pe", f"PT0{n}"))
            pe.wait_ge(*done("dve", "P1"))
            for i, n in enumerate("abcd"):
                for j in range(4):
                    h, kb = 2 * i + j // 2, j % 2
                    last = turn_(bank[2 + i][:, j * P:(j + 1) * P], sm1[:, h, kb * P:(kb + 1) * P], ident[:, :])
                last.then_inc(*tell("pe", f"PT1{n}"))
            for t in range(NT):
                pe.wait_ge(*done("act", f"sg{6 + t}"))
                pe.wait_ge(*done("act", "PT0b" if t == 0 else "PT1d"))
                for h in range(NH):
                    vh = h // GROUP
                    for kb in range(t + 1):
                        pt = PT0[:, h, :] if t == 0 else PT1[:, h, kb, :]
                        last = mm(bank[6 + t][DH * (h % 2):DH * (h % 2) + DH, (h // 2) * P:(h // 2 + 1) * P],
                                  v_sb[:, kb, vh * DH:(vh + 1) * DH], pt, start=(kb == 0), stop=(kb == t))
                last.then_inc(*tell("pe", f"o{t}"))
            pe.wait_ge(p_in, 16)
            for k in range(2):
                for t in range(NT):
                    last = turn_(bank[0][:, (2 * k + t) * P:(2 * k + t + 1) * P], p_sb[:, t, k * P:(k + 1) * P], ident[:, :])
            last.then_inc(*tell("pe", "pT"))
            pe.wait_ge(branch_in[0], 16)
            for i in range(4):
                for c in range(2):
                    j = 2 * i + c
                    for k in range(NG):
                        last = mm(bank[2 + i][:, c * S:(c + 1) * S], bp_sb[:, k, j * P:(j + 1) * P], y1T[:, k, :],
                                  start=(k == 0), stop=(k == NG - 1))
                last.then_inc(*tell("pe", f"yp{i}"))
            pe.wait_ge(branch_in[1], 16)
            pe.wait_ge(*done("act", "o1"))
            for i, b in enumerate([6, 7, 0, 1]):
                if i == 2:
                    pe.wait_ge(*done("act", "pT"))
                for c in range(2):
                    j = 2 * i + c
                    for k in range(AW // P):
                        last = mm(bank[b][:, c * S:(c + 1) * S], ba_sb[:, k, j * P:(j + 1) * P], oT[:, k, :],
                                  start=(k == 0), stop=(k == AW // P - 1))
                last.then_inc(*tell("pe", f"ya{i}"))
            def turn_half(n, i, b):
                pe.wait_ge(*done("dve", f"h{n}{i}"))
                for c in range(4):
                    k = 4 * (i % 2) + c
                    last = turn_(bank[b][:, c * P:(c + 1) * P], hn[:, i // 2, k * P:(k + 1) * P], ident[:, :])
                last.then_inc(*tell("pe", f"hT{n}{i}"))

            pe.wait_ge(*done("dve", "yp3"))
            for t in range(NT):
                for k in range(KD):
                    if t == 0 and k % 4 == 0:
                        pe.wait_ge(wout_in[k // 4], 16)
                    if t == 0 and k % 2 == 0:
                        pe.wait_ge(*done("pool", f"m{k // 2}"))
                    if t and k == 4:
                        last.then_inc(*tell("pe", "wout_low"))
                        pe.wait_ge(*done("dve", "ya1"))
                        for i in range(2):
                            turn_half(2, i, 6 + i)
                    for n in range(D // HALF):
                        last = mm(bank[2 + 2 * t + n][:, :], mT[:, k, t * P:(t + 1) * P], wide[:, k, n * HALF:(n + 1) * HALF],
                                  start=(k == 0), stop=(k == KD - 1), skip_group_check=True)
                last.then_inc(*tell("pe", f"wout{t}"))

            def logits(t, ks):
                for k in ks:
                    last = mm(bank[0][:, t * E:(t + 1) * E], h2T[:, k, t * P:(t + 1) * P], router_sb[:, k, :],
                              start=(k == 0), stop=(k == KD - 1), skip_group_check=True)
                return last

            low, high = range(KD // 2), range(KD // 2, KD)
            pe.wait_ge(router_in, 16)
            pe.wait_ge(*done("dve", "ya3"))
            pe.wait_ge(*done("act", "hT20"))
            pe.wait_ge(*done("dve", "hT21"))
            logits(0, range(KD))
            for i in range(2, 4):
                turn_half(2, i, i)
            pe.wait_ge(*done("act", "hT22"))
            logits(1, low)
            pe.wait_ge(*done("dve", "hT23"))
            logits(1, high).then_inc(*tell("pe", "logits"))

            def embed(i):
                for k in range(2):
                    last = mm(bank[[6, 7, 4, 5][i]][:, :], pT[:, k, (i // 2) * P:(i // 2 + 1) * P],
                              proj_sb[:, k, (i % 2) * HALF:(i % 2 + 1) * HALF], start=(k == 0), stop=(k == 1))
                last.then_inc(*tell("pe", f"ppj{i}"))

            pe.wait_ge(proj_in, 16)
            embed(0)
            pe.wait_ge(*done("dve", "mask"))
            mm(bank[1][:, 0:E], tri[:, :], mask[:, 0, :], start=True, stop=True)
            mm(bank[1][:, E:2 * E], ones[:, :], mask[:, 0, :], start=True, stop=False)
            mm(bank[1][:, E:2 * E], tri[:, :], mask[:, 1, :], start=False, stop=True).then_inc(*tell("pe", "pos"))
            mm(bank[1][:, 2 * E:3 * E], ones[:, :], mask[:, 0, :], start=True, stop=False)
            mm(bank[1][:, 2 * E:3 * E], ones[:, :], mask[:, 1, :], start=False, stop=True).then_inc(*tell("pe", "count"))
            embed(1)

            def gather():
                for t in range(NT):
                    for q in range(2):
                        last = mm(xg_ps[q * SLOT:(q + 1) * SLOT, :], sel[:, t, :], hn[:, t, q * HALF:(q + 1) * HALF],
                                  start=(t == 0), stop=(t == NT - 1), skip_group_check=True)
                return last

            def turn_block(dst, src):
                for c in range(4):
                    last = turn_(dst[:, c * P:(c + 1) * P], src[:, c * P:(c + 1) * P], ident[:, :])
                return last

            pe.wait_ge(*done("dve", "sel_first"))
            gather().then_inc(gathered, 1)
            pe.wait_ge(*done("dve", "p1"))
            pe.wait_ge(*done("dve", "gt"))
            for t in range(NT):
                last = turn_(bank[1][0:E, t * P:(t + 1) * P], gate[:, t, 0:E], ident[:, :])
            last.then_inc(*tell("pe", "combT"))
            embed(2)
            pe.wait_ge(xg_ready, 1)
            turn_block(xg_ps, xg_rows).then_inc(xg_turned, 1)
            embed(3)
            pe.wait_ge(b1_in, 16)
            pe.wait_ge(*done("act", "combT"))

            def scatter(t):
                for q in range(2):
                    rows = slice(q * SLOT, (q + 1) * SLOT)
                    last = mm(acc[2 * t + q][:, :], gselT[rows, t * P:(t + 1) * P], y_sb[rows, :],
                              start=False, stop=False, skip_group_check=True)
                return last

            def turn_gates():
                for t in range(NT):
                    last = turn_(xg_ps[:, t * P:(t + 1) * P], gsel[:, t, :, :], ident[:, :])
                return last

            def expert(turn, turn_next, arrived, arrived_low, last_turn, odd):
                if last_turn is not None:
                    pe.wait_ge(xgT_ready, turn)
                    pe.wait_ge(gsel_ready, last_turn)
                    turn_gates().then_inc(gsel_turned, 1)
                w1_parts = [(ps, q, 2 * i + q) for i, ps in enumerate((lin_ps, up_ps)) for q in range(2)]
                pe.wait_ge(picked, turn)
                for ps, q, n in w1_parts:
                    mm(ps[q * SLOT:(q + 1) * SLOT, :], pick[:, :], b1_sb[:, n * HALF:(n + 1) * HALF],
                       start=True, stop=False, skip_group_check=True)
                pe.wait_ge(xgT_ready, turn)
                for k in range(KD):
                    own = odd and k < ODD
                    rows = odd_unit[k] if own else ring[:, k, :]
                    pe.wait_ge(odd_in[k] if own else ring_in[k], arrived_low if k < ODD else arrived)
                    for ps, q, n in w1_parts:
                        last = mm(ps[q * SLOT:(q + 1) * SLOT, :], xgT[:, k % 4, k // 4, :], rows[:, n * HALF:(n + 1) * HALF],
                                  start=False, stop=(k == KD - 1), skip_group_check=True)
                    last.then_inc(odd_used[k] if own else ring_used[k], 1)
                pe.wait_ge(sel_ready, turn)
                if last_turn is not None:
                    pe.wait_ge(gselT_ready, last_turn)
                gather().then_inc(gathered, 1)
                if last_turn is not None:
                    pe.wait_ge(y_ready, last_turn)
                    for t in range(NT):
                        scatter(t)
                else:
                    pe.wait_ge(*done("act", "ppj3"))
                    pe.wait_ge(b2_in, 16)
                    pe.wait_ge(b2_high_in, 16)
                    for t in range(NT):
                        for n in range(D // HALF):
                            last = mm(acc[2 * t + n][:, :], combT[:, t * P:(t + 1) * P], b2_halves[n],
                                      start=True, stop=False, skip_group_check=True)
                    last.then_inc(*tell("pe", "b2"))
                pe.wait_ge(act_ready, turn)
                turn_block(y_ps, act_rows).then_inc(act_turned, 1)
                pe.wait_ge(xg_ready, turn_next)
                turn_block(xg_ps, xg_rows).then_inc(xg_turned, 1)
                pe.wait_ge(actT_ready, turn)
                for k in range(KF):
                    u = KD + k // 2
                    if k % 2 == 0:
                        pe.wait_ge(ring_in[u], arrived)
                    w2u = ring[:, u, :].rearrange("p (k n) -> p k n", k=2)
                    for q in range(2):
                        last = mm(y_ps[q * SLOT:(q + 1) * SLOT, :], actT[:, k % 4, k // 4, :], w2u[:, k % 2, q * HALF:(q + 1) * HALF],
                                  start=(k == 0), stop=(k == KF - 1), skip_group_check=True)
                    if k % 2:
                        last.then_inc(ring_used[u], 1)

            expert(1, 2, 16, 16, None, False)
            expert(2, 3, 32, 16, 1, True)
            pe.wait_ge(*done("dve", "pairs"))
            n_pairs = pe.value_load(pairs[0:1, 0:1], min_val=E // 2, max_val=MAXIT // 2)
            with pe.Fori(1, n_pairs) as j:
                arrived_low = pe.snap(j * 16 + 16)
                for parity in range(2):
                    last_turn, turn, turn_next = [pe.snap(j * 2 + parity + i) for i in range(3)]
                    expert(turn, turn_next, pe.snap(j * 32 + 16 * parity + 16), arrived_low, last_turn, parity == 1)
            n_it = pe.snap(n_pairs * 2)
            pe.wait_ge(xgT_ready, pe.snap(n_pairs * 2 + 1))
            pe.wait_ge(gsel_ready, n_it)
            turn_gates().then_inc(gsel_turned, 1)
            pe.wait_ge(gselT_ready, n_it)
            pe.wait_ge(y_ready, n_it)
            for t in range(NT):
                scatter(t).then_inc(*tell("pe", f"moe{t}"))

            def gate_part(t, n, ks):
                (w_hi, w_lo), (h_hi, h_lo) = gate_parts, hp_parts
                for k in ks:
                    if t == 0 and n == 0:
                        pe.wait_ge(*done(gate_rest(k), f"gate_rest{k}"))
                    for i, (h, w) in enumerate([(h_hi, w_hi), (h_lo, w_hi), (h_hi, w_lo)]):
                        last = mm(bank[4 + 2 * t + n][:, :], h[:, k, t * P:(t + 1) * P], w[:, k, n * HALF:(n + 1) * HALF],
                                  start=(k == 0 and i == 0), stop=(k == KD - 1 and i == 2), skip_group_check=True)
                if k == KD - 1:
                    last.then_inc(*tell("pe", f"pg{2 * t + n}"))

            for i in range(2):
                turn_half(3, i, i)
            pe.wait_ge(*done("dve", "hp_rest0"))
            gate_part(0, 0, low)
            pe.wait_ge(*done("dve", "x2b"))
            gate_part(0, 1, low)
            pe.wait_ge(*done("dve", "hp_rest1"))
            gate_part(0, 0, high)
            for i in range(2, 4):
                turn_half(3, i, i)
            gate_part(0, 1, high)
            pe.wait_ge(*done("dve", "hp_rest3"))
            gate_part(1, 0, range(KD))
            gate_part(1, 1, range(KD))


_INS = ["x", "p", "norm1_g", "w_in", "pool_w", "pool_scale", "w_branch_pool", "w_branch_attn", "w_out",
        "norm2_g", "router_w", "router_b", "exp_w1", "exp_b1", "exp_w2", "exp_b2",
        "ple_norm_g", "ple_gate_w", "ple_proj_w", "final_g"]


def kernel(**inputs):
    import numpy as _np
    import concourse.bacc as _bacc
    from concourse import mybir as _mybir
    from concourse.bass_utils import run_bass_kernel_spmd as _run

    nc = _bacc.Bacc("TRN2", target_bir_lowering=False, num_devices=1)
    arrays, args = {}, []
    for name in _INS:
        a = _np.ascontiguousarray(inputs[name])
        arrays[f"in_{name}"] = a
        args.append(nc.dram_tensor(f"in_{name}", a.shape, _mybir.dt.from_np(a.dtype), kind="ExternalInput").ap())
    shape = inputs["x"].shape
    out = nc.dram_tensor("out_x", shape, _mybir.dt.float32, kind="ExternalOutput").ap()
    hybrid_block(nc, *args, out)
    r = _run(nc, [arrays], core_ids=[0])
    return r.results[0]["out_x"]
```
